# Optimizing a Trainium2 kernel written in Bass

```python
import math
import jax
import jax.numpy as jnp
from jax import lax
import numpy as np

D_MODEL = 1024
BATCH = 1
SEQ = 256
DEPTH = 1
DEC_BATCH = 8
DEC_SEQ = 8
PAST_LEN = 2048
PAGE_SIZE = 128

MIX_W = D_MODEL
SSM_W = MIX_W // 2
SSM_CH = 16
SSM_GROUPS = SSM_W // SSM_CH
SSM_P = 64
N_HEADS = 8
V_DIM = (MIX_W - SSM_W) // N_HEADS
NOPE_DIM = 64
ROPE_DIM = 32
QK_DIM = NOPE_DIM + ROPE_DIM
Q_RANK = D_MODEL // 4
KV_RANK = D_MODEL // 8
D_IN = SSM_W + Q_RANK + KV_RANK + ROPE_DIM
ROPE_BASE = 10000.0
Q_BLOCK = 128
N_GROUPS = 4
EXPERTS_PER_GROUP = 8
N_EXPERTS = N_GROUPS * EXPERTS_PER_GROUP
TOP_K = 2
D_EXPERT = D_MODEL // 4
EPS = 1e-6
DT_MIN = 0.001
DT_MAX = 0.1

kernel_name = 'hymba_s5_mla_hier_moe_step'

def rms_norm(x, g):
    xf = x.astype(jnp.float32)
    xf = xf * lax.rsqrt(jnp.mean(xf * xf, axis=-1, keepdims=True) + EPS)
    return (xf * g.astype(jnp.float32)).astype(x.dtype)

def rope_tables(pos):
    inv_freq = ROPE_BASE ** (-jnp.arange(0, ROPE_DIM, 2, dtype=jnp.float32) / ROPE_DIM)
    ang = pos.astype(jnp.float32)[:, None] * inv_freq[None, :]
    return jnp.cos(ang), jnp.sin(ang)

def apply_rope(x, cos, sin):
    xf = x.astype(jnp.float32)
    x1, x2 = xf[..., :ROPE_DIM // 2], xf[..., ROPE_DIM // 2:]
    return jnp.concatenate([x1 * cos - x2 * sin, x1 * sin + x2 * cos], axis=-1).astype(x.dtype)

def in_projection(n, w_in):
    z = jnp.einsum('btd,de->bte', n, w_in)
    o1, o2, o3 = SSM_W, SSM_W + Q_RANK, SSM_W + Q_RANK + KV_RANK
    return z[..., :o1], z[..., o1:o2], z[..., o2:o3], z[..., o3:]

def s5_discretize(p):
    f = jnp.float32
    a_re, a_im = p['ssm_a_re'].astype(f), p['ssm_a_im'].astype(f)
    dt = jnp.exp(p['ssm_log_dt'].astype(f))[:, None]
    mag, ang = jnp.exp(a_re * dt), a_im * dt
    lb_re, lb_im = mag * jnp.cos(ang), mag * jnp.sin(ang)
    den = a_re * a_re + a_im * a_im
    num_re = lb_re - 1.0
    coef_re = (num_re * a_re + lb_im * a_im) / den
    coef_im = (lb_im * a_re - num_re * a_im) / den
    b_re, b_im = p['ssm_b_re'].astype(f), p['ssm_b_im'].astype(f)
    bb_re = coef_re[..., None] * b_re - coef_im[..., None] * b_im
    bb_im = coef_re[..., None] * b_im + coef_im[..., None] * b_re
    return lb_re, lb_im, bb_re, bb_im

def complex_affine_combine(e1, e2):
    a1r, a1i, b1r, b1i = e1
    a2r, a2i, b2r, b2i = e2
    return (a2r * a1r - a2i * a1i, a2r * a1i + a2i * a1r,
            a2r * b1r - a2i * b1i + b2r, a2r * b1i + a2i * b1r + b2i)

def s5_mixer(u, h0_re, h0_im, p):
    f = jnp.float32
    nb, t = u.shape[0], u.shape[1]
    lb_re, lb_im, bb_re, bb_im = s5_discretize(p)
    uf = u.astype(f)
    ug = uf.reshape(nb, t, SSM_GROUPS, SSM_CH)
    bu_re = jnp.einsum('btgc,gpc->btgp', ug, bb_re)
    bu_im = jnp.einsum('btgc,gpc->btgp', ug, bb_im)
    if h0_re is not None:
        h0r, h0i = h0_re.astype(f), h0_im.astype(f)
        bu_re = bu_re.at[:, 0].add(lb_re * h0r - lb_im * h0i)
        bu_im = bu_im.at[:, 0].add(lb_re * h0i + lb_im * h0r)
    a_re = jnp.broadcast_to(lb_re, (1, t, SSM_GROUPS, SSM_P))
    a_im = jnp.broadcast_to(lb_im, (1, t, SSM_GROUPS, SSM_P))
    _, _, h_re, h_im = lax.associative_scan(complex_affine_combine, (a_re, a_im, bu_re, bu_im), axis=1)
    c_re, c_im = p['ssm_c_re'].astype(f), p['ssm_c_im'].astype(f)
    y = jnp.einsum('btgp,gcp->btgc', h_re, c_re) - jnp.einsum('btgp,gcp->btgc', h_im, c_im)
    y = y.reshape(nb, t, SSM_W) + p['ssm_d'].astype(f) * uf
    y = jax.nn.gelu(y)
    out = y * jax.nn.sigmoid(y @ p['ssm_w_glu'].astype(f) + p['ssm_b_glu'].astype(f))
    return out.astype(u.dtype), h_re[:, -1], h_im[:, -1]

def mla_queries(cq, pos, p):
    q = jnp.einsum('btr,rhd->bthd', rms_norm(cq, p['q_norm_g']), p['w_uq'])
    cos, sin = rope_tables(pos)
    q = jnp.concatenate([q[..., :NOPE_DIM], apply_rope(q[..., NOPE_DIM:], cos[:, None], sin[:, None])], axis=-1)
    return rms_norm(q, p['qk_norm_q']) * (1.0 / math.sqrt(QK_DIM))

def mla_latent(ckv_raw, kr_raw, pos, p):
    cos, sin = rope_tables(pos)
    return rms_norm(ckv_raw, p['kv_norm_g']), apply_rope(kr_raw, cos, sin)

def mla_keys(ckv, kr, w_uk, qk_norm_k):
    k_nope = jnp.einsum('btr,rhd->bthd', ckv, w_uk)
    k_rope = jnp.broadcast_to(kr[:, :, None, :], k_nope.shape[:-1] + (ROPE_DIM,))
    return rms_norm(jnp.concatenate([k_nope, k_rope.astype(k_nope.dtype)], axis=-1), qk_norm_k)

def mla_prompt_attention(q, ckv, kr, p):
    nb, t = q.shape[0], q.shape[1]
    k = mla_keys(ckv, kr, p['w_uk'], p['qk_norm_k'])
    v = jnp.einsum('btr,rhd->bthd', ckv, p['w_uv'])
    n_blocks = t // Q_BLOCK
    qb = q.reshape(nb, n_blocks, Q_BLOCK, N_HEADS, QK_DIM).swapaxes(0, 1)
    kpos = jnp.arange(t)

    def block(args):
        q_blk, blk = args
        s = jnp.einsum('bqhd,bkhd->bhqk', q_blk, k).astype(jnp.float32)
        qpos = blk * Q_BLOCK + jnp.arange(Q_BLOCK)
        s = jnp.where(kpos[None, :] <= qpos[:, None], s, -jnp.inf)
        pr = jax.nn.softmax(s, axis=-1)
        return jnp.einsum('bhqk,bkhd->bqhd', pr.astype(v.dtype), v)

    o = lax.map(block, (qb, jnp.arange(n_blocks)))
    return o.swapaxes(0, 1).reshape(nb, t, N_HEADS * V_DIM)

def mla_sample_attention(q, ckv_new, kr_new, cache_ckv, cache_krope, page_table, p):
    f = jnp.float32
    nb, t = q.shape[0], q.shape[1]

    def page_step(carry, pages):
        m, l, acc = carry
        ckv_p = cache_ckv[pages]
        kr_p = cache_krope[pages]
        k_p = mla_keys(ckv_p, kr_p, p['w_uk'], p['qk_norm_k'])
        s = jnp.einsum('bthd,bkhd->bhtk', q, k_p).astype(f)
        m_new = jnp.maximum(m, s.max(axis=-1))
        corr = jnp.exp(m - m_new)
        pr = jnp.exp(s - m_new[..., None])
        l = l * corr + pr.sum(axis=-1)
        acc = acc * corr[..., None] + jnp.einsum('bhtk,bkr->bhtr', pr, ckv_p.astype(f))
        return (m_new, l, acc), None

    init = (jnp.full((nb, N_HEADS, t), -jnp.inf, f),
            jnp.zeros((nb, N_HEADS, t), f),
            jnp.zeros((nb, N_HEADS, t, KV_RANK), f))
    (m, l, acc), _ = lax.scan(page_step, init, page_table.T)
    k_new = mla_keys(ckv_new, kr_new, p['w_uk'], p['qk_norm_k'])
    s = jnp.einsum('bthd,bkhd->bhtk', q, k_new).astype(f)
    s = jnp.where(jnp.tril(jnp.ones((t, t), dtype=bool)), s, -jnp.inf)
    m_f = jnp.maximum(m, s.max(axis=-1))
    corr = jnp.exp(m - m_f)
    pr = jnp.exp(s - m_f[..., None])
    l = l * corr + pr.sum(axis=-1)
    acc = acc * corr[..., None] + jnp.einsum('bhtk,bkr->bhtr', pr, ckv_new.astype(f))
    o_lat = acc / l[..., None]
    o = jnp.einsum('bhtr,rhd->bthd', o_lat, p['w_uv'].astype(f))
    return o.reshape(nb, t, N_HEADS * V_DIM).astype(q.dtype)

def merge_heads(ssm_out, attn_out, p):
    y = jnp.concatenate([rms_norm(ssm_out, p['out_norm_ssm']), rms_norm(attn_out, p['out_norm_attn'])], axis=-1)
    return jnp.einsum('btm,md->btd', y, p['w_out'])

def hier_moe(x, p):
    f = jnp.float32

    def per_seq(xs):
        t = xs.shape[0]
        lg = (xs @ p['w_router_group'] + p['b_router_group']).astype(f)
        g = jnp.argmax(lg, axis=-1)
        p_sel = jax.nn.softmax(lg, axis=-1).max(axis=-1, keepdims=True)
        le = (xs @ p['w_router_expert'] + p['b_router_expert']).astype(f)
        le = le.reshape(t, N_GROUPS, EXPERTS_PER_GROUP)
        le_g = jnp.einsum('tge,tg->te', le, jax.nn.one_hot(g, N_GROUPS, dtype=f))
        top_v, top_i = lax.top_k(le_g, TOP_K)
        w = jax.nn.softmax(top_v, axis=-1) * p_sel
        eidx = g[:, None] * EXPERTS_PER_GROUP + top_i
        gate = jnp.einsum('tk,tke->te', w, jax.nn.one_hot(eidx, N_EXPERTS, dtype=f))
        hg = jnp.einsum('td,edf->tef', xs, p['w_gate'])
        hu = jnp.einsum('td,edf->tef', xs, p['w_up'])
        h = jax.nn.silu(hg) * hu * gate[:, :, None].astype(hg.dtype)
        return jnp.einsum('tef,efd->td', h, p['w_down'])

    return lax.map(per_seq, x)

def decoder_layer(x_p, x_s, cache_ckv, cache_krope, st_re, st_im, page_table, p):
    nb_p, t_p = x_p.shape[0], x_p.shape[1]
    pos_p = jnp.arange(t_p)
    u, cq, ckv_raw, kr_raw = in_projection(rms_norm(x_p, p['norm1_g']), p['w_in'])
    ssm_p, hp_re, hp_im = s5_mixer(u, None, None, p)
    q = mla_queries(cq, pos_p, p)
    ckv_p, kr_p = mla_latent(ckv_raw, kr_raw, pos_p, p)
    att_p = mla_prompt_attention(q, ckv_p, kr_p, p)
    h_p = x_p + merge_heads(ssm_p, att_p, p)
    y_p = h_p + hier_moe(rms_norm(h_p, p['norm2_g']), p)
    pos_s = PAST_LEN + jnp.arange(x_s.shape[1])
    u, cq, ckv_raw, kr_raw = in_projection(rms_norm(x_s, p['norm1_g']), p['w_in'])
    ssm_s, hs_re, hs_im = s5_mixer(u, st_re, st_im, p)
    q = mla_queries(cq, pos_s, p)
    ckv_s, kr_s = mla_latent(ckv_raw, kr_raw, pos_s, p)
    att_s = mla_sample_attention(q, ckv_s, kr_s, cache_ckv, cache_krope, page_table, p)
    h_s = x_s + merge_heads(ssm_s, att_s, p)
    y_s = h_s + hier_moe(rms_norm(h_s, p['norm2_g']), p)
    n_pg = t_p // PAGE_SIZE
    return (y_p, y_s,
            ckv_p.reshape(nb_p, n_pg, PAGE_SIZE, KV_RANK), kr_p.reshape(nb_p, n_pg, PAGE_SIZE, ROPE_DIM),
            hp_re, hp_im, ckv_s, kr_s, hs_re, hs_im)

def setup_inputs(seed: int = 0) -> dict:
    key = jax.random.key(seed)
    ks = jax.random.split(key, 40)
    f = jnp.float32

    def nrm(i, shape, scale):
        return scale * jax.random.normal(ks[i], shape, f)

    def gain(i, n):
        return 1.0 + 0.01 * jax.random.normal(ks[i], (DEPTH, n), f)

    n_pages = PAST_LEN // PAGE_SIZE
    n_used = DEC_BATCH * n_pages
    n_pool = n_used + n_used // 4
    page_table = jax.random.permutation(ks[0], n_pool)[:n_used].reshape(DEC_BATCH, n_pages).astype(jnp.int32)
    n_idx = jnp.arange(SSM_P, dtype=f)
    gps = (DEPTH, SSM_GROUPS, SSM_P)
    return {
        'x_prompt': nrm(1, (BATCH, SEQ, D_MODEL), 1.0),
        'x_sample': nrm(2, (DEC_BATCH, DEC_SEQ, D_MODEL), 1.0),
        'cache_ckv': nrm(3, (DEPTH, n_pool, PAGE_SIZE, KV_RANK), 1.0),
        'cache_krope': nrm(4, (DEPTH, n_pool, PAGE_SIZE, ROPE_DIM), 1.0),
        'state_ssm_re': nrm(5, (DEPTH, DEC_BATCH, SSM_GROUPS, SSM_P), 0.5),
        'state_ssm_im': nrm(6, (DEPTH, DEC_BATCH, SSM_GROUPS, SSM_P), 0.5),
        'page_table': page_table,
        'norm1_g': gain(7, D_MODEL),
        'w_in': nrm(8, (DEPTH, D_MODEL, D_IN), D_MODEL ** -0.5),
        'ssm_a_re': -0.5 * (1.0 + nrm(9, gps, 0.01)),
        'ssm_a_im': jnp.pi * (n_idx + nrm(10, gps, 0.01)),
        'ssm_log_dt': jax.random.uniform(ks[11], (DEPTH, SSM_GROUPS), f, math.log(DT_MIN), math.log(DT_MAX)),
        'ssm_b_re': nrm(12, (DEPTH, SSM_GROUPS, SSM_P, SSM_CH), (2 * SSM_CH) ** -0.5),
        'ssm_b_im': nrm(13, (DEPTH, SSM_GROUPS, SSM_P, SSM_CH), (2 * SSM_CH) ** -0.5),
        'ssm_c_re': nrm(14, (DEPTH, SSM_GROUPS, SSM_CH, SSM_P), (2 * SSM_P) ** -0.5),
        'ssm_c_im': nrm(15, (DEPTH, SSM_GROUPS, SSM_CH, SSM_P), (2 * SSM_P) ** -0.5),
        'ssm_d': nrm(16, (DEPTH, SSM_W), 1.0),
        'ssm_w_glu': nrm(17, (DEPTH, SSM_W, SSM_W), SSM_W ** -0.5),
        'ssm_b_glu': nrm(18, (DEPTH, SSM_W), 0.01),
        'q_norm_g': gain(19, Q_RANK),
        'w_uq': nrm(20, (DEPTH, Q_RANK, N_HEADS, QK_DIM), Q_RANK ** -0.5),
        'kv_norm_g': gain(21, KV_RANK),
        'w_uk': nrm(22, (DEPTH, KV_RANK, N_HEADS, NOPE_DIM), KV_RANK ** -0.5),
        'w_uv': nrm(23, (DEPTH, KV_RANK, N_HEADS, V_DIM), KV_RANK ** -0.5),
        'qk_norm_q': gain(24, QK_DIM),
        'qk_norm_k': gain(25, QK_DIM),
        'out_norm_ssm': gain(26, SSM_W),
        'out_norm_attn': gain(27, N_HEADS * V_DIM),
        'w_out': nrm(28, (DEPTH, MIX_W, D_MODEL), MIX_W ** -0.5),
        'norm2_g': gain(29, D_MODEL),
        'w_router_group': nrm(30, (DEPTH, D_MODEL, N_GROUPS), D_MODEL ** -0.5),
        'b_router_group': nrm(31, (DEPTH, N_GROUPS), 0.01),
        'w_router_expert': nrm(32, (DEPTH, D_MODEL, N_EXPERTS), D_MODEL ** -0.5),
        'b_router_expert': nrm(33, (DEPTH, N_EXPERTS), 0.01),
        'w_gate': nrm(34, (DEPTH, N_EXPERTS, D_MODEL, D_EXPERT), D_MODEL ** -0.5),
        'w_up': nrm(35, (DEPTH, N_EXPERTS, D_MODEL, D_EXPERT), D_MODEL ** -0.5),
        'w_down': nrm(36, (DEPTH, N_EXPERTS, D_EXPERT, D_MODEL), D_EXPERT ** -0.5),
    }

def reference(x_prompt, x_sample, cache_ckv, cache_krope, state_ssm_re, state_ssm_im, page_table,
              norm1_g, w_in, ssm_a_re, ssm_a_im, ssm_log_dt, ssm_b_re, ssm_b_im, ssm_c_re, ssm_c_im,
              ssm_d, ssm_w_glu, ssm_b_glu, q_norm_g, w_uq, kv_norm_g, w_uk, w_uv, qk_norm_q, qk_norm_k,
              out_norm_ssm, out_norm_attn, w_out, norm2_g, w_router_group, b_router_group,
              w_router_expert, b_router_expert, w_gate, w_up, w_down):
    h_p, h_s = x_prompt, x_sample
    ckv_p_l, kr_p_l, re_p_l, im_p_l = [], [], [], []
    ckv_s_l, kr_s_l, re_s_l, im_s_l = [], [], [], []
    for layer in range(DEPTH):
        p = {
            'norm1_g': norm1_g[layer], 'w_in': w_in[layer],
            'ssm_a_re': ssm_a_re[layer], 'ssm_a_im': ssm_a_im[layer], 'ssm_log_dt': ssm_log_dt[layer],
            'ssm_b_re': ssm_b_re[layer], 'ssm_b_im': ssm_b_im[layer],
            'ssm_c_re': ssm_c_re[layer], 'ssm_c_im': ssm_c_im[layer], 'ssm_d': ssm_d[layer],
            'ssm_w_glu': ssm_w_glu[layer], 'ssm_b_glu': ssm_b_glu[layer],
            'q_norm_g': q_norm_g[layer], 'w_uq': w_uq[layer], 'kv_norm_g': kv_norm_g[layer],
            'w_uk': w_uk[layer], 'w_uv': w_uv[layer],
            'qk_norm_q': qk_norm_q[layer], 'qk_norm_k': qk_norm_k[layer],
            'out_norm_ssm': out_norm_ssm[layer], 'out_norm_attn': out_norm_attn[layer], 'w_out': w_out[layer],
            'norm2_g': norm2_g[layer],
            'w_router_group': w_router_group[layer], 'b_router_group': b_router_group[layer],
            'w_router_expert': w_router_expert[layer], 'b_router_expert': b_router_expert[layer],
            'w_gate': w_gate[layer], 'w_up': w_up[layer], 'w_down': w_down[layer],
        }
        (h_p, h_s, ckv_p, kr_p, hp_re, hp_im, ckv_s, kr_s, hs_re, hs_im) = decoder_layer(
            h_p, h_s, cache_ckv[layer], cache_krope[layer], state_ssm_re[layer], state_ssm_im[layer],
            page_table, p)
        ckv_p_l.append(ckv_p); kr_p_l.append(kr_p); re_p_l.append(hp_re); im_p_l.append(hp_im)
        ckv_s_l.append(ckv_s); kr_s_l.append(kr_s); re_s_l.append(hs_re); im_s_l.append(hs_im)
    return (h_p, h_s,
            jnp.stack(ckv_p_l), jnp.stack(kr_p_l), jnp.stack(re_p_l), jnp.stack(im_p_l),
            jnp.stack(ckv_s_l), jnp.stack(kr_s_l), jnp.stack(re_s_l), jnp.stack(im_s_l))


_drawn_inputs = setup_inputs


def setup_inputs(seed=0):
    import zlib

    import numpy as np

    out = dict(_drawn_inputs(seed))
    spreads = {}
    factors = {'norm1_g': 2.953,
     'ssm_a_re': 8.0,
     'ssm_b_glu': 4.879,
     'q_norm_g': 2.943,
     'kv_norm_g': 3.914,
     'qk_norm_q': 2.757,
     'qk_norm_k': 6.322,
     'out_norm_ssm': 4.648,
     'out_norm_attn': 4.984,
     'norm2_g': 3.174,
     'b_router_group': 3.638,
     'b_router_expert': 3.615}
    for name, (base, spread) in spreads.items():
        noise = np.random.default_rng([zlib.crc32(name.encode()), seed]).standard_normal(out[name].shape)
        drawn = base * np.exp(spread * noise) if base else spread * noise
        out[name] = jnp.asarray(drawn.astype(out[name].dtype))
    for name, factor in factors.items():
        out[name] = (out[name] * factor).astype(out[name].dtype)
    return out
```

```python
import math
from contextlib import ExitStack

import numpy as np

import concourse.bass as bass
from concourse import mybir

ALU = mybir.AluOpType
ACT = mybir.ActivationFunctionType
AX = mybir.AxisListType.X
F32 = mybir.dt.float32
U32 = mybir.dt.uint32
I32 = mybir.dt.int32

P = 128
D = 1024
SEQ = 256
NB, NQ = 8, 8
NS = NB * NQ
T = SEQ + NS
TT = 3
TP = TT * P
KD = D // P
SSM_W, CH, GROUPS, SP = 512, 16, 32, 64
LT = GROUPS * SP // P
H, VD, NOPE, ROPE = 8, 64, 64, 32
HR = ROPE // 2
QK = NOPE + ROPE
QR, KR = 256, 128
ZW = QR + KR + ROPE
DIN = SSM_W + ZW
PAGE, NPG, POOL = 128, 16, 160
UP = 8
RUN = 8
NG, EG, NE, FE = 4, 8, 32, 256
EPS = 1e-6
NEG = -1e30
MAGIC = 1.5 * 2.0 ** 23
TWO_PI = 6.283185
SLOTS = 128
ROUNDS = -(-T // SLOTS)
FAR = 65536.0

_COLS = [("ident", P), ("tri", P), ("ones", P), ("causal", 3 * P), ("smask", NS), ("slot", SLOTS),
         ("step", T), ("carry", T), ("tok", TT), ("valid", TT), ("early8", 64), ("early4", 16), ("quad", 4),
         ("cos", TT * HR), ("sin", TT * HR), ("pgsel", P), ("pgrow", 1), ("even", P)]
COL = {}
_at = 0
for _n, _w in _COLS:
    COL[_n] = (_at, _w)
    _at += _w
NCONST = _at
LASTING = COL["cos"][0]


def shape_constants():
    c = np.zeros((P, NCONST), np.float32)

    def col(name):
        a, w = COL[name]
        return c[:, a:a + w]

    p = np.arange(P)
    col("ident")[:] = np.eye(P)
    col("tri")[:] = p[:, None] < p[None, :]
    col("ones")[:] = 1.0
    col("causal")[:, 0:P] = col("causal")[:, 2 * P:] = np.where(p[None, :] <= p[:, None], 0.0, NEG)
    key_b, key_t = p // NQ, p % NQ
    for b in range(NB):
        for q in range(NQ):
            col("smask")[:, b * NQ + q] = np.where((key_b == b) & (key_t <= q), 0.0, NEG)
    col("slot")[:] = np.arange(SLOTS)[None, :]
    step = np.concatenate([np.arange(1, SEQ + 1), np.tile(np.arange(1, NQ + 1), NB)])
    col("step")[:] = step[None, :]
    col("carry")[:] = (step != 1)[None, :]
    inv = (np.float32(10000.0) ** (-np.arange(0, ROPE, 2, dtype=np.float32) / np.float32(ROPE))).astype(np.float32)
    pos = np.zeros((TT, P), np.float32)
    pos[0], pos[1] = np.arange(P), np.arange(P, 2 * P)
    pos[2, :NS] = NPG * PAGE + np.arange(NS) % NQ
    ang = (pos[:, :, None] * inv[None, None, :]).astype(np.float32).transpose(1, 0, 2).reshape(P, -1)
    col("cos")[:], col("sin")[:] = np.cos(ang), np.sin(ang)
    col("pgsel")[:UP] = (p[None, :] // (P // UP)) == np.arange(UP)[:, None]
    col("pgrow")[:, 0] = p % (PAGE // RUN)
    col("tok")[:] = p[:, None] + P * np.arange(TT)[None, :]
    col("valid")[:] = col("tok") < T
    e = np.arange(8)
    col("early8")[:] = (e[None, :] < e[:, None]).reshape(1, 64)
    col("early4")[:] = (e[None, :4] < e[:4, None]).reshape(1, 16)
    col("even")[:] = (p[:, None] // SP) == ((p[None, :] // CH) % 2)
    col("quad")[:] = (p[:, None] // 32) == np.arange(4)[None, :]
    return c


_ROWS = [("log_dt", 16), ("norm1_g", 8), ("ssm_d", 4), ("ssm_b_glu", 4), ("q_norm_g", 2), ("out_norm_ssm", 4),
         ("out_norm_attn", 4), ("ssm_a_re", 16), ("ssm_a_im", 16)]
ROW = {}
_at = 0
for _n, _w in _ROWS:
    ROW[_n] = (_at, _at + _w)
    _at += _w
NROW = _at


class Chain:

    def __init__(self, eng, sem):
        self.eng, self.sem, self.n = eng, sem, 0

    def inc(self, ins):
        ins.then_inc(self.sem, 1)
        self.n += 1
        return ins

    def sync(self):
        self.eng.wait_ge(self.sem, self.n)

    def link(self, ins):
        self.inc(ins)
        self.sync()
        return ins


def build_program(nc, I, O):
    with ExitStack() as ctx:
        def sb(name, n, dt=F32):
            return ctx.enter_context(nc.sbuf_tensor(name, [P, n], dt))

        sems = {}

        def S(name):
            if name not in sems:
                sems[name] = ctx.enter_context(nc.semaphore(name))
            return sems[name]

        chains = {}

        def chain(eng, name):
            if name not in chains:
                chains[name] = Chain(eng, S(name))
            return chains[name]

        ps = [ctx.enter_context(nc.psum_tensor(f"bank{i}", [P, 512], F32)) for i in range(8)]

        xs_dram = nc.dram_tensor("normed_tokens", [T, D], F32).ap()
        y2_dram = nc.dram_tensor("expert_rows", [2 * T, D], F32).ap()

        cst = sb("constants", LASTING)

        def C(name, rows=P):
            a, w = COL[name]
            if a >= LASTING:
                return cst_early[0:rows, a - LASTING:a - LASTING + w]
            return cst[0:rows, a:a + w]

        x = sb("x", TT * D)
        R = sb("region_ssm_then_ring", 18432)
        O1 = sb("region_projection_then_w_out", 8192)
        cst_early = O1[:, 7392:7392 + NCONST - LASTING]
        ident = C("ident")
        QT = sb("region_qT", 3072)
        KT = sb("region_kT", 3072)
        CA = sb("region_cache_then_prompt", 5120)
        UQ = sb("region_w_uq", 1536)
        LP = sb("region_loop", 2560)
        uT = sb("uT", 4 * T)
        w_uk = sb("w_uk", H * NOPE)
        w_uv = sb("w_uv", H * VD)
        v = sb("v_prompt", 2 * 512)
        CT = sb("ssm_c_T", 1024)
        vrow = sb("vector_rows", P)
        vec = sb("vector_columns", NROW)
        ckvn = sb("ckv_normed", TT * KR)
        krn = sb("k_rope", TT * ROPE)
        ckvT = sb("ckv_new_T", TP)
        g_row = sb("gain_rows", KR + 2 * QK)
        par = sb("ssm_params", 16 * 16)
        small = sb("small", 160)
        st0 = QT[:, 2560:2816]
        n2 = QT[:, 2816:3072]
        soft = KT[:, 2560:2824]
        kr2 = KT[:, 2824:2832]
        w_r = uT[:, 0:KD * 36]
        b_r = uT[:, KD * 36:(KD + 1) * 36]
        pgf = sb("page_table_f", 2 * 16)
        pgt = sb("page_table_i", 16, I32)
        olat = vrow

        w_in = R[:, 0:KD * DIN].rearrange("p (k n) -> p k n", k=KD)
        bre, bim = R[:, 0:5120], R[:, 5120:10240]
        tmp = [R[:, 10240 + 640 * i:10240 + 640 * (i + 1)] for i in range(8)]
        Ssb = [R[:, 15360 + 1088 * i:15360 + 1088 * (i + 1)] for i in range(2)]
        xn = O1[:, 0:3072]
        nT = O1[:, 3072:6144].rearrange("p (k t) -> p k t", k=KD)
        z = O1[:, 6144:6144 + TT * ZW].rearrange("p (i n) -> p i n", i=TT)
        q = O1[:, 0:2304].rearrange("p (i h d) -> p i h d", i=TT, h=H)
        kk = O1[:, 2304:4608].rearrange("p (i h d) -> p i h d", i=TT, h=H)
        cqn = O1[:, 4608:4608 + TT * QR].rearrange("p (i n) -> p i n", i=TT)
        cqT = O1[:, 5376:5376 + 768].rearrange("p (k t) -> p k t", k=2)
        w_out = O1[:, 0:8192].rearrange("p (k n) -> p k n", k=8)
        qT = QT[:, 0:H * T].rearrange("p (h t) -> p h t", h=H)
        kT = KT[:, 0:H * T].rearrange("p (h t) -> p h t", h=H)
        w_uq = UQ[:, :].rearrange("p (k n) -> p k n", k=2)
        w_ukT = UQ[:, 0:1024].rearrange("p (h r) -> p h r", h=H)
        olT = UQ[:, 0:512]
        qa = UQ[:, 512:1024]
        s_new = UQ[:, 1024:1536]
        qrp = R[:, 17792:18304]
        bdr, bdi = LP[:, 0:512], LP[:, 512:1024]
        braw = LP[:, 1024:1536].rearrange("p (a i c) -> p a i c", a=2, i=LT)
        cT = [LP[:, 0:512], LP[:, 512:1024]]
        krT = [LP[:, 1024:1280], LP[:, 1280:1536]]
        sq = [LP[:, 1536:2048], LP[:, 2048:2560]]
        cache = [CA[:, 1280 * i:1280 * i + 1024] for i in range(4)]
        cachr = [CA[:, 1280 * i + 1024:1280 * (i + 1)] for i in range(4)]

        limits = {}

        def limit(pool, last_row, count):
            if isinstance(count, int):
                return last_row
            if last_row not in limits:
                limits[last_row] = pool.alloc_register(f"last_row_{last_row}")
            reg = limits[last_row]
            pool.reg_add(reg, count, last_row)
            pool.reg_alu(reg, reg, last_row, ALU.min)
            return reg

        def bc(ap, dim, n):
            shape = list(ap.shape)
            shape.insert(dim, n)
            return ap.unsqueeze(dim).to_broadcast(shape)

        def v3(ap, a):
            return ap.rearrange("p (a b) -> p a b", a=a)

        PER = dict(kr_transposed=2, kr_copied=2, c_transposed=4, c_copied=4, keys_made=16, squared=16,
                   summed=16, scored=16, sums_ready=2, rs_key=2, scaled=2, dve_seq=7, act_seq=4,
                   tail_dve=3, max_ready=1, max_T=1, diag_ready=1, max_row=1, centred=1, exp_done=1,
                   exp_summed=1, values_done=1, lat_scaled=1, lat_T=1, lat_copied=1,
                   turns=1, fractions=1, trig=1, rotated=1, scanned=1, products=1, states=1)

        def at(name, b, k):
            return b * PER[name] + k

        def need(eng, name, value):
            if not isinstance(value, int) or value > 0:
                eng.wait_ge(S(name), value)

        def wait(eng, name, b, k):
            need(eng, name, at(name, b, k))

        TB, KRB, SB, AB, MB = 2, 3, (4, 5), 6, 7
        tri_c, eye = C("tri"), ident
        smx, ssum = soft[:, 0:NS], soft[:, NS:2 * NS]
        sdiag = soft[0:NS, 2 * NS:3 * NS]
        m64, rl = soft[0:NS, 4 * NS:4 * NS + 1], soft[0:NS, 4 * NS + 1:4 * NS + 2]
        cache_rows = I["cache_ckv"][0].rearrange("n (r s) d -> (n r) (s d)", s=RUN)
        rope_rows = I["cache_krope"][0].rearrange("n (r s) d -> (n r) (s d)", s=RUN)
        far_row = POOL * (PAGE // RUN) - 1

        krsq = R[:, 17536:17792]

        def gather_unit(pool, slot, b):
            off = bass.IndirectOffsetOnAxis(ap=page_idx[:, slot:slot + 1], axis=0)
            last = limit(pool, far_row, b)
            pool.indirect_dma_start(out=cache[slot], out_offset=None, in_=cache_rows, in_offset=off,
                                    bounds_check=last, oob_is_err=False).then_inc(S(f"pages{slot}"), 16)
            pool.indirect_dma_start(out=cachr[slot], out_offset=None, in_=rope_rows, in_offset=off,
                                    bounds_check=last, oob_is_err=False).then_inc(S(f"pages{slot}"), 16)

        def seq_slices(b):
            return bass.ds(b * NS, NS), bass.ds(b * 2, 2), bass.ds(b * (2 * T), 2 * T)

        def two(ap):
            return v3(ap, 2)

        f_t, f_f, f_cos, f_sin, f_1, f_2, f_3, f_4 = tmp

        def pool_seq(pool, b, par, gather):
            _, til, sl = seq_slices(b)
            wait(pool, "states", b, 0)
            pool.tensor_tensor(two(f_t), bc(C("step"), 1, 2), bc(p_f[:, til], 2, T), ALU.mult).then_inc(S("turns"), 1)
            wait(pool, "trig", b, 1)
            pool.tensor_tensor(f_1, bre[:, sl], f_cos, ALU.mult)
            pool.tensor_tensor(f_2, bim[:, sl], f_sin, ALU.mult)
            pool.tensor_tensor(f_3, bim[:, sl], f_cos, ALU.mult)
            pool.tensor_tensor(f_4, bre[:, sl], f_sin, ALU.mult)
            pool.tensor_tensor(two(f_t), bc(C("carry"), 1, 2), bc(p_mag[:, til], 2, T), ALU.mult).then_inc(S("rotated"), 1)
            if gather:
                wait(pool, "values_done", b, 0)
                for u in range(2):
                    slot = 2 * (1 - par) + u
                    pool.tensor_copy(page_idx[:, slot:slot + 1], page_all[:, bass.ds(b * 2 + (2 + u), 1)]).then_inc(S("index_copied"), 1)
                    pool.wait_ge(S("index_copied"), b * 2 + (u - 1))
                    gather_unit(pool, slot, b)
            wait(pool, "scanned", b, 1)
            pool.tensor_tensor(f_1, f_2, f_cos, ALU.mult)
            pool.tensor_tensor(f_3, f_4, f_sin, ALU.mult)
            pool.tensor_tensor(f_t, f_2, f_sin, ALU.mult)
            pool.tensor_tensor(f_f, f_4, f_cos, ALU.mult).then_inc(S("products"), 1)

        def pe_seq(pe, b, half, par, t):
            sl, _, _ = seq_slices(b)

            def transposes(g):
                u, slot = g // 2, 2 * par + g // 2
                if g % 2 == 0:
                    pe.wait_ge(S(f"pages{slot}"), half * 32 + 32)
                    wait(pe, "kr_copied", b, u)
                    for j in range(2):
                        ins = pe.transpose(ps[KRB][:, j * P:(j + 1) * P], cachr[slot][:, j * P:(j + 1) * P], ident)
                    ins.then_inc(S("kr_transposed"), 1)
                wait(pe, "c_copied", b, g)
                for i in range(4):
                    c = (4 * (g % 2) + i) * P
                    ins = pe.transpose(ps[TB][:, i * P:(i + 1) * P], cache[slot][:, c:c + P], ident)
                ins.then_inc(S("c_transposed"), 1)

            def keys_scores(g):
                u = g // 2
                wait(pe, "c_copied", b, g + 1)
                if g % 2 == 0:
                    wait(pe, "kr_copied", b, u + 1)
                    wait(pe, "scaled", b, u - 1)
                for i in range(4):
                    n = 4 * g + i
                    wait(pe, "squared", b, n - 1)
                    lat = cT[g % 2][:, i * P:(i + 1) * P]
                    pe.matmul(ps[n % 2][:, :], lat, w_uk[:, :], start=True, stop=True).then_inc(S("keys_made"), 1)
                    o = ps[SB[u]][:, (n % 8) * NS:(n % 8 + 1) * NS]
                    pe.matmul(o, lat, qa[:, sl], start=True, stop=False)
                    pe.matmul(o, krT[u][:, (n % 8 // 4) * P:(n % 8 // 4 + 1) * P],
                              qrs[par][:, NS * i:NS * (i + 1)], start=False, stop=True).then_inc(S("scored"), 1)

            transposes(0)
            transposes(1)
            keys_scores(0)
            if t is not None:
                pe_tail(pe, t, 1 - par, 0)
            transposes(2)
            keys_scores(1)
            if t is not None:
                pe_tail(pe, t, 1 - par, 1)
            transposes(3)
            keys_scores(2)
            if t is not None:
                pe_tail(pe, t, 1 - par, 2)
            keys_scores(3)
            if t is not None:
                pe_tail(pe, t, 1 - par, 3)

        def pe_tail(pe, t, par, part):
            if part == 0:
                wait(pe, "max_ready", t, 1)
                wait(pe, "lat_copied", t, 0)
                pe.transpose(ps[MB][:, 0:P], soft[:, 0:P], ident).then_inc(S("max_T"), 1)
            if part == 1:
                wait(pe, "diag_ready", t, 1)
                pe.matmul(ps[MB][:, 128:128 + NS], C("ones", NS), sdiag, start=True, stop=True).then_inc(S("max_row"), 1)
            if part == 2:
                wait(pe, "exp_done", t, 1)
                wait(pe, "lat_scaled", t, 0)
                for n in range(16):
                    slot, c = 2 * par + n // 8, (n % 8) * P
                    pe.matmul(ps[AB][0:NS, 0:KR], Ssb[par][:, n * NS:(n + 1) * NS], cache[slot][:, c:c + P],
                              start=(n == 0), stop=False)
                pe.matmul(ps[AB][0:NS, 0:KR], Ssb[par][:, 1024:1088], ckvn[:, 2 * KR:3 * KR], start=False, stop=True)
                wait(pe, "exp_summed", t, 1)
                pe.matmul(ps[AB][0:NS, KR:KR + 1], ssum, C("ones")[:, 0:1], start=True, stop=True).then_inc(S("values_done"), 1)
            if part == 3:
                wait(pe, "lat_scaled", t, 1)
                pe.transpose(ps[MB][:, 256:384], olat[:, :], ident).then_inc(S("lat_T"), 1)

        def act_seq_(act, b, par, t):
            def copy_latents(g):
                wait(act, "c_transposed", b, g + 1)
                wait(act, "scored", b, 4 * (g - 1))
                act.activation(cT[g % 2], ps[TB][:, :], ACT.Copy).then_inc(S("c_copied"), 1)

            def square(n):
                wait(act, "keys_made", b, n + 1)
                wait(act, "summed", b, n - 1)
                act.activation(sq[n % 2], ps[n % 2][:, :], ACT.Square, scale=QK ** -0.5).then_inc(S("squared"), 1)

            def key_rsqrt(s, u, parity):
                ap = n2[:, parity * P + u * 64:parity * P + (u + 1) * 64]
                wait(act, "sums_ready", s, u + 1)
                act.activation(ap, ap, ACT.Ln, bias=EPS).then_inc(S("act_rs"), 1)
                act.wait_ge(S("act_rs"), s * 2 + (u + 1))
                act.activation(ap, ap, ACT.Exp, scale=-0.5).then_inc(S("rs_key"), 1)

            copy_latents(0)
            if t is not None:
                key_rsqrt(t, 1, 1 - par)
            copy_latents(1)
            for n in range(4):
                square(n)
            copy_latents(2)
            for n in range(4, 8):
                square(n)
            copy_latents(3)
            square(8)
            key_rsqrt(b, 0, par)
            square(9)
            if t is not None:
                act_tail(act, t, 1 - par)
            for n in range(10, 16):
                square(n)
                if n == 10:
                    wait(act, "fractions", b, 1)
                    act.activation(f_1, f_f, ACT.Abs).then_inc(S("act_trig"), 1)
                    act.activation(f_sin, f_f, ACT.Sin, scale=TWO_PI).then_inc(S("act_trig"), 1)
                    act.wait_ge(S("act_trig"), b * 2 + 1)
                    act.activation(f_cos, f_1, ACT.Sin, scale=-TWO_PI, bias=math.pi / 2).then_inc(S("trig"), 1)
            if t is not None:
                act_olat(act, t)

        def act_tail(act, t, par):
            wait(act, "centred", t, 1)
            act.activation(Ssb[par], Ssb[par], ACT.Exp).then_inc(S("exp_done"), 1)

        def act_olat(act, t):
            wait(act, "lat_T", t, 1)
            o = olT.rearrange("p (h b q) -> p h b q", h=H, b=NB)[:, :, bass.ds(t, 1), :]
            act.activation(o, ps[MB][:, 256:256 + NS].rearrange("p (h o q) -> p h o q", h=H, o=1), ACT.Copy).then_inc(S("lat_copied"), 1)

        def scale_scores(ve, s, u, par):
            wait(ve, "rs_key", s, u + 1)
            wait(ve, "scored", s, 8 * (u + 1))
            rs = n2[:, par * P + u * 64:par * P + (u + 1) * 64]
            ve.tensor_tensor(v3(Ssb[par][:, u * 512:(u + 1) * 512], 64), v3(ps[SB[u]][:, :], 64), bc(rs, 2, NQ),
                             ALU.mult).then_inc(S("scaled"), 1)

        def ve_tail(ve, t, par, part):
            s64 = Ssb[par][0:NS, 1024:1088]
            if part == 0:
                scale_scores(ve, t, 1, par)
                ve.tensor_tensor(v3(s64, H), v3(s_new[0:NS, bass.ds(t * NS, NS)], H),
                                 bc(C("smask", NS)[:, bass.ds(t * NQ, NQ)], 1, H), ALU.add).then_inc(S("tail_dve"), 1)
                ve.wait_ge(S("tail_dve"), t * 3 + 1)
                ve.tensor_reduce(smx, Ssb[par].rearrange("p (n j) -> p j n", j=NS), AX, ALU.max).then_inc(S("max_ready"), 1)
            if part == 1:
                wait(ve, "max_T", t, 1)
                ve.tensor_reduce(m64, ps[MB][0:NS, 0:P], AX, ALU.max).then_inc(S("tail_dve"), 1)
                ve.wait_ge(S("tail_dve"), t * 3 + 2)
                ve.tensor_scalar(sdiag, ident[0:NS, 0:NS], m64, None, ALU.mult).then_inc(S("diag_ready"), 1)
            if part == 2:
                wait(ve, "max_row", t, 1)
                s = v3(Ssb[par], 17)
                ve.tensor_tensor(s, s, bc(ps[MB][:, 128:128 + NS], 1, 17), ALU.subtract).then_inc(S("centred"), 1)
            if part == 3:
                wait(ve, "exp_done", t, 1)
                ve.tensor_reduce(ssum, Ssb[par].rearrange("p (n j) -> p j n", j=NS), AX, ALU.add).then_inc(S("exp_summed"), 1)
            if part == 4:
                wait(ve, "values_done", t, 1)
                ve.reciprocal(rl, ps[AB][0:NS, KR:KR + 1]).then_inc(S("tail_dve"), 1)
                ve.wait_ge(S("tail_dve"), t * 3 + 3)
                wait(ve, "lat_T", t, 0)
                ve.tensor_scalar(olat[0:NS, :], ps[AB][0:NS, 0:KR], rl, None, ALU.mult).then_inc(S("lat_scaled"), 1)

        def ve_seq(ve, b, half, par, t):
            sl, til, tsl = seq_slices(b)

            def copy_rope(u):
                wait(ve, "kr_transposed", b, u + 1)
                wait(ve, "scored", b, 8 * (u - 1))
                ve.tensor_copy(krT[u], ps[KRB][:, 0:256]).then_inc(S("kr_copied"), 1)

            def sums(g):
                for n in range(4 * g, 4 * g + 4):
                    wait(ve, "squared", b, n + 1)
                    ve.tensor_reduce(n2[:, par * P + n * H:par * P + (n + 1) * H], v3(sq[n % 2], H), AX, ALU.add).then_inc(S("summed"), 1)

            def add_rope(u):
                ap = v3(n2[:, par * P + u * 64:par * P + (u + 1) * 64], 8)
                ve.tensor_reduce(kr2[:, :], v3(krsq, 8), AX, ALU.add).then_inc(S("dve_seq"), 1)
                ve.wait_ge(S("dve_seq"), b * 6 + (3 * u + 2))
                ve.tensor_scalar(kr2[:, :], kr2[:, :], 1 / QK, None, ALU.mult).then_inc(S("dve_seq"), 1)
                ve.wait_ge(S("dve_seq"), b * 6 + (3 * u + 3))
                wait(ve, "summed", b, 8 * (u + 1))
                ve.tensor_tensor(ap, ap, bc(kr2[:, :], 2, H), ALU.add).then_inc(S("sums_ready"), 1)

            def rope_squares(u):
                slot = 2 * par + u
                ve.tensor_tensor(krsq, cachr[slot], cachr[slot], ALU.mult).then_inc(S("dve_seq"), 1)
                ve.wait_ge(S("dve_seq"), b * 6 + (3 * u + 1))

            wait(ve, "scored", b, -16)
            ve.tensor_tensor(qrs[par].rearrange("p (s j) -> p s j", s=4), bc(qrp[:, sl], 1, 4),
                             bc(C("quad"), 2, NS), ALU.mult)
            copy_rope(0)
            if t is not None:
                ve_tail(ve, t, 1 - par, 0)
            wait(ve, "turns", b, 1)
            ve.tensor_scalar(f_2, f_t, MAGIC, MAGIC, ALU.add, ALU.subtract).then_inc(S("dve_f"), 1)
            ve.wait_ge(S("dve_f"), b + 1)
            ve.tensor_tensor(f_f, f_t, f_2, ALU.subtract).then_inc(S("fractions"), 1)
            sums(0)
            if t is not None:
                ve_tail(ve, t, 1 - par, 1)
            copy_rope(1)
            sums(1)
            rope_squares(0)
            add_rope(0)
            if t is not None:
                ve_tail(ve, t, 1 - par, 2)
            sums(2)
            wait(ve, "values_done", b, -1)
            scale_scores(ve, b, 0, par)
            if t is not None:
                ve_tail(ve, t, 1 - par, 3)
            sums(3)
            rope_squares(1)
            add_rope(1)
            if t is not None:
                ve_tail(ve, t, 1 - par, 4)
            wait(ve, "rotated", b, 1)
            ve.tensor_tensor(f_1, f_1, f_2, ALU.add).then_inc(S("dve_ssm"), 1)
            ve.tensor_tensor(f_3, f_3, f_4, ALU.subtract).then_inc(S("dve_ssm"), 1)
            ve.wait_ge(S("dve_ssm"), b * 6 + 2)
            for a, f in ((0, f_1), (1, f_3)):
                first = two(f)[:, :, SEQ:T].rearrange("p i (b q) -> p i b q", b=NB)[:, :, :, 0]
                h0 = st0[:, a * P:(a + 1) * P].rearrange("p (b i) -> p i b", b=NB)[:, til, :]
                ve.tensor_tensor(first, first, h0, ALU.add).then_inc(S("dve_ssm"), 1)
            ve.wait_ge(S("dve_ssm"), b * 6 + 4)
            ve.tensor_tensor_scan(f_2, f_t, f_1, 0.0, ALU.mult, ALU.add).then_inc(S("dve_ssm"), 1)
            ve.tensor_tensor_scan(f_4, f_t, f_3, 0.0, ALU.mult, ALU.add).then_inc(S("scanned"), 1)
            wait(ve, "products", b, 1)
            ve.tensor_tensor(bre[:, tsl], f_1, f_3, ALU.subtract).then_inc(S("dve_ssm"), 1)
            ve.tensor_tensor(bim[:, tsl], f_t, f_f, ALU.add).then_inc(S("states"), 1)

        def pairs_from(eng, n, body):
            body(0)
            with eng.Fori(1, n) as i:
                body(i)

        def rounds(eng, seq):
            seq(0, 0, 0, None)

            def two_sequences(i):
                seq(i * 2 + 1, i, 1, i * 2)
                seq(i * 2 + 2, i + 1, 0, i * 2 + 1)

            pairs_from(eng, (NB - 2) // 2, two_sequences)
            seq(NB - 1, NB // 2 - 1, 1, NB - 2)

        def pool_loop(pool):
            pool.wait_ge(S("pole_exps_ready"), 2)
            used(pool, "bu31")
            used(pool, "qr")
            rounds(pool, lambda b, half, par, t: pool_seq(pool, b, par, t is not None and not (isinstance(b, int) and b == NB - 1)))
            post_pool(pool)

        def pe_loop(pe):
            rounds(pe, lambda b, half, par, t: pe_seq(pe, b, half, par, t))
            for part in range(4):
                pe_tail(pe, NB - 1, 1, part)
            post_pe(pe)

        def act_loop(act):
            def seq(b, half, par, t):
                act_seq_(act, b, par, t)
            rounds(act, seq)
            ap = n2[:, P + 64:2 * P]
            wait(act, "sums_ready", NB - 1, 2)
            act.activation(ap, ap, ACT.Ln, bias=EPS).then_inc(S("act_rs"), 1)
            act.wait_ge(S("act_rs"), 2 * NB)
            act.activation(ap, ap, ACT.Exp, scale=-0.5).then_inc(S("rs_key"), 1)
            act_tail(act, NB - 1, 1)
            act_olat(act, NB - 1)
            post_act(act)

        def ve_loop(ve):
            for name in ("qr", "qa", "sn"):
                used(ve, name)
            rounds(ve, lambda b, half, par, t: ve_seq(ve, b, half, par, t))
            for part in range(5):
                ve_tail(ve, NB - 1, 1, part)
            post_ve(ve)
        qrs = [ckvT[:, 0:256], g_row[:, 0:256]]
        page_idx = sb("page_row_index", 4, U32)
        page_all = sb("page_row_indices", 2 * NB, U32)
        sraw = R[:, 10240:10496]
        craw = R[:, 10496:11520].rearrange("p (a m e s) -> p a m e s", a=2, m=4, e=2)
        xst = R[:, 11520:12544].rearrange("p (a i e c) -> p a i e c", a=2, i=LT, e=2)
        junk = R[:, 14080:15104]
        rt = [R[:, 12544 + 384 * i:12544 + 384 * (i + 1)] for i in range(4)]
        qr4 = R[:, 14080:15104].rearrange("p (h e d) -> p h e d", h=H, e=4)
        ldt = small[:, 0:2]
        ms1, ms2, msq, msk = small[:, 2:5], small[:, 5:11], small[:, 16:40], small[:, 40:64]
        msA, msS, msH = small[:, 64:67], small[:, 67:70], small[:, 70:73]

        def prm(k):
            return par[:, 16 * k:16 * k + 16]

        (p_dt, p_mag, p_ang, p_k, p_th, p_f, p_sin, p_cos, p_lr, p_li, p_den, p_cr, p_ci, p_a, p_b,
         p_ab) = [prm(k) for k in range(16)]

        def vcol(name):
            a, b = ROW[name]
            return vec[:, a:b]

        order = [("vec", 6), ("xT0", 0), ("xT1", 1), ("xT2", 2), ("xT3", 3), ("xT4", 4), ("xT5", 5),
                 ("page", 7), ("ct0", 6), ("u0", 0), ("u1", 1), ("u2", 2), ("u3", 3),
                 ("z0", 4), ("z1", 5), ("z2", 7), ("ct1", 6), ("bd0", 0), ("bd1", 1), ("cq0", 2), ("cq1", 3),
                 ("ckvT", 4), ("q00", 5), ("q01", 6), ("q10", 7), ("q11", 0), ("q20", 1), ("q21", 2),
                 ("k0", 3), ("k1", 4), ("k2", 5), ("v0", 6), ("v1", 7)]
        order += [(f"bu{i}", i % 8) for i in range(2 * LT)]
        order += [(f"qT{h}", h) for h in range(8)] + [(f"kT{h}", h) for h in range(8)]
        order += [("uk0", 0), ("uk1", 1), ("qr", 2), ("qa", 3), ("sn", 4)]
        nth, uses = {}, [0] * 8
        for name, b in order:
            nth[name] = (b, uses[b])
            uses[b] += 1
        pre_uses = list(uses)

        def fill(eng, name):
            b, n = nth[name]
            if n:
                eng.wait_ge(S(f"free{b}"), n)
            return ps[b]

        def filled(ins, name):
            ins.then_inc(S(f"full{nth[name][0]}"), 1)

        def read(eng, name):
            b, n = nth[name]
            eng.wait_ge(S(f"full{b}"), n + 1)
            return ps[b]

        def was_read(ins, name):
            return ins.then_inc(S(f"free{nth[name][0]}"), 1)

        def used(eng, name):
            b, n = nth[name]
            eng.wait_ge(S(f"free{b}"), n + 1)

        w_glu = LP[:, 0:2048].rearrange("p (k n) -> p k n", k=4)
        hstates = LP[:, 2048:2560]
        hlast = tmp[0][:, 0:2 * P]
        yT, g1, g2 = R[:, 12288:13568], R[:, 13568:14848], R[:, 14848:16128]
        soT = R[:, 16128:17664].rearrange("p (m t) -> p m t", m=4)
        sqT = KT[:, 0:1536].rearrange("p (m t) -> p m t", m=4)
        junk_a, junk_h = KT[:, 1536:2048], R[:, 13568:14592]
        Sp = CA[:, 0:3072].rearrange("p (h t) -> p h t", h=H)
        PT = [CA[:, 3072 + 384 * i:3072 + 384 * (i + 1)] for i in range(2)]
        g2row = CA[:, 3840:4864]
        att = QT[:, 0:1536]
        attT = QT[:, 1536:3072].rearrange("p (k t) -> p k t", k=4)
        xs = KT
        xsT = O1[:, 0:3072].rearrange("p (k t) -> p k t", k=KD)
        pm = [small[:, 80 + 16 * i:96 + 16 * i] for i in range(4)]
        nbg = small[:, 144:148]
        post = [(f"y{m}", m) for m in range(4)] + [("hf0", 4), ("hf1", 5)]
        post += [(f"s{h}", (6, 7, 4, 5)[h % 4]) for h in range(H)] + [("as", 0)]
        post += [(f"g{m}", m) for m in range(4)]
        post += [("o0", 0), ("o1", 1)]
        post += [(f"p{h}", 4 + h % 4) for h in range(H)]
        post += [("at0", 2), ("at1", 3), ("at2", 4), ("ss", 5)]
        post += [(f"w{i}{a}", 4 * (i % 2) + a) for i in range(TT) for a in range(4)]
        post += [(f"xt{i}", 4 + i % 4) for i in range(6)] + [("rt", 0), ("cum", 1)]
        for name, b in post:
            nth[name] = (b, uses[b])
            uses[b] += 1

        _off = [0]

        def rv(n):
            a = _off[0]
            _off[0] += n
            return QT[:, a:a + n]

        lgt, mask4, mask8a, mask8b = rv(108), rv(12), rv(24), rv(24)
        le8, work8, pairs, one = rv(24), rv(24), rv(192), rv(96)
        m4, m8, e4, w12, psel, tsum = rv(3), rv(6), rv(12), rv(6), rv(3), rv(3)
        routed, second, posm, pay = rv(96), rv(96), rv(96), rv(288)
        cnt, lst, gates = rv(1), rv(96), rv(NE)
        assert _off[0] <= 3072
        gall, sall = sb("gather_rows", NE, U32), sb("scatter_rows", NE, U32)
        gsi = sb("expert_row_index", 4, U32)
        most = sb("most_tokens", 1, I32)
        oh = CA[:, 0:3072].rearrange("p (i e s) -> p i e s", i=TT, e=8)
        ring = [R[:, 6144 * i:6144 * (i + 1)] for i in range(2)]
        Xg = [R[:, 12288 + D * i:12288 + D * (i + 1)] for i in range(2)]
        XgT = [R[:, 14336 + D * i:14336 + D * (i + 1)] for i in range(2)]
        Yo = [R[:, 16384 + D * i:16384 + D * (i + 1)] for i in range(2)]
        exb, rcb, hmb, hS, hTb = [O1[:, 256 * i + 3072:256 * (i + 1) + 3072] for i in range(5)]
        outs_total = 6 + 4 + 3

        def load_expert(sp, r, e, eh, s):
            sl = bass.ds(e, 1)
            need(sp, "gate_up_done", r * NE + e - 1)
            for a, name in enumerate(("w_gate", "w_up")):
                sp.dma_start(ring[s][:, 2048 * a:2048 * (a + 1)],
                             I[name][0][sl].rearrange("e (p k) f -> (e p) (k f)", k=KD)).then_inc(S(f"gate_up_loaded{s}"), 16)
            need(sp, "down_done", (r * NE + e) * 2 - 2)
            sp.dma_start(ring[s][:, 4096:6144],
                         I["w_down"][0][sl].rearrange("e (p j) n -> (e p) (j n)", j=2)).then_inc(S(f"down_loaded{s}"), 16)

        def more_rounds(eng, round_):
            eng.wait_ge(S("counts_ready"), 1)
            n = eng.value_load(most[0:1, 0:1], min_val=0, max_val=T)
            with eng.Fori(1, ROUNDS) as r:
                with eng.If(n > r * SLOTS):
                    round_(r)
                eng.nop()

        def post_sync(sp):
            wait(sp, "scored", NB - 1, 16)
            wait(sp, "summed", NB - 1, 16)
            sp.dma_start(w_glu, I["ssm_w_glu"][0].rearrange("(k p) n -> p k n", p=P)).then_inc(S("w_glu_loaded"), 16)
            wait(sp, "values_done", NB - 1, 1)
            sp.dma_start(g2row, I["norm2_g"].to_broadcast([P, D])).then_inc(S("g2_loaded"), 16)
            with nc.allow_non_contiguous_dma(reason="router weights"):
                used(sp, "y3")
                sp.dma_start(w_r[:, :].rearrange("p (k n) -> p k n", k=KD)[:, :, 0:NG],
                             I["w_router_group"][0].rearrange("(k p) n -> p k n", p=P)).then_inc(S("router_loaded"), 16)
                sp.dma_start(w_r[:, :].rearrange("p (k n) -> p k n", k=KD)[:, :, NG:],
                             I["w_router_expert"][0].rearrange("(k p) n -> p k n", p=P)).then_inc(S("router_loaded"), 16)
                sp.dma_start(b_r[:, 0:NG], I["b_router_group"].to_broadcast([P, NG])).then_inc(S("router_loaded"), 16)
                sp.dma_start(b_r[:, NG:], I["b_router_expert"].to_broadcast([P, NE])).then_inc(S("router_loaded"), 16)
            used(sp, "hf0")
            used(sp, "hf1")
            for a, (pn, sn) in enumerate((("re_p", "re_s"), ("im_p", "im_s"))):
                sp.dma_start(O[pn].rearrange("o (i e) p -> (o i) (e p)", e=2), hstates[0:LT, 256 * a:256 * a + P]).then_inc(S("outputs_stored"), 16)
                sp.dma_start(O[sn].rearrange("o b (i e) p -> (o b i) (e p)", e=2), hstates[:, 256 * a + P:256 * (a + 1)]).then_inc(S("outputs_stored"), 16)
            for s in range(2):
                load_expert(sp, 0, s, 0, s)
            for i in range(TT):
                n = P if i < 2 else NS
                sp.wait_ge(S("xs_ready"), i + 1)
                sp.dma_start(xs_dram[i * P:i * P + n, :], xs[0:n, i * D:(i + 1) * D]).then_inc(S("xs_stored"), 16)

            def round_(r):
                load_expert(sp, r, 2, 1, 0)

                def two_experts(i):
                    load_expert(sp, r, i * 2 + 3, i + 1, 1)
                    load_expert(sp, r, i * 2 + 4, i + 2, 0)

                pairs_from(sp, (NE - 4) // 2, two_experts)
                load_expert(sp, r, NE - 1, NE // 2 - 1, 1)

            round_(0)

            def later(r):
                sp.wait_ge(S("down_done"), r * (2 * NE))
                for s in range(2):
                    load_expert(sp, r, s, 0, s)
                round_(r)

            more_rounds(sp, later)
            sp.wait_ge(S("moe_done"), 1)
            for i in range(TT):
                n = P if i < 2 else NS
                for a in range(2):
                    sp.dma_start(R[0:n, 3072 * a + i * D:3072 * a + (i + 1) * D],
                                 y2_dram[a * T + i * P:a * T + i * P + n, :]).then_inc(S(f"rows{i}_back"), 16)
            for i in range(TT):
                sp.wait_ge(S("y_ready"), i + 1)
                if i < 2:
                    sp.dma_start(O["y_p"][0, i * P:(i + 1) * P, :], x[:, i * D:(i + 1) * D]).then_inc(S("outputs_stored"), 16)
                else:
                    sp.dma_start(O["y_s"].rearrange("b t d -> (b t) d"), x[0:NS, 2 * D:]).then_inc(S("outputs_stored"), 16)
            sp.wait_ge(S("outputs_stored"), 16 * outs_total)

        def post_pool(pool):
            wait(pool, "centred", NB - 1, 1)
            wait(pool, "values_done", NB - 1, 1)
            pool.memset(soT[:, :, T:TP], 0.0).then_inc(S("post_pads"), 1)
            used(pool, "s7")
            pool.memset(sqT[:, :, T:TP], 0.0).then_inc(S("post_pads"), 1)
            pool.wait_ge(S("post_pads"), 2)
            pool.memset(att[NS:P, 1024:1536], 0.0).then_inc(S("post_pads"), 1)
            pool.wait_ge(S("post_pads"), 3)
            pool.wait_ge(S("xs_ready"), TT)
            for i in range(2):
                pool.memset(Xg[i], 0.0).then_inc(S("gather_cleared"), 1)
            pool.wait_ge(S("gather_cleared"), 2)
            pool.wait_ge(S("xs_stored"), 16 * TT)

            column = pool.alloc_register("expert_column")

            def column_of(r, e):
                if not isinstance(e, int):
                    return bass.ds(e, 1)
                if isinstance(r, int):
                    return slice(e, e + 1)
                pool.reg_add(column, r, e)
                pool.reg_alu(column, column, e, ALU.min)
                return bass.ds(pool.snap(column, min_val=0, max_val=NE - 1), 1)

            def gather(r, e, eh, s):
                need(pool, "x_T", (r * NE + e) * 2 - 2)
                pool.tensor_copy(gsi[:, s:s + 1], gall[:, column_of(r, e)]).then_inc(S("gather_index"), 1)
                pool.wait_ge(S("gather_index"), r * NE + e + 1)
                last = limit(pool, T - 1, r * NE + e)
                pool.indirect_dma_start(out=Xg[s], out_offset=None, in_=xs_dram,
                                        in_offset=bass.IndirectOffsetOnAxis(ap=gsi[:, s:s + 1], axis=0),
                                        bounds_check=last, oob_is_err=False).then_inc(S(f"tokens{s}"), 16)

            def scatter(r, e, eh, s):
                pool.wait_ge(S("y_copied0"), r * NE + e + 1)
                pool.wait_ge(S("y_copied1"), r * NE + e + 1)
                value = (r * (NE // 2) + eh) * 16
                need(pool, f"scattered{s}", value)
                pool.tensor_copy(gsi[:, 2 + s:3 + s], sall[:, column_of(r, e)]).then_inc(S("scatter_index"), 1)
                pool.wait_ge(S("scatter_index"), r * NE + e + 1)
                last = limit(pool, 2 * T - 1, r * NE + e)
                pool.indirect_dma_start(out=y2_dram, out_offset=bass.IndirectOffsetOnAxis(ap=gsi[:, 2 + s:3 + s], axis=0),
                                        in_=Yo[s], in_offset=None, bounds_check=last, oob_is_err=False).then_inc(S(f"scattered{s}"), 16)

            def round_(r):
                pool.wait_ge(S("lists_ready"), r + 1)
                gather(r, 0, 0, 0)
                gather(r, 1, 0, 1)
                gather(r, 2, 1, 0)
                def two_experts(i):
                    gather(r, i * 2 + 3, i + 1, 1)
                    scatter(r, i * 2, i, 0)
                    gather(r, i * 2 + 4, i + 2, 0)
                    scatter(r, i * 2 + 1, i, 1)

                pairs_from(pool, (NE - 4) // 2, two_experts)
                gather(r, NE - 1, NE // 2 - 1, 1)
                for e in range(NE - 4, NE):
                    scatter(r, e, e // 2, e % 2)
                for s in range(2):
                    pool.wait_ge(S(f"scattered{s}"), (r + 1) * (16 * NE // 2))

            round_(0)
            more_rounds(pool, round_)
            pool.memset(small[0:1, 150:151], 0.0).then_inc(S("moe_done"), 1)

        def post_pe(pe):
            wait(pe, "scaled", NB - 1, 2)
            wait(pe, "squared", NB - 1, 16)
            wait(pe, "kr_copied", NB - 1, 2)
            wait(pe, "lat_copied", NB - 1, 1)
            wait(pe, "states", NB - 1, 1)
            for m in range(4):
                b = fill(pe, f"y{m}")
                for j in range(4):
                    i = 4 * m + j
                    o = b[32 * j:32 * j + 32, 0:T]
                    c = m * P + 32 * j
                    pe.matmul(o, CT[:, c:c + 32], bre[:, i * T:(i + 1) * T], start=True, stop=False)
                    ins = pe.matmul(o, CT[:, 512 + c:512 + c + 32], bim[:, i * T:(i + 1) * T], start=False, stop=True)
                filled(ins, f"y{m}")
            for a, src in enumerate((bre, bim)):
                b = fill(pe, f"hf{a}")
                per_tile = v3(src, LT)
                pe.transpose(b[0:LT, 0:P], per_tile[:, :, SEQ - 1], ident)
                pe.wait_ge(S("last_states"), a + 1)
                filled(pe.transpose(b[:, P:2 * P], hlast[:, a * P:(a + 1) * P], ident), f"hf{a}")
            for h in range(H):
                b = fill(pe, f"s{h}")
                pe.matmul(b[:, 0:P], qT[0:QK, h, 0:P], kT[0:QK, h, 0:P], start=True, stop=True)
                filled(pe.matmul(b[:, P:3 * P], qT[0:QK, h, P:2 * P], kT[0:QK, h, 0:2 * P], start=True, stop=True), f"s{h}")
            b = fill(pe, "as")
            for h in range(H):
                ins = pe.matmul(b[0:NS, h * VD:(h + 1) * VD], olT[:, h * NS:(h + 1) * NS], w_uv[:, h * VD:(h + 1) * VD],
                                start=True, stop=True)
            filled(ins, "as")
            pe.wait_ge(S("gelu_ready"), 1)
            pe.wait_ge(S("w_glu_loaded"), 16)
            for m in range(4):
                b = fill(pe, f"g{m}")
                for k in range(4):
                    ins = pe.matmul(b[:, 0:T], w_glu[:, k, m * P:(m + 1) * P], yT[:, k * T:(k + 1) * T],
                                    start=(k == 0), stop=(k == 3))
                filled(ins, f"g{m}")
            pe.wait_ge(S("prompt_exp_ready"), 1)
            o0, o1 = fill(pe, "o0"), fill(pe, "o1")

            def prompt_T(h):
                b = fill(pe, f"p{h}")
                for j in range(3):
                    ins = pe.transpose(b[:, j * P:(j + 1) * P], Sp[:, h, j * P:(j + 1) * P], ident)
                filled(ins, f"p{h}")

            prompt_T(0)
            for h in range(H):
                if h + 1 < H:
                    prompt_T(h + 1)
                used(pe, f"p{h}")
                pt, c = PT[h % 2], slice(h * VD, (h + 1) * VD)
                v0, v1 = v[:, h * VD:(h + 1) * VD], v[:, 512 + h * VD:512 + (h + 1) * VD]
                i0 = pe.matmul(o0[:, c], pt[:, 0:P], v0, start=True, stop=True)
                if h == H - 1:
                    filled(i0, "o0")
                pe.matmul(o1[:, c], pt[:, P:2 * P], v0, start=True, stop=False)
                i1 = pe.matmul(o1[:, c], pt[:, 2 * P:3 * P], v1, start=False, stop=True)
                if h == H - 1:
                    filled(i1, "o1")
                else:
                    i1.then_inc(S("prompt_values"), 1)
            pe.wait_ge(S("att_ready"), 3)
            pe.wait_ge(S("post_pads"), 3)
            for i in range(TT):
                b = fill(pe, f"at{i}")
                for k in range(4):
                    ins = pe.transpose(b[:, k * P:(k + 1) * P], att[:, i * 512 + k * P:i * 512 + (k + 1) * P], ident)
                filled(ins, f"at{i}")
            pe.wait_ge(S("ssm_squared"), 1)
            b = fill(pe, "ss")
            for i in range(TT):
                for m in range(4):
                    ins = pe.matmul(b[:, i:i + 1], sqT[:, m, i * P:(i + 1) * P], C("ones")[:, 0:1], start=(m == 0), stop=(m == 3))
            filled(ins, "ss")
            pe.wait_ge(S("w_out_loaded"), 16)
            pe.wait_ge(S("so_ready"), 1)
            for i in range(TT):
                used(pe, f"at{i}")
            for i in range(TT):
                for a in range(4):
                    src, k0, n0 = (soT, 0, 512 * a) if a < 2 else (attT, 4, 512 * (a - 2))
                    b = fill(pe, f"w{i}{a}")
                    for k in range(4):
                        ins = pe.matmul(b[:, :], src[:, k, i * P:(i + 1) * P], w_out[:, k0 + k, n0:n0 + 512],
                                        start=(k == 0), stop=(k == 3))
                    filled(ins, f"w{i}{a}")
            for i in range(TT):
                pe.wait_ge(S("xs_ready"), i + 1)
                for g in range(2):
                    b = fill(pe, f"xt{2 * i + g}")
                    for k in range(4):
                        c = i * D + (4 * g + k) * P
                        ins = pe.transpose(b[:, k * P:(k + 1) * P], xs[:, c:c + P], ident)
                    filled(ins, f"xt{2 * i + g}")
            for i in range(6):
                used(pe, f"xt{i}")
            pe.wait_ge(S("router_loaded"), 64)
            b = fill(pe, "rt")
            wr = w_r[:, :].rearrange("p (k n) -> p k n", k=KD)
            for i in range(TT):
                for k in range(KD):
                    ins = pe.matmul(b[:, i * 36:(i + 1) * 36], xsT[:, k, i * P:(i + 1) * P], wr[:, k, :],
                                    start=(k == 0), stop=(k == KD - 1))
            filled(ins, "rt")
            pe.wait_ge(S("routed_ready"), 1)
            b = fill(pe, "cum")
            for i in range(TT + 1):
                before = range(min(i + 1, TT))
                for j in before:
                    ins = pe.matmul(b[:, i * NE:(i + 1) * NE], C("tri") if j == i else C("ones"), routed[:, j * NE:(j + 1) * NE],
                                    start=(j == 0), stop=(j == before[-1]))
            filled(ins, "cum")
            for i in range(8):
                pe.wait_ge(S(f"free{i}"), uses[i])

            def lists(r):
                for c in range(4):
                    pe.wait_ge(S("onehots_ready"), r * 4 + (c + 1))
                    for e in range(8):
                        n = 8 * c + e
                        for i in range(TT):
                            ins = pe.matmul(ps[7][:, n * 3:n * 3 + 3], oh[:, i, e, :],
                                            pay[:, (i * NE + n) * 3:(i * NE + n) * 3 + 3], start=(i == 0), stop=(i == TT - 1))
                    ins.then_inc(S("lists_made"), 1)

            def xT(r, e, eh, s):
                pe.wait_ge(S(f"tokens{s}"), (r * (NE // 2) + eh + 1) * 16)
                for g in range(2):
                    need(pe, f"x_copied{g}", r * NE + e)
                    view = Xg[s].rearrange("p (c k) -> p k c", k=KD)
                    for k in range(4):
                        ins = pe.transpose(ps[g][:, k * P:(k + 1) * P], view[:, 4 * g + k, :], ident)
                    ins.then_inc(S("x_T"), 1)

            def gate_up(r, e, eh, s):
                pe.wait_ge(S(f"gate_up_loaded{s}"), (r * (NE // 2) + eh + 1) * 32)
                for g in range(2):
                    pe.wait_ge(S(f"x_copied{g}"), r * NE + e + 1)
                need(pe, "act_ready", r * NE + e - 1)
                w = ring[s][:, 0:4096].rearrange("p (a k f) -> p k a f", a=2, k=KD)
                for k in range(KD):
                    ins = pe.matmul(ps[2 + s][:, :].rearrange("p (a f) -> p a f", a=2), XgT[s][:, k * P:(k + 1) * P], w[:, k],
                                    start=(k == 0), stop=(k == KD - 1))
                ins.then_inc(S("gate_up_done"), 1)

            def h_T(r, e, eh, s):
                pe.wait_ge(S("act_ready"), r * NE + e + 1)
                need(pe, "h_copied", r * NE + e)
                view = hS.rearrange("p (c j) -> p j c", j=2)
                for j in range(2):
                    ins = pe.transpose(ps[4][:, j * P:(j + 1) * P], view[:, j, :], ident)
                ins.then_inc(S("h_T"), 1)

            def down(r, e, eh, s):
                pe.wait_ge(S("h_copied"), r * NE + e + 1)
                pe.wait_ge(S(f"down_loaded{s}"), (r * (NE // 2) + eh + 1) * 16)
                for g in range(2):
                    need(pe, f"y_copied{g}", r * NE + e)
                    w = ring[s][:, 4096:6144].rearrange("p (j n) -> p j n", j=2)
                    for j in range(2):
                        ins = pe.matmul(ps[5 + g][:, :], hTb[:, j * P:(j + 1) * P],
                                        w[:, j, g * 512:(g + 1) * 512], start=(j == 0), stop=(j == 1))
                    ins.then_inc(S("down_done"), 1)

            def round_(r):
                lists(r)
                xT(r, 0, 0, 0)
                gate_up(r, 0, 0, 0)
                xT(r, 1, 0, 1)
                h_T(r, 0, 0, 0)
                def two_experts(i):
                    gate_up(r, i * 2 + 1, i, 1)
                    xT(r, i * 2 + 2, i + 1, 0)
                    down(r, i * 2, i, 0)
                    h_T(r, i * 2 + 1, i, 1)
                    gate_up(r, i * 2 + 2, i + 1, 0)
                    xT(r, i * 2 + 3, i + 1, 1)
                    down(r, i * 2 + 1, i, 1)
                    h_T(r, i * 2 + 2, i + 1, 0)

                pairs_from(pe, (NE - 2) // 2, two_experts)
                e = NE - 1
                gate_up(r, e, e // 2, 1)
                down(r, e - 1, (e - 1) // 2, 0)
                h_T(r, e, e // 2, 1)
                down(r, e, e // 2, 1)

            round_(0)
            more_rounds(pe, round_)

        def post_act(act):
            st = chain(act, "act_steps")

            def rsqrt(ap, src, scale):
                st.link(act.activation(ap, src, ACT.Ln, bias=EPS, scale=scale))
                return act.activation(ap, ap, ACT.Exp, scale=-0.5)

            wait(act, "states", NB - 1, 1)
            for a, src in enumerate((bre, bim)):
                last = v3(src, LT)[:, :, SEQ:T].rearrange("p i (b q) -> p b i q", b=NB)[:, :, :, NQ - 1]
                act.activation(v3(hlast[:, a * P:(a + 1) * P], NB), last, ACT.Copy).then_inc(S("last_states"), 1)
            act.wait_ge(S("gelu_inner"), 1)
            act.activation(g1, g1, ACT.Exp, scale=-2 * math.sqrt(2 / math.pi)).then_inc(S("gelu_exp"), 1)
            for a in range(2):
                b = read(act, f"hf{a}")
                st.inc(act.activation(hstates[0:LT, 256 * a:256 * a + P], b[0:LT, 0:P], ACT.Copy))
                st.sync()
                was_read(act.activation(hstates[:, 256 * a + P:256 * (a + 1)], b[:, P:2 * P], ACT.Copy), f"hf{a}")
            act.wait_ge(S("bias_negated"), 1)
            act.wait_ge(S("gelu_ready"), 1)
            for m in range(4):
                b = read(act, f"g{m}")
                was_read(act.activation(g1[:, m * T:(m + 1) * T], b[:, 0:T], ACT.Exp, scale=-1.0, bias=nbg[:, m:m + 1]), f"g{m}")
            act.wait_ge(S("prompt_centred"), 1)
            act.activation(CA[:, 0:3072], CA[:, 0:3072], ACT.Exp).then_inc(S("prompt_exp_ready"), 1)
            for h in range(H):
                if h >= 2:
                    act.wait_ge(S("prompt_values"), h - 1)
                b = read(act, f"p{h}")
                was_read(act.activation(PT[h % 2], b[:, 0:384], ACT.Copy), f"p{h}")
            act.wait_ge(S("glu_out"), 1)
            used(act, "s7")
            act.activation(sqT[:, :, 0:T], v3(yT, 4), ACT.Square).then_inc(S("ssm_squared"), 1)
            act.wait_ge(S("att_ready"), 3)
            act.wait_ge(S("post_pads"), 3)
            for i in range(TT):
                st.link(act.activation(junk_a, att[:, i * 512:(i + 1) * 512], ACT.Square, scale=512 ** -0.5, accum_out=msA[:, i:i + 1]))
            rsqrt(msA, msA, 1.0).then_inc(S("rs_att_ready"), 1)
            b = read(act, "ss")
            st.link(act.activation(msS, b[:, 0:TT], ACT.Ln, bias=EPS, scale=1 / 512))
            was_read(act.activation(msS, msS, ACT.Exp, scale=-0.5), "ss")
            for i in range(TT):
                act.wait_ge(S("h_ready"), i + 1)
                st.link(act.activation(junk_h, x[:, i * D:(i + 1) * D], ACT.Square, scale=1 / 32, accum_out=msH[:, i:i + 1]))
                rsqrt(msH[:, i:i + 1], msH[:, i:i + 1], 1.0).then_inc(S("rs2_ready"), 1)
            for i in range(1, 6, 2):
                b = read(act, f"xt{i}")
                was_read(act.activation(xsT[:, 4:8, (i // 2) * P:(i // 2 + 1) * P], v3(b[:, :], 4), ACT.Copy), f"xt{i}")
            act.wait_ge(S("router_diffs"), 1)
            st.link(act.activation(e4, e4, ACT.Exp))
            act.activation(w12[:, 0:3], w12[:, 0:3], ACT.Exp).then_inc(S("router_exp"), 1)

            def x_copy(r, e, s):
                act.wait_ge(S("x_T"), (r * NE + e) * 2 + 1)
                need(act, "gate_up_done", r * NE + e - 1)
                act.activation(XgT[s][:, 0:512], ps[0][:, :], ACT.Copy).then_inc(S("x_copied0"), 1)

            def exp_(r, e, s):
                act.wait_ge(S("gate_up_done"), r * NE + e + 1)
                need(act, "act_ready", r * NE + e)
                act.activation(exb, ps[2 + s][:, 0:FE], ACT.Exp, scale=-1.0).then_inc(S("gate_exp"), 1)

            def y_copy(r, e, eh, s):
                act.wait_ge(S("down_done"), (r * NE + e) * 2 + 1)
                value = (r * (NE // 2) + eh) * 16
                need(act, f"scattered{s}", value)
                act.activation(Yo[s][:, 0:512], ps[5][:, :], ACT.Copy).then_inc(S("y_copied0"), 1)

            def round_(r):
                x_copy(r, 0, 0)
                exp_(r, 0, 0)
                x_copy(r, 1, 1)
                def two_experts(i):
                    exp_(r, i * 2 + 1, 1)
                    x_copy(r, i * 2 + 2, 0)
                    y_copy(r, i * 2, i, 0)
                    exp_(r, i * 2 + 2, 0)
                    x_copy(r, i * 2 + 3, 1)
                    y_copy(r, i * 2 + 1, i, 1)

                pairs_from(act, (NE - 2) // 2, two_experts)
                e = NE - 1
                exp_(r, e, 1)
                y_copy(r, e - 1, (e - 1) // 2, 0)
                y_copy(r, e, e // 2, 1)

            round_(0)
            more_rounds(act, round_)

        def post_ve(ve):
            st = chain(ve, "dve_steps")
            tt = ve.tensor_tensor
            for m in range(4):
                b = read(ve, f"y{m}")
                was_read(ve.scalar_tensor_tensor(out=yT[:, m * T:(m + 1) * T], in0=uT[:, m * T:(m + 1) * T],
                                                 scalar=vcol("ssm_d")[:, m:m + 1], in1=b[:, 0:T], op0=ALU.mult, op1=ALU.add), f"y{m}")
            for m in range(4):
                used(ve, f"y{m}")
            st.link(tt(g1, yT, yT, ALU.mult))
            st.link(ve.tensor_scalar(g1, g1, 0.044715, 1.0, ALU.mult, ALU.add))
            st.link(tt(g1, g1, yT, ALU.mult))
            ve.tensor_scalar(g1, g1, -50.0, None, ALU.max).then_inc(S("gelu_inner"), 1)
            for h in range(H):
                b = read(ve, f"s{h}")
                was_read(tt(Sp[:, h, :], b[:, 0:384], C("causal"), ALU.add), f"s{h}")
            ve.wait_ge(S("gelu_exp"), 1)
            st.link(ve.tensor_scalar(g2, g1, 1.0, None, ALU.add))
            st.link(ve.reciprocal(g2, g2))
            tt(yT, yT, g2, ALU.mult).then_inc(S("gelu_ready"), 1)
            ve.tensor_scalar(nbg, vcol("ssm_b_glu"), -1.0, None, ALU.mult).then_inc(S("bias_negated"), 1)
            for h in range(H):
                used(ve, f"s{h}")
            b = read(ve, "as")
            was_read(ve.tensor_copy(att[0:NS, 1024:1536], b[0:NS, :]), "as")
            blocks = (Sp[:, :, 0:P], Sp[:, :, P:3 * P])
            for i, s in enumerate(blocks):
                st.link(ve.tensor_reduce(pm[0][:, 8 * i:8 * i + 8], s, AX, ALU.max))
            for i, s in enumerate(blocks):
                ins = tt(s, s, bc(pm[0][:, 8 * i:8 * i + 8], 2, (i + 1) * P), ALU.subtract)
                if i == 0:
                    st.inc(ins)
            ins.then_inc(S("prompt_centred"), 1)
            for m in range(4):
                used(ve, f"g{m}")
            st.link(ve.tensor_scalar(g2, g1, 1.0, None, ALU.add))
            st.link(ve.reciprocal(g2, g2))
            tt(yT, yT, g2, ALU.mult).then_inc(S("glu_out"), 1)
            ve.wait_ge(S("glu_out"), 1)
            tt(soT[:, :, 0:T], v3(yT, 4), bc(vcol("out_norm_ssm"), 2, T), ALU.mult).then_inc(S("so_ready"), 1)
            ve.wait_ge(S("prompt_exp_ready"), 1)
            for i, s in enumerate(blocks):
                st.link(ve.tensor_reduce(pm[1][:, 8 * i:8 * i + 8], s, AX, ALU.add))
            st.link(ve.reciprocal(pm[1], pm[1]))
            used(ve, "as")
            for i in range(2):
                b = read(ve, f"o{i}")
                was_read(tt(v3(att[:, i * 512:(i + 1) * 512], H), v3(b[:, :], H), bc(pm[1][:, 8 * i:8 * i + 8], 2, VD), ALU.mult), f"o{i}")
            used(ve, "o0")
            used(ve, "o1")
            st.link(ve.tensor_copy(pm[2][:, 0:1], pm[1][:, 0:1]))
            ve.tensor_copy(pm[2][:, 1:2], pm[2][:, 0:1]).then_inc(S("att_ready"), 3)
            for i in range(TT):
                b = read(ve, f"at{i}")
                was_read(tt(attT[:, :, i * P:(i + 1) * P], v3(b[:, :], 4), bc(vcol("out_norm_attn"), 2, P), ALU.mult), f"at{i}")
            used(ve, "ss")
            ve.wait_ge(S("rs_att_ready"), 1)
            for i in range(TT):
                for a in range(4):
                    b = read(ve, f"w{i}{a}")
                    o = x[:, i * D + 512 * (a % 2):i * D + 512 * (a % 2 + 1)]
                    rs = (msS if a < 2 else msA)[:, i:i + 1]
                    if a == 2:
                        used(ve, f"w{i}0")
                        used(ve, f"w{i}1")
                    was_read(ve.scalar_tensor_tensor(out=o, in0=b[:, :], scalar=rs, in1=o, op0=ALU.mult, op1=ALU.add), f"w{i}{a}")
                used(ve, f"w{i}2")
                used(ve, f"w{i}3")
                ve.tensor_copy(pm[2][:, 2 + i:3 + i], pm[2][:, 0:1]).then_inc(S("h_ready"), 1)
            ve.wait_ge(S("g2_loaded"), 16)
            for i in range(TT):
                ve.wait_ge(S("rs2_ready"), i + 1)
                ve.scalar_tensor_tensor(out=xs[:, i * D:(i + 1) * D], in0=x[:, i * D:(i + 1) * D], scalar=msH[:, i:i + 1],
                                        in1=g2row, op0=ALU.mult, op1=ALU.mult).then_inc(S("xs_ready"), 1)
            for i in range(0, 6, 2):
                b = read(ve, f"xt{i}")
                was_read(ve.tensor_copy(xsT[:, 0:4, (i // 2) * P:(i // 2 + 1) * P], v3(b[:, :], 4)), f"xt{i}")
            b = read(ve, "rt")
            lg = v3(lgt, TT)
            was_read(tt(lg, v3(b[:, 0:108], TT), bc(b_r[:, :], 1, TT), ALU.add), "rt")
            used(ve, "rt")

            def first_max(src, n, m, mask):
                st.link(ve.tensor_reduce(m, src, AX, ALU.max))
                eq = v3(one[:, 0:TT * n], TT)
                st.link(tt(eq, src, bc(m, 2, n), ALU.is_equal))
                prs = pairs[:, 0:TT * n * n].rearrange("p (i a b) -> p i a b", i=TT, a=n)
                early = C("early8" if n == 8 else "early4").rearrange("p (a b) -> p a b", a=n)
                st.link(tt(prs, bc(eq, 2, n), bc(early, 1, TT), ALU.mult))
                st.link(ve.tensor_reduce(work8[:, 0:TT * n], prs.rearrange("p i a b -> p (i a) b"), AX, ALU.add))
                st.link(ve.scalar_tensor_tensor(out=mask, in0=work8[:, 0:TT * n], scalar=0.0, in1=one[:, 0:TT * n],
                                                op0=ALU.is_equal, op1=ALU.mult))

            first_max(lg[:, :, 0:NG], NG, m4, mask4)
            st.inc(tt(v3(e4, TT), lg[:, :, 0:NG], bc(m4, 2, NG), ALU.subtract))
            grp = mask4.rearrange("p (i g) -> p i g", i=TT)
            t32 = one.rearrange("p (i g e) -> p i g e", i=TT, g=NG)
            st.link(tt(t32, lg[:, :, NG:].rearrange("p i (g e) -> p i g e", g=NG), bc(grp, 3, EG), ALU.mult))
            st.link(ve.tensor_reduce(v3(le8, TT), t32.rearrange("p i g e -> p i e g"), AX, ALU.add))
            first_max(v3(le8, TT), EG, m8[:, 0:3], mask8a)
            st.link(ve.scalar_tensor_tensor(out=le8, in0=mask8a, scalar=NEG, in1=le8, op0=ALU.mult, op1=ALU.add))
            first_max(v3(le8, TT), EG, m8[:, 3:6], mask8b)
            tt(w12[:, 0:3], m8[:, 3:6], m8[:, 0:3], ALU.subtract).then_inc(S("router_diffs"), 1)
            ve.wait_ge(S("router_exp"), 1)
            st.link(ve.tensor_reduce(psel, v3(e4, TT), AX, ALU.add))
            st.link(ve.tensor_scalar(tsum, w12[:, 0:3], 1.0, None, ALU.add))
            st.link(tt(psel, psel, tsum, ALU.mult))
            st.link(ve.reciprocal(psel, psel))
            st.link(tt(w12[:, 3:6], w12[:, 0:3], psel, ALU.mult))
            m8a, m8b = v3(mask8a, TT), v3(mask8b, TT)
            ga, gb = v3(work8, TT), v3(le8, TT)
            st.link(tt(ga, m8a, bc(psel, 2, EG), ALU.mult))
            st.link(tt(gb, m8b, bc(w12[:, 3:6], 2, EG), ALU.mult))
            st.link(tt(ga, ga, gb, ALU.add))
            st.link(tt(m8a, m8a, m8b, ALU.add))

            def spread(dst, src8):
                return tt(dst, bc(src8, 2, NG), bc(grp, 3, EG), ALU.mult)

            def four(ap):
                return ap.rearrange("p (i g e) -> p i g e", i=TT, g=NG)

            st.link(spread(four(routed), m8a))
            tt(v3(routed, TT), v3(routed, TT), bc(C("valid"), 2, NE), ALU.mult).then_inc(S("routed_ready"), 1)
            st.link(spread(four(second), m8b))
            pv = pay.rearrange("p (i e c) -> p i e c", i=TT, e=NE)
            st.link(spread(pay.rearrange("p (i g e c) -> p i g e c", i=TT, g=NG, e=EG)[:, :, :, :, 2], ga))
            st.link(ve.tensor_scalar(tsum, C("tok"), 1.0, None, ALU.add))
            st.link(ve.tensor_scalar(v3(second, TT), v3(second, TT), float(T), None, ALU.mult))
            st.link(tt(pv[:, :, :, 1], v3(second, TT), bc(tsum, 2, NE), ALU.add))
            st.link(ve.tensor_scalar(v3(second, TT), v3(second, TT), 0.0, None, ALU.mult))
            st.link(tt(pv[:, :, :, 0], v3(second, TT), bc(tsum, 2, NE), ALU.add))
            b = read(ve, "cum")
            st.link(ve.scalar_tensor_tensor(out=posm, in0=b[:, 0:3 * NE], scalar=1.0, in1=routed, op0=ALU.add, op1=ALU.mult))
            st.link(ve.tensor_scalar(posm, posm, -1.0, None, ALU.add))
            st.link(ve.tensor_reduce(cnt, b[:, 3 * NE:4 * NE], AX, ALU.max))
            st.inc(ve.tensor_copy(most[:, :], cnt))
            was_read(ve.tensor_copy(pm[2][:, 6:7], cnt), "cum")
            used(ve, "cum")
            ve.tensor_copy(pm[2][:, 7:8], cnt).then_inc(S("counts_ready"), 1)

            def lists(r):
                for c in range(4):
                    need(ve, "lists_made", r * 4 + c)
                    for i in range(TT):
                        p = posm[:, i * NE + 8 * c:i * NE + 8 * c + 8]
                        ins = tt(oh[:, i], bc(p, 2, SLOTS), bc(C("slot"), 1, 8), ALU.is_equal)
                    ins.then_inc(S("onehots_ready"), 1)
                ve.wait_ge(S("lists_made"), r * 4 + 4)
                l3 = ps[7][:, 0:3 * NE].rearrange("p (e c) -> p c e", c=3)
                ve.tensor_scalar(lst[:, 0:2 * NE].rearrange("p (c e) -> p c e", c=2), l3[:, 0:2, :], 0.0, FAR,
                                 ALU.is_equal, ALU.mult).then_inc(S("list_steps"), 1)
                ve.wait_ge(S("list_steps"), r * 2 + 1)
                for a, dst in enumerate((gall, sall)):
                    ve.scalar_tensor_tensor(out=dst[:, :], in0=l3[:, a, :], scalar=-1.0, in1=lst[:, a * NE:(a + 1) * NE],
                                            op0=ALU.add, op1=ALU.add)
                ve.tensor_scalar(posm, posm, float(-SLOTS), None, ALU.add).then_inc(S("list_steps"), 1)
                ve.wait_ge(S("list_steps"), r * 2 + 2)
                ve.tensor_copy(gates, l3[:, 2, :]).then_inc(S("lists_ready"), 1)
                ve.wait_ge(S("lists_ready"), r + 1)

            def x_copy(r, e, s):
                ve.wait_ge(S("x_T"), (r * NE + e) * 2 + 2)
                need(ve, "gate_up_done", r * NE + e - 1)
                ve.tensor_copy(XgT[s][:, 512:1024], ps[1][:, :]).then_inc(S("x_copied1"), 1)

            def silu(r, e, s):
                G = r * NE + e
                ve.wait_ge(S("gate_exp"), G + 1)
                ve.tensor_scalar(rcb, exb, 1.0, None, ALU.add).then_inc(S("silu_steps"), 1)
                ve.wait_ge(S("silu_steps"), G * 3 + 1)
                ve.reciprocal(rcb, rcb).then_inc(S("silu_steps"), 1)
                ve.wait_ge(S("silu_steps"), G * 3 + 2)
                tt(hmb, ps[2 + s][:, 0:FE], rcb, ALU.mult).then_inc(S("silu_steps"), 1)
                ve.wait_ge(S("silu_steps"), G * 3 + 3)
                need(ve, "h_T", G)
                col = bass.ds(e, 1)
                ve.scalar_tensor_tensor(out=hS, in0=hmb, scalar=gates[:, col], in1=ps[2 + s][:, FE:2 * FE], op0=ALU.mult,
                                        op1=ALU.mult).then_inc(S("act_ready"), 1)

            def h_copy(r, e, s):
                G = r * NE + e
                ve.wait_ge(S("h_T"), G + 1)
                need(ve, "down_done", G * 2)
                ve.tensor_copy(hTb, ps[4][:, 0:256]).then_inc(S("h_copied"), 1)

            def y_copy(r, e, eh, s):
                ve.wait_ge(S("down_done"), (r * NE + e) * 2 + 2)
                value = (r * (NE // 2) + eh) * 16
                need(ve, f"scattered{s}", value)
                ve.tensor_copy(Yo[s][:, 512:1024], ps[6][:, :]).then_inc(S("y_copied1"), 1)

            def round_(r):
                lists(r)
                x_copy(r, 0, 0)
                silu(r, 0, 0)
                x_copy(r, 1, 1)
                h_copy(r, 0, 0)
                def two_experts(i):
                    silu(r, i * 2 + 1, 1)
                    x_copy(r, i * 2 + 2, 0)
                    y_copy(r, i * 2, i, 0)
                    h_copy(r, i * 2 + 1, 1)
                    silu(r, i * 2 + 2, 0)
                    x_copy(r, i * 2 + 3, 1)
                    y_copy(r, i * 2 + 1, i, 1)
                    h_copy(r, i * 2 + 2, 0)

                pairs_from(ve, (NE - 2) // 2, two_experts)
                e = NE - 1
                silu(r, e, 1)
                y_copy(r, e - 1, (e - 1) // 2, 0)
                h_copy(r, e, 1)
                y_copy(r, e, e // 2, 1)

            round_(0)
            more_rounds(ve, round_)
            for i in range(TT):
                n = P if i < 2 else NS
                ve.wait_ge(S(f"rows{i}_back"), 32)
                h = x[0:n, i * D:(i + 1) * D]
                st.link(tt(h, h, R[0:n, i * D:(i + 1) * D], ALU.add))
                tt(h, h, R[0:n, 3072 + i * D:3072 + (i + 1) * D], ALU.add).then_inc(S("y_ready"), 1)

        block = ctx.enter_context(nc.Block())

        def v3(ap, a):
            return ap.rearrange("p (a b) -> p a b", a=a)

        @block.sync
        def _(sp):
            sp.dma_start(x[:, 0:D], I["x_prompt"][0, 0:P, :]).then_inc(S("x0_loaded"), 16)
            sp.dma_start(x[:, D:2 * D], I["x_prompt"][0, P:2 * P, :]).then_inc(S("x1_loaded"), 16)
            sp.dma_start(x[0:NS, 2 * D:3 * D], I["x_sample"].rearrange("b t d -> (b t) d")).then_inc(S("x2_loaded"), 16)
            sp.dma_start(cst[:, :], I["shape_constants"][:, 0:LASTING]).then_inc(S("constants_loaded"), 16)
            sp.dma_start(cst_early, I["shape_constants"][:, LASTING:]).then_inc(S("constants_loaded"), 16)
            with nc.allow_non_contiguous_dma(reason="small tables"):
                sp.dma_start(ldt[0:LT, :], I["ssm_log_dt"].rearrange("o (i e) -> (o i) e", e=2)).then_inc(S("log_dt_loaded"), 16)
                sp.dma_start(pgt[0:UP, :], I["page_table"].rearrange("b (h g) -> g (b h)", g=UP)).then_inc(S("pages_loaded"), 16)
            for name in ("norm1_g", "ssm_d", "ssm_b_glu", "q_norm_g", "out_norm_ssm", "out_norm_attn"):
                a, b = ROW[name]
                sp.dma_start(vrow[a:b, :], I[name].rearrange("o (r p) -> (o r) p", p=P)).then_inc(S("rows_loaded"), 16)
            for name in ("ssm_a_re", "ssm_a_im"):
                a, b = ROW[name]
                sp.dma_start(vrow[a:b, :], I[name].rearrange("o (i e) p -> (o i) (e p)", e=2)).then_inc(S("rows_loaded"), 16)
            for a, name in enumerate(("state_ssm_re", "state_ssm_im")):
                sp.dma_start(sraw[:, a * P:(a + 1) * P],
                             I[name].rearrange("o b (i e) p -> (o b i) (e p)", e=2)).then_inc(S("rows_loaded"), 16)
            for k0 in (0, 4):
                sp.dma_start(w_in[:, k0:k0 + 4, :],
                             I["w_in"][0, k0 * P:(k0 + 4) * P, :].rearrange("(k p) n -> p k n", p=P)).then_inc(S("w_in_loaded"), 16)
            with nc.allow_non_contiguous_dma(reason="64-byte rows of the input matrices"):
                for a, name in enumerate(("ssm_b_re", "ssm_b_im")):
                    sp.dma_start(braw[:, a], I[name].rearrange("o (i e) p c -> (o e p) i c", e=2)).then_inc(S("b_loaded"), 16)
                for a, name in enumerate(("ssm_c_re", "ssm_c_im")):
                    for e in range(2):
                        sp.dma_start(craw[:, a, :, e, :],
                                     I[name].rearrange("o (m g) c p -> (o g c) m p", m=4)).then_inc(S("c_loaded"), 16)
            sp.dma_start(g_row[:, 0:KR], I["kv_norm_g"].to_broadcast([P, KR])).then_inc(S("gains_loaded"), 16)
            sp.dma_start(g_row[:, KR:KR + QK], I["qk_norm_q"].to_broadcast([P, QK])).then_inc(S("gains_loaded"), 16)
            sp.dma_start(g_row[:, KR + QK:], I["qk_norm_k"].to_broadcast([P, QK])).then_inc(S("gains_loaded"), 16)
            sp.dma_start(w_uq[:, :, :], I["w_uq"][0].rearrange("(k p) h d -> p k (h d)", p=P)).then_inc(S("w_uq_loaded"), 16)
            sp.dma_start(w_uk[:, :], I["w_uk"][0].rearrange("r h d -> r (h d)")).then_inc(S("w_kv_loaded"), 16)
            sp.dma_start(w_uv[:, :], I["w_uv"][0].rearrange("r h d -> r (h d)")).then_inc(S("w_kv_loaded"), 16)
            sp.wait_ge(S("latents_ready"), 2)
            for i in range(2):
                sp.dma_start(O["ckv_p"][0, i], ckvn[:, i * KR:(i + 1) * KR]).then_inc(S("outputs_stored"), 16)
                sp.dma_start(O["kr_p"][0, i], krn[:, i * ROPE:(i + 1) * ROPE]).then_inc(S("outputs_stored"), 16)
            sp.dma_start(O["ckv_s"].rearrange("o b t r -> (o b t) r"), ckvn[0:NS, 2 * KR:]).then_inc(S("outputs_stored"), 16)
            sp.dma_start(O["kr_s"].rearrange("o b t r -> (o b t) r"), krn[0:NS, 2 * ROPE:]).then_inc(S("outputs_stored"), 16)
            used(sp, "qT7")
            used(sp, "kT7")
            used(sp, "qr")
            sp.dma_start(w_out, I["w_out"][0].rearrange("(k p) n -> p k n", p=P)).then_inc(S("w_out_loaded"), 16)
            post_sync(sp)

        @block.gpsimd
        def _(pool):
            pool.memset(x[64:P, 2 * D:3 * D], 0.0).then_inc(S("pads_set"), 1)
            pool.wait_ge(S("pads_set"), 1)
            pool.memset(R[:, 11520:12544], 0.0).then_inc(S("pads_set"), 1)
            for i in range(2):
                pool.wait_ge(S("pads_set"), 2 + i)
                pool.memset(Ssb[i][64:P, 1024:1088], NEG).then_inc(S("pads_set"), 1)
            pool.wait_ge(S("pads_set"), 4)
            pool.memset(soft[:, NS:P], 0.0).then_inc(S("pads_set"), 1)
            used(pool, "vec")
            pool.wait_ge(S("pads_set"), 5)
            pool.memset(vrow[NS:P, :], 0.0).then_inc(S("pads_set"), 1)
            pool.wait_ge(S("pads_set"), 6)
            pool.wait_ge(S("page_rows_ready"), 1)
            for u in range(4):
                gather_unit(pool, u, 0)
            pool_loop(pool)

        @block.tensor
        def _(pe):
            pe.wait_ge(S("constants_loaded"), 32)
            pe.wait_ge(S("rows_loaded"), 16 * 10)
            pe.wait_ge(S("log_dt_spread"), 1)
            b = fill(pe, "vec")
            pe.transpose(b[:, 0:NROW], vrow[0:NROW, :], ident[0:NROW, 0:NROW])
            pe.transpose(b[:, 128:256], sraw[:, 0:P], ident)
            filled(pe.transpose(b[:, 256:384], sraw[:, P:2 * P], ident), "vec")
            for i in range(TT):
                pe.wait_ge(S("xn_ready"), i + 1)
                for g in range(2):
                    b = fill(pe, f"xT{2 * i + g}")
                    for k in range(4):
                        c = i * D + (4 * g + k) * P
                        ins = pe.transpose(b[:, k * P:(k + 1) * P], xn[:, c:c + P], ident)
                    filled(ins, f"xT{2 * i + g}")
            pe.wait_ge(S("page_table_ready"), 1)
            b = fill(pe, "page")
            filled(pe.matmul(b[:, 0:16], C("pgsel", UP), pgf[0:UP, 0:16], start=True, stop=True), "page")
            pe.wait_ge(S("c_loaded"), 64)

            def c_transposes(a):
                b = fill(pe, f"ct{a}")
                for m in range(4):
                    ins = pe.transpose(b[:, m * P:(m + 1) * P], craw[:, a, m].rearrange("p e s -> p (e s)"), ident)
                filled(ins, f"ct{a}")

            c_transposes(0)
            pe.wait_ge(S("w_in_loaded"), 32)
            for i in range(6):
                used(pe, f"xT{i}")
            for m in range(4):
                b = fill(pe, f"u{m}")
                for k in range(KD):
                    ins = pe.matmul(b[:, 0:T], w_in[:, k, m * P:(m + 1) * P], nT[:, k, 0:T],
                                    start=(k == 0), stop=(k == KD - 1))
                filled(ins, f"u{m}")
            for i in range(TT):
                b = fill(pe, f"z{i}")
                for k in range(KD):
                    ins = pe.matmul(b[:, 0:ZW], nT[:, k, i * P:(i + 1) * P], w_in[:, k, SSM_W:DIN],
                                    start=(k == 0), stop=(k == KD - 1))
                filled(ins, f"z{i}")
            c_transposes(1)
            pe.wait_ge(S("b_spread"), 4)
            for a in range(2):
                b = fill(pe, f"bd{a}")
                for m in range(4):
                    ins = pe.transpose(b[:, m * P:(m + 1) * P],
                                       xst[:, a, 4 * m:4 * m + 4].rearrange("p i e c -> p (i e c)"), ident)
                filled(ins, f"bd{a}")
            pe.wait_ge(S("cq_ready"), 3)
            for k in range(2):
                b = fill(pe, f"cq{k}")
                for i in range(TT):
                    ins = pe.transpose(b[:, i * P:(i + 1) * P], cqn[:, i, k * P:(k + 1) * P], ident)
                filled(ins, f"cq{k}")
            pe.wait_ge(S("latents_ready"), 2)
            b = fill(pe, "ckvT")
            for i in range(TT):
                ins = pe.transpose(b[:, i * P:(i + 1) * P], ckvn[:, i * KR:(i + 1) * KR], ident)
            filled(ins, "ckvT")
            used(pe, "cq0")
            used(pe, "cq1")
            pe.wait_ge(S("w_uq_loaded"), 16)
            for i in range(TT):
                for g, (lo, hi) in enumerate(((0, 512), (512, 768))):
                    b = fill(pe, f"q{i}{g}")
                    for k in range(2):
                        ins = pe.matmul(b[:, 0:hi - lo], cqT[:, k, i * P:(i + 1) * P], w_uq[:, k, lo:hi],
                                        start=(k == 0), stop=(k == 1))
                    filled(ins, f"q{i}{g}")
            pe.wait_ge(S("w_kv_loaded"), 32)
            used(pe, "ckvT")
            for i in range(TT):
                b = fill(pe, f"k{i}")
                filled(pe.matmul(b[:, :], ckvT[:, i * P:(i + 1) * P], w_uk[:, :], start=True, stop=True), f"k{i}")
            for i in range(2):
                b = fill(pe, f"v{i}")
                filled(pe.matmul(b[:, :], ckvT[:, i * P:(i + 1) * P], w_uv[:, :], start=True, stop=True), f"v{i}")
            used(pe, "bd0")
            used(pe, "bd1")
            used(pe, "u3")
            for i in range(LT):
                m, j = i // 4, 32 * (i % 4)
                for a, bd in enumerate((bdr, bdi)):
                    name = f"bu{2 * i + a}"
                    b = fill(pe, name)
                    filled(pe.matmul(b[:, 0:T], bd[j:j + 32, m * P:(m + 1) * P], uT[j:j + 32, m * T:(m + 1) * T],
                                     start=True, stop=True), name)
            for what, src, ready in (("qT", q, "q_ready"), ("kT", kk, "k_ready")):
                pe.wait_ge(S(ready), 1)
                for h in range(H):
                    b = fill(pe, f"{what}{h}")
                    for i in range(TT):
                        ins = pe.transpose(b[0:QK, i * P:(i + 1) * P], src[:, i, h, :], ident)
                    filled(ins, f"{what}{h}")
            for g in range(2):
                b = fill(pe, f"uk{g}")
                for h in range(4):
                    c = (4 * g + h) * NOPE
                    ins = pe.transpose(b[0:NOPE, h * P:(h + 1) * P], w_uk[:, c:c + NOPE], ident)
                filled(ins, f"uk{g}")
            b = fill(pe, "qr")
            pe.wait_ge(S("q_rope_spread"), 1)
            for h in range(H):
                ins = pe.transpose(b[:, h * NS:(h + 1) * NS], qr4[0:NS, h].rearrange("p e d -> p (e d)"), ident[0:NS, 0:NS])
            filled(ins, "qr")
            used(pe, "uk1")
            used(pe, "uk0")
            for h in range(H):
                used(pe, f"qT{h}")
                used(pe, f"kT{h}")
            b = fill(pe, "qa")
            for h in range(H):
                ins = pe.matmul(b[:, h * NS:(h + 1) * NS], w_ukT[0:NOPE, h, :], qT[0:NOPE, h, SEQ:T], start=True, stop=True)
            filled(ins, "qa")
            b = fill(pe, "sn")
            for h in range(H):
                ins = pe.matmul(b[0:NS, h * NS:(h + 1) * NS], kT[0:QK, h, SEQ:T], qT[0:QK, h, SEQ:T], start=True, stop=True)
            filled(ins, "sn")
            for i in range(8):
                pe.wait_ge(S(f"free{i}"), pre_uses[i])
            pe_loop(pe)

        @block.scalar
        def _(act):
            st = chain(act, "act_steps")

            def rsqrt(ap, scale=1.0):
                st.link(act.activation(ap, ap, ACT.Ln, bias=EPS, scale=scale))
                return act.activation(ap, ap, ACT.Exp, scale=-0.5)

            act.wait_ge(S("pads_set"), 1)
            for i in range(TT):
                act.wait_ge(S(f"x{i}_loaded"), 16)
                st.link(act.activation(junk, x[:, i * D:(i + 1) * D], ACT.Square, scale=1 / 32, accum_out=ms1[:, i:i + 1]))
                rsqrt(ms1[:, i:i + 1]).then_inc(S("rs1_ready"), 1)
            used(act, "vec")
            act.activation(p_dt, vcol("log_dt"), ACT.Exp).then_inc(S("pole_exps_ready"), 1)
            act.wait_ge(S("angles_ready"), 1)
            act.activation(p_mag, p_b, ACT.Exp).then_inc(S("pole_exps_ready"), 1)
            st.link(act.activation(p_ab, p_f, ACT.Abs))
            act.activation(p_sin, p_f, ACT.Sin, scale=TWO_PI).then_inc(S("trig0_ready"), 1)
            act.activation(p_cos, p_ab, ACT.Sin, scale=-TWO_PI, bias=math.pi / 2).then_inc(S("trig0_ready"), 1)
            for m in range(4):
                b = read(act, f"u{m}")
                was_read(act.activation(uT[:, m * T:(m + 1) * T], b[:, 0:T], ACT.Copy), f"u{m}")
            for i in range(TT):
                b = read(act, f"z{i}")
                was_read(act.activation(z[:, i, :], b[:, 0:ZW], ACT.Copy), f"z{i}")
                used(act, f"z{i}")
                st.inc(act.activation(junk[:, 0:QR], z[:, i, 0:QR], ACT.Square, scale=1 / 16, accum_out=ms2[:, i:i + 1]))
                st.inc(act.activation(junk[:, QR:QR + KR], z[:, i, QR:QR + KR], ACT.Square, scale=KR ** -0.5,
                                      accum_out=ms2[:, 3 + i:4 + i]))
                st.sync()
            rsqrt(ms2).then_inc(S("rs_latent_ready"), 1)
            for i in range(TT):
                for g, (lo, hi) in enumerate(((0, 512), (512, 768))):
                    b = read(act, f"q{i}{g}")
                    o = O1[:, i * 768 + lo:i * 768 + hi]
                    was_read(act.activation(o, b[:, 0:hi - lo], ACT.Copy), f"q{i}{g}")
            for i in range(TT):
                b = read(act, f"k{i}")
                was_read(act.activation(kk[:, i, :, 0:NOPE], v3(b[:, :], H), ACT.Copy), f"k{i}")
            for i in range(2):
                b = read(act, f"v{i}")
                was_read(act.activation(v[:, i * 512:(i + 1) * 512], b[:, :], ACT.Copy), f"v{i}")
            act.wait_ge(S("q_rotated"), 1)
            act.activation(QT[:, 0:2304], O1[:, 0:2304], ACT.Square, scale=QK ** -0.5).then_inc(S("qk_squared"), 1)
            act.wait_ge(S("k_filled"), 1)
            for i in range(TT):
                used(act, f"k{i}")
            act.activation(KT[:, 0:2304], O1[:, 2304:4608], ACT.Square, scale=QK ** -0.5).then_inc(S("qk_squared"), 1)
            act.wait_ge(S("qk_sums_ready"), 1)
            rsqrt(msq).then_inc(S("rs_qk_ready"), 1)
            act.wait_ge(S("qk_sums_ready"), 2)
            rsqrt(msk).then_inc(S("rs_qk_ready"), 1)
            for i in range(LT):
                for a, dst in enumerate((bre, bim)):
                    b = read(act, f"bu{2 * i + a}")
                    was_read(act.activation(dst[:, i * T:(i + 1) * T], b[:, 0:T], ACT.Copy), f"bu{2 * i + a}")
            for h in range(H):
                b = read(act, f"kT{h}")
                was_read(act.activation(kT[0:QK, h, :], b[0:QK, 0:T], ACT.Copy), f"kT{h}")
            act_loop(act)

        @block.vector
        def _(ve):
            st = chain(ve, "dve_steps")
            ve.wait_ge(S("log_dt_loaded"), 16)
            ve.tensor_copy(v3(vrow[0:LT, :], 2), bc(ldt[0:LT, :], 2, SP)).then_inc(S("log_dt_spread"), 1)
            ve.wait_ge(S("pages_loaded"), 16)
            ve.tensor_copy(pgf[0:UP, 0:16], pgt[0:UP, :]).then_inc(S("page_table_ready"), 1)
            for i in range(TT):
                ve.wait_ge(S("rs1_ready"), i + 1)
                ve.tensor_scalar(xn[:, i * D:(i + 1) * D], x[:, i * D:(i + 1) * D], ms1[:, i:i + 1], None,
                                 ALU.mult).then_inc(S("xn_ready"), 1)
            b = read(ve, "vec")
            st.inc(ve.tensor_copy(st0[:, :], b[:, 128:384]))
            was_read(ve.tensor_copy(vec[:, :], b[:, 0:NROW]), "vec")
            used(ve, "vec")
            for i in range(6):
                b = read(ve, f"xT{i}")
                k0, t0 = 4 * (i % 2), (i // 2) * P
                was_read(ve.tensor_tensor(nT[:, k0:k0 + 4, t0:t0 + P], v3(b[:, :], 4),
                                          bc(vcol("norm1_g")[:, k0:k0 + 4], 2, P), ALU.mult), f"xT{i}")
            b = read(ve, "page")
            was_read(ve.tensor_scalar(page_all[:, :], b[:, 0:16], float(PAGE // RUN), C("pgrow"), ALU.mult, ALU.add), "page")
            used(ve, "page")
            ve.tensor_copy(page_idx[:, :], page_all[:, 0:4]).then_inc(S("page_rows_ready"), 1)
            ar, ai = vcol("ssm_a_re"), vcol("ssm_a_im")
            c1 = 6.28125
            ve.wait_ge(S("pole_exps_ready"), 1)
            st.inc(ve.tensor_tensor(p_ang, ai, p_dt, ALU.mult))
            st.link(ve.tensor_tensor(p_b, ar, p_dt, ALU.mult))
            st.link(ve.tensor_scalar(p_k, p_ang, 1 / (2 * math.pi), MAGIC, ALU.mult, ALU.add))
            st.link(ve.tensor_scalar(p_k, p_k, MAGIC, None, ALU.subtract))
            st.link(ve.scalar_tensor_tensor(out=p_th, in0=p_k, scalar=-c1, in1=p_ang, op0=ALU.mult, op1=ALU.add))
            st.link(ve.scalar_tensor_tensor(out=p_th, in0=p_k, scalar=-(2 * math.pi - c1), in1=p_th, op0=ALU.mult, op1=ALU.add))
            st.link(ve.tensor_scalar(p_f, p_th, 1 / (2 * math.pi), 0.5, ALU.mult, ALU.min))
            ve.tensor_scalar(p_f, p_f, -0.5, None, ALU.max).then_inc(S("angles_ready"), 1)
            ve.wait_ge(S("pole_exps_ready"), 2)
            ve.wait_ge(S("trig0_ready"), 2)
            ve.wait_ge(S("b_loaded"), 32)
            ve.wait_ge(S("pads_set"), 4)
            st.inc(ve.tensor_tensor(p_lr, p_mag, p_cos, ALU.mult))
            st.inc(ve.tensor_tensor(p_li, p_mag, p_sin, ALU.mult))
            st.inc(ve.tensor_tensor(p_a, ar, ar, ALU.mult))
            st.inc(ve.tensor_tensor(p_den, ai, ai, ALU.mult))
            st.sync()
            st.inc(ve.tensor_scalar(p_lr, p_lr, -1.0, None, ALU.add))
            st.link(ve.tensor_tensor(p_den, p_den, p_a, ALU.add))
            st.inc(ve.reciprocal(p_den, p_den))
            st.inc(ve.tensor_tensor(p_a, p_lr, ar, ALU.mult))
            st.inc(ve.tensor_tensor(p_b, p_li, ai, ALU.mult))
            st.inc(ve.tensor_tensor(p_k, p_li, ar, ALU.mult))
            st.inc(ve.tensor_tensor(p_th, p_lr, ai, ALU.mult))
            st.sync()
            st.inc(ve.tensor_tensor(p_cr, p_a, p_b, ALU.add))
            st.inc(ve.tensor_tensor(p_ci, p_k, p_th, ALU.subtract))
            st.sync()
            st.inc(ve.tensor_tensor(p_cr, p_cr, p_den, ALU.mult))
            st.inc(ve.tensor_tensor(p_ci, p_ci, p_den, ALU.mult))
            st.sync()
            t = [v3(rt[i][:, 0:256], LT) for i in range(4)]
            crb, cib = bc(p_cr, 2, CH), bc(p_ci, 2, CH)
            ve.wait_ge(S("rs1_ready"), 3)
            st.inc(ve.tensor_tensor(t[0], crb, braw[:, 0], ALU.mult))
            st.inc(ve.tensor_tensor(t[1], cib, braw[:, 1], ALU.mult))
            st.inc(ve.tensor_tensor(t[2], crb, braw[:, 1], ALU.mult))
            st.inc(ve.tensor_tensor(t[3], cib, braw[:, 0], ALU.mult))
            st.sync()
            for e in range(2):
                r = slice(64 * e, 64 * e + 64)
                ve.tensor_tensor(xst[r, 0, :, e, :], t[0][r], t[1][r], ALU.subtract).then_inc(S("b_spread"), 1)
                ve.tensor_tensor(xst[r, 1, :, e, :], t[2][r], t[3][r], ALU.add).then_inc(S("b_spread"), 1)
            for a in range(2):
                s = v3(st0[:, a * P:(a + 1) * P], NB)
                st.inc(ve.tensor_tensor(s, s, bc(p_mag, 1, NB), ALU.mult))
            b = read(ve, "ct0")
            was_read(ve.tensor_tensor(v3(CT[:, 0:512], 4), v3(b[:, :], 4), bc(C("even"), 1, 4), ALU.mult), "ct0")
            b = read(ve, "ct1")
            was_read(ve.scalar_tensor_tensor(out=v3(CT[:, 512:1024], 4), in0=v3(b[:, :], 4), scalar=-1.0,
                                             in1=bc(C("even"), 1, 4), op0=ALU.mult, op1=ALU.mult), "ct1")
            ve.wait_ge(S("rs_latent_ready"), 1)
            ve.wait_ge(S("gains_loaded"), 48)
            for i in range(TT):
                ve.tensor_scalar(cqn[:, i, :], z[:, i, 0:QR], ms2[:, i:i + 1], None, ALU.mult).then_inc(S("cq_ready"), 1)
            for i in range(TT):
                ins = ve.scalar_tensor_tensor(out=ckvn[:, i * KR:(i + 1) * KR], in0=z[:, i, QR:QR + KR],
                                              scalar=ms2[:, 3 + i:4 + i], in1=g_row[:, 0:KR], op0=ALU.mult, op1=ALU.mult)
                if i < 2:
                    st.inc(ins)
            ins.then_inc(S("latents_ready"), 1)
            cos3, sin3 = v3(C("cos"), TT), v3(C("sin"), TT)

            def rotate(x1, x2, cos, sin, t, out1, out2, sem):
                st.inc(ve.tensor_tensor(t[0], x1, cos, ALU.mult))
                st.inc(ve.tensor_tensor(t[1], x2, sin, ALU.mult))
                st.inc(ve.tensor_tensor(t[2], x1, sin, ALU.mult))
                st.inc(ve.tensor_tensor(t[3], x2, cos, ALU.mult))
                st.sync()
                st.inc(ve.tensor_tensor(out1, t[0], t[1], ALU.subtract))
                ve.tensor_tensor(out2, t[2], t[3], ALU.add).then_inc(sem, 1)

            kr3 = v3(krn[:, :], TT)
            zr = z[:, :, QR + KR:ZW]
            ve.wait_ge(S("b_spread"), 4)
            rotate(zr[:, :, 0:HR], zr[:, :, HR:ROPE], cos3, sin3, [v3(r[:, 0:TT * HR], TT) for r in rt],
                   kr3[:, :, 0:HR], kr3[:, :, HR:], S("latents_ready"))
            st.link(ve.scalar_tensor_tensor(out=g_row[:, KR:KR + QK], in0=g_row[:, KR:KR + QK], scalar=QK ** -0.5,
                                            in1=g_row[:, KR + QK:], op0=ALU.mult, op1=ALU.mult))
            for a, dst in ((0, bdr), (1, bdi)):
                b = read(ve, f"bd{a}")
                was_read(ve.tensor_copy(dst, b[:, :]), f"bd{a}")
            for k in range(2):
                b = read(ve, f"cq{k}")
                was_read(ve.tensor_scalar(cqT[:, k, :], b[:, 0:TP], vcol("q_norm_g")[:, k:k + 1], None, ALU.mult), f"cq{k}")
            b = read(ve, "ckvT")
            was_read(ve.tensor_copy(ckvT[:, :], b[:, 0:TP]), "ckvT")
            for i in range(TT):
                used(ve, f"q{i}1")
            ve.wait_ge(S("latents_ready"), 2)
            t = [r.rearrange("p (i h d) -> p i h d", i=TT, h=H) for r in rt]
            rotate(q[:, :, :, NOPE:NOPE + HR], q[:, :, :, NOPE + HR:], bc(cos3, 2, H), bc(sin3, 2, H), t,
                   q[:, :, :, NOPE:NOPE + HR], q[:, :, :, NOPE + HR:], S("q_rotated"))
            ve.tensor_copy(kk[:, :, :, NOPE:], bc(kr3, 2, H)).then_inc(S("k_filled"), 1)
            ve.wait_ge(S("qk_squared"), 1)
            ve.tensor_reduce(msq, v3(QT[:, 0:2304], 24), AX, ALU.add).then_inc(S("qk_sums_ready"), 1)
            ve.wait_ge(S("qk_squared"), 2)
            ve.tensor_reduce(msk, v3(KT[:, 0:2304], 24), AX, ALU.add).then_inc(S("qk_sums_ready"), 1)
            ve.wait_ge(S("rs_qk_ready"), 1)
            qf, kf = v3(O1[:, 0:2304], 24), v3(O1[:, 2304:4608], 24)
            st.link(ve.tensor_tensor(qf, qf, bc(msq, 2, QK), ALU.mult))
            ve.tensor_tensor(qf, qf, bc(g_row[:, KR:KR + QK], 1, 24), ALU.mult).then_inc(S("q_ready"), 1)
            ve.wait_ge(S("rs_qk_ready"), 2)
            ve.tensor_tensor(kf, kf, bc(msk, 2, QK), ALU.mult).then_inc(S("k_ready"), 1)
            ve.wait_ge(S("q_ready"), 1)
            ve.tensor_copy(qr4[0:NS], bc(q[0:NS, 2, :, NOPE:], 2, 4)).then_inc(S("q_rope_spread"), 1)
            for h in range(H):
                b = read(ve, f"qT{h}")
                was_read(ve.tensor_copy(qT[0:QK, h, :], b[0:QK, 0:T]), f"qT{h}")
            for g in range(2):
                b = read(ve, f"uk{g}")
                was_read(ve.tensor_copy(w_ukT[0:NOPE, 4 * g:4 * g + 4, :], v3(b[0:NOPE, :], 4)), f"uk{g}")
            for name, dst, rows in (("qr", qrp, P), ("qa", qa, P), ("sn", s_new, NS)):
                b = read(ve, name)
                o = dst[0:rows, :].rearrange("p (b h t) -> p h b t", b=NB, h=H)
                was_read(ve.tensor_copy(o, b[0:rows, :].rearrange("p (h b t) -> p h b t", h=H, b=NB)), name)
            ve_loop(ve)


_INS = ["x_prompt", "x_sample", "cache_ckv", "cache_krope", "state_ssm_re", "state_ssm_im", "page_table", "norm1_g",
        "w_in", "ssm_a_re", "ssm_a_im", "ssm_log_dt", "ssm_b_re", "ssm_b_im", "ssm_c_re", "ssm_c_im", "ssm_d",
        "ssm_w_glu", "ssm_b_glu", "q_norm_g", "w_uq", "kv_norm_g", "w_uk", "w_uv", "qk_norm_q", "qk_norm_k",
        "out_norm_ssm", "out_norm_attn", "w_out", "norm2_g", "w_router_group", "b_router_group", "w_router_expert",
        "b_router_expert", "w_gate", "w_up", "w_down"]
_OUTS = [("y_p", (1, SEQ, D)), ("y_s", (NB, NQ, D)), ("ckv_p", (1, 1, SEQ // PAGE, PAGE, KR)),
         ("kr_p", (1, 1, SEQ // PAGE, PAGE, ROPE)), ("re_p", (1, 1, GROUPS, SP)), ("im_p", (1, 1, GROUPS, SP)),
         ("ckv_s", (1, NB, NQ, KR)), ("kr_s", (1, NB, NQ, ROPE)), ("re_s", (1, NB, GROUPS, SP)), ("im_s", (1, NB, GROUPS, SP))]


def program_outputs(O):
    views = dict(O)
    for name in ("ckv_p", "kr_p"):
        views[name] = O[name][0]
    for name in ("re_p", "im_p"):
        views[name] = O[name][0]
    return views


def kernel(**inputs):
    import numpy as _np
    import concourse.bacc as _bacc
    from concourse import mybir as _mybir
    from concourse.bass_utils import run_bass_kernel_spmd as _run

    nc = _bacc.Bacc("TRN2", target_bir_lowering=False, num_devices=1)
    arrays, I, O = {}, {}, {}
    for name in _INS:
        a = _np.ascontiguousarray(inputs[name])
        arrays[f"in_{name}"] = a
        I[name] = nc.dram_tensor(f"in_{name}", a.shape, _mybir.dt.from_np(a.dtype), kind="ExternalInput").ap()
    a = shape_constants()
    arrays["in_shape_constants"] = a
    I["shape_constants"] = nc.dram_tensor("in_shape_constants", a.shape, _mybir.dt.from_np(a.dtype), kind="ExternalInput").ap()
    for name, shape in _OUTS:
        O[name] = nc.dram_tensor(f"out_{name}", shape, F32, kind="ExternalOutput").ap()
    build_program(nc, I, program_outputs(O))
    r = _run(nc, [arrays], core_ids=[0])
    return tuple(r.results[0][f"out_{name}"] for name, _ in _OUTS)
```

```python
import math
from contextlib import ExitStack

import numpy as np

import concourse.bass as bass
from concourse import mybir

ALU = mybir.AluOpType
ACT = mybir.ActivationFunctionType
AX = mybir.AxisListType.X
F32 = mybir.dt.float32
U32 = mybir.dt.uint32
I32 = mybir.dt.int32

P = 128
D = 1024
SEQ = 256
NB, NQ = 8, 8
NS = NB * NQ
T = SEQ + NS
TT = 3
TP = TT * P
KD = D // P
SSM_W, CH, GROUPS, SP = 512, 16, 32, 64
LT = GROUPS * SP // P
H, VD, NOPE, ROPE = 8, 64, 64, 32
HR = ROPE // 2
QK = NOPE + ROPE
QR, KR = 256, 128
ZW = QR + KR + ROPE
DIN = SSM_W + ZW
PAGE, NPG, POOL = 128, 16, 160
UP = 8
RUN = 8
NG, EG, NE, FE = 4, 8, 32, 256
EPS = 1e-6
NEG = -1e30
MAGIC = 1.5 * 2.0 ** 23
TWO_PI = 6.283185
SLOTS = 64
HD = D // 2
LN_EXP = "natural_log_exp_and_others"
ROUNDS = -(-T // SLOTS)
FAR = 65536.0

_COLS = [("ident", P), ("tri", P), ("ones", P), ("causal", 3 * P), ("smask", NS), ("ramp", NE),
         ("step", T), ("carry", T), ("tok", TT), ("valid", TT), ("beyond", TT), ("half", 1), ("early8", 64), ("early4", 16), ("quad", 4),
         ("cos", TT * HR), ("sin", TT * HR), ("pgsel", P), ("pgrow", 1), ("even", P)]
COL = {}
_at = 0
for _n, _w in _COLS:
    COL[_n] = (_at, _w)
    _at += _w
NCONST = _at
LASTING = COL["cos"][0]


def shape_constants():
    c = np.zeros((P, NCONST), np.float32)

    def col(name):
        a, w = COL[name]
        return c[:, a:a + w]

    p = np.arange(P)
    col("ident")[:] = np.eye(P)
    col("tri")[:] = p[:, None] < p[None, :]
    col("ones")[:] = 1.0
    col("causal")[:, 0:P] = col("causal")[:, 2 * P:] = np.where(p[None, :] <= p[:, None], 0.0, NEG)
    key_b, key_t = p // NQ, p % NQ
    for b in range(NB):
        for q in range(NQ):
            col("smask")[:, b * NQ + q] = np.where((key_b == b) & (key_t <= q), 0.0, NEG)
    col("ramp")[:] = np.arange(NE)[None, :]
    step = np.concatenate([np.arange(1, SEQ + 1), np.tile(np.arange(1, NQ + 1), NB)])
    col("step")[:] = step[None, :]
    col("carry")[:] = (step != 1)[None, :]
    inv = (np.float32(10000.0) ** (-np.arange(0, ROPE, 2, dtype=np.float32) / np.float32(ROPE))).astype(np.float32)
    pos = np.zeros((TT, P), np.float32)
    pos[0], pos[1] = np.arange(P), np.arange(P, 2 * P)
    pos[2, :NS] = NPG * PAGE + np.arange(NS) % NQ
    ang = (pos[:, :, None] * inv[None, None, :]).astype(np.float32).transpose(1, 0, 2).reshape(P, -1)
    col("cos")[:], col("sin")[:] = np.cos(ang), np.sin(ang)
    col("pgsel")[:UP] = (p[None, :] // (P // UP)) == np.arange(UP)[:, None]
    col("pgrow")[:, 0] = p % (PAGE // RUN)
    col("tok")[:] = p[:, None] + P * np.arange(TT)[None, :]
    col("valid")[:] = col("tok") < T
    col("beyond")[:] = np.where(col("tok") < T, 0.0, FAR)
    col("half")[:, 0] = p // SLOTS
    e = np.arange(8)
    col("early8")[:] = (e[None, :] < e[:, None]).reshape(1, 64)
    col("early4")[:] = (e[None, :4] < e[:4, None]).reshape(1, 16)
    col("even")[:] = (p[:, None] // SP) == ((p[None, :] // CH) % 2)
    col("quad")[:] = (p[:, None] // 32) == np.arange(4)[None, :]
    return c


def empty_lists():
    return np.full((ROUNDS * SLOTS * NE, 4), FAR, np.float32)


_ROWS = [("log_dt", 16), ("norm1_g", 8), ("ssm_d", 4), ("ssm_b_glu", 4), ("q_norm_g", 2), ("out_norm_ssm", 4),
         ("out_norm_attn", 4), ("ssm_a_re", 16), ("ssm_a_im", 16),
         ("qk_norm_q", 1), ("qk_norm_k", 1)]
ROW = {}
_at = 0
for _n, _w in _ROWS:
    ROW[_n] = (_at, _at + _w)
    _at += _w
NROW = _at


class Chain:

    def __init__(self, eng, sem):
        self.eng, self.sem, self.n = eng, sem, 0

    def inc(self, ins):
        ins.then_inc(self.sem, 1)
        self.n += 1
        return ins

    def sync(self):
        self.eng.wait_ge(self.sem, self.n)

    def link(self, ins):
        self.inc(ins)
        self.sync()
        return ins


def build_program(nc, I, O):
    with ExitStack() as ctx:
        def sb(name, n, dt=F32):
            return ctx.enter_context(nc.sbuf_tensor(name, [P, n], dt))

        sems = {}

        def S(name):
            if name not in sems:
                sems[name] = ctx.enter_context(nc.semaphore(name))
            return sems[name]

        chains = {}

        def chain(eng, name):
            if name not in chains:
                chains[name] = Chain(eng, S(name))
            return chains[name]

        ps = [ctx.enter_context(nc.psum_tensor(f"bank{i}", [P, 512], F32)) for i in range(8)]

        xs_dram = nc.dram_tensor("normed_tokens", [T, D], F32).ap()
        lists_dram = nc.dram_tensor("slot_lists", [ROUNDS * SLOTS * NE, 4], F32).ap()
        y2_dram = nc.dram_tensor("expert_rows", [2 * T, D], F32).ap()

        cst = sb("constants", LASTING)

        def C(name, rows=P):
            a, w = COL[name]
            if a >= LASTING:
                return cst_early[0:rows, a - LASTING:a - LASTING + w]
            return cst[0:rows, a:a + w]

        x = sb("x", TT * D)
        R = sb("region_ssm_then_ring", 18432)
        O1 = sb("region_projection_then_w_out", 8192)
        cst_early = O1[:, 7392:7392 + NCONST - LASTING]
        ident = C("ident")
        QT = sb("region_qT", 3072)
        KT = sb("region_kT", 3072)
        CA = sb("region_cache_then_prompt", 5120)
        UQ = sb("region_w_uq", 1536)
        LP = sb("region_loop", 2560)
        uT = sb("uT", 4 * T)
        w_uk = sb("w_uk", H * NOPE)
        w_uv = sb("w_uv", H * VD)
        v = sb("v_prompt", 2 * 512)
        CT = sb("ssm_c_T", 1024)
        vrow = sb("vector_rows", P)
        vec = sb("vector_columns", NROW)
        ckvn = sb("ckv_normed", TT * KR)
        krn = sb("k_rope", TT * ROPE)
        ckvT = sb("ckv_new_T", TP)
        g_row = sb("gain_rows", KR + 2 * QK)
        par = sb("ssm_params", 16 * 16)
        small = sb("small", 160)
        st0 = QT[:, 2560:2816]
        n2 = QT[:, 2816:3072]
        soft = KT[:, 2560:2824]
        kr2 = KT[:, 2824:2832]
        w_r = uT[:, 0:KD * 36]
        b_r = uT[:, KD * 36:(KD + 1) * 36]
        pgf = sb("page_table_f", 2 * 16)
        pgt = sb("page_table_i", 16, I32)
        olat = vrow

        w_in = R[:, 0:KD * DIN].rearrange("p (k n) -> p k n", k=KD)
        bre, bim = R[:, 0:5120], R[:, 5120:10240]
        tmp = [R[:, 10240 + 640 * i:10240 + 640 * (i + 1)] for i in range(8)]
        Ssb = [R[:, 15360 + 1088 * i:15360 + 1088 * (i + 1)] for i in range(2)]
        xn = O1[:, 0:3072]
        nT = O1[:, 3072:6144].rearrange("p (k t) -> p k t", k=KD)
        z = O1[:, 6144:6144 + TT * ZW].rearrange("p (i n) -> p i n", i=TT)
        q = O1[:, 0:2304].rearrange("p (i h d) -> p i h d", i=TT, h=H)
        kk = O1[:, 2304:4608].rearrange("p (i h d) -> p i h d", i=TT, h=H)
        cqn = O1[:, 4608:4608 + TT * QR].rearrange("p (i n) -> p i n", i=TT)
        cqT = O1[:, 5376:5376 + 768].rearrange("p (k t) -> p k t", k=2)
        w_out = O1[:, 0:8192].rearrange("p (k n) -> p k n", k=8)
        qT = QT[:, 0:H * T].rearrange("p (h t) -> p h t", h=H)
        kT = KT[:, 0:H * T].rearrange("p (h t) -> p h t", h=H)
        w_uq = UQ[:, :].rearrange("p (k n) -> p k n", k=2)
        w_ukT = UQ[:, 0:1024].rearrange("p (h r) -> p h r", h=H)
        olT = UQ[:, 0:512]
        qa = UQ[:, 512:1024]
        s_new = UQ[:, 1024:1536]
        qrp = R[:, 17792:18304]
        bd4 = [r[:, 0:2048].rearrange("p (j c) -> p j c", j=4) for r in (QT, KT)]
        braw = LP[:, 1024:1536].rearrange("p (a i c) -> p a i c", a=2, i=LT)
        cT = [LP[:, 0:512], LP[:, 512:1024]]
        krT = [LP[:, 1024:1280], LP[:, 1280:1536]]
        sq = [LP[:, 1536:2048], LP[:, 2048:2560]]
        cache = [CA[:, 1280 * i:1280 * i + 1024] for i in range(4)]
        cachr = [CA[:, 1280 * i + 1024:1280 * (i + 1)] for i in range(4)]

        limits = {}

        def limit(pool, last_row, count):
            if isinstance(count, int):
                return last_row
            if last_row not in limits:
                limits[last_row] = pool.alloc_register(f"last_row_{last_row}")
            reg = limits[last_row]
            pool.reg_add(reg, count, last_row)
            pool.reg_alu(reg, reg, last_row, ALU.min)
            return reg

        def bc(ap, dim, n):
            shape = list(ap.shape)
            shape.insert(dim, n)
            return ap.unsqueeze(dim).to_broadcast(shape)

        def v3(ap, a):
            return ap.rearrange("p (a b) -> p a b", a=a)

        PER = dict(kr_transposed=2, kr_copied=2, c_transposed=4, c_copied=4, keys_made=16, squared=16,
                   summed=16, scored=16, sums_ready=2, rs_key=2, scaled=2, dve_seq=4, carried=1,
                   tail_dve=3, max_ready=1, max_T=1, diag_ready=1, max_row=1, centred=1, exp_done=1,
                   exp_summed=1, values_done=1, lat_scaled=1, lat_T=1, lat_copied=1,
                   turns=1, fractions=1, trig=1, rotated=1, scanned=1, products=1, states=1)

        def at(name, b, k):
            return b * PER[name] + k

        def need(eng, name, value):
            if not isinstance(value, int) or value > 0:
                eng.wait_ge(S(name), value)

        def wait(eng, name, b, k):
            need(eng, name, at(name, b, k))

        TB, KRB, SB, AB, MB = 2, 3, (4, 5), 6, 7
        tri_c, eye = C("tri"), ident
        smx, ssum = soft[:, 0:NS], soft[:, NS:2 * NS]
        sdiag = soft[0:NS, 2 * NS:3 * NS]
        m64, rl = soft[0:NS, 4 * NS:4 * NS + 1], soft[0:NS, 4 * NS + 1:4 * NS + 2]
        cache_rows = I["cache_ckv"][0].rearrange("n (r s) d -> (n r) (s d)", s=RUN)
        rope_rows = I["cache_krope"][0].rearrange("n (r s) d -> (n r) (s d)", s=RUN)
        far_row = POOL * (PAGE // RUN) - 1

        krsq = R[:, 17536:17792]

        def gather_unit(pool, slot, b):
            off = bass.IndirectOffsetOnAxis(ap=page_idx[:, slot:slot + 1], axis=0)
            last = limit(pool, far_row, b)
            pool.indirect_dma_start(out=cache[slot], out_offset=None, in_=cache_rows, in_offset=off,
                                    bounds_check=last, oob_is_err=False).then_inc(S(f"pages{slot}"), 16)
            pool.indirect_dma_start(out=cachr[slot], out_offset=None, in_=rope_rows, in_offset=off,
                                    bounds_check=last, oob_is_err=False).then_inc(S(f"pages{slot}"), 16)

        def seq_slices(b):
            return bass.ds(b * NS, NS), bass.ds(b * 2, 2), bass.ds(b * (2 * T), 2 * T)

        def two(ap):
            return v3(ap, 2)

        f_t, f_f, f_cos, f_sin, f_1, f_2, f_3, f_4 = tmp

        def pool_seq(pool, b, par, gather):
            _, til, sl = seq_slices(b)
            wait(pool, "trig", b, 1)
            pool.tensor_tensor(f_1, bre[:, sl], f_cos, ALU.mult)
            pool.tensor_tensor(f_2, bim[:, sl], f_sin, ALU.mult)
            pool.tensor_tensor(f_3, bim[:, sl], f_cos, ALU.mult)
            pool.tensor_tensor(f_4, bre[:, sl], f_sin, ALU.mult).then_inc(S("rotated"), 1)
            def gather_next(u):
                wait(pool, "values_done", b, 0)
                slot = 2 * (1 - par) + u
                pool.tensor_copy(page_idx[:, slot:slot + 1], page_all[:, bass.ds(b * 2 + (2 + u), 1)]).then_inc(S("index_copied"), 1)
                pool.wait_ge(S("index_copied"), b * 2 + (u - 1))
                gather_unit(pool, slot, b)

            if gather:
                gather_next(0)
            wait(pool, "scanned", b, 1)
            pool.tensor_tensor(f_1, f_2, f_cos, ALU.mult)
            pool.tensor_tensor(f_3, f_4, f_sin, ALU.mult)
            pool.tensor_tensor(f_t, f_2, f_sin, ALU.mult)
            pool.tensor_tensor(f_f, f_4, f_cos, ALU.mult).then_inc(S("products"), 1)
            if gather:
                gather_next(1)

        PE_TAIL = {2: 0, 5: 1, 10: 2, 14: 3}
        DVE_AT = {"states": -1, "tail": (-1, 1, 3, 6, 8, 12), "fractions": 0, "rope 0": 2, "copy rope": 4, "scan inputs": 7,
                  "scan 0": 9, "scan 1": 10, "scale": 12, "rope 1": 13}
        ACT_AT = {"turns": 0, "trig": 2, "latents 2": 3, "exp": 7, "latents 3": 7, "rsqrt": 9}

        def pe_seq(pe, b, half, par, t):
            sl, _, _ = seq_slices(b)

            def transposes(g):
                u, slot = g // 2, 2 * par + g // 2
                if g % 2 == 0:
                    pe.wait_ge(S(f"pages{slot}"), half * 32 + 32)
                    wait(pe, "kr_copied", b, u)
                    for j in range(2):
                        ins = pe.transpose(ps[KRB][:, j * P:(j + 1) * P], cachr[slot][:, j * P:(j + 1) * P], ident)
                    ins.then_inc(S("kr_transposed"), 1)
                wait(pe, "c_copied", b, g)
                for i in range(4):
                    c = (4 * (g % 2) + i) * P
                    ins = pe.transpose(ps[TB][:, i * P:(i + 1) * P], cache[slot][:, c:c + P], ident)
                ins.then_inc(S("c_transposed"), 1)

            def keys_scores(g):
                u = g // 2
                wait(pe, "c_copied", b, g + 1)
                if g % 2 == 0:
                    wait(pe, "kr_copied", b, u + 1)
                    wait(pe, "scaled", b, u - 1)
                for i in range(4):
                    n = 4 * g + i
                    wait(pe, "squared", b, n - 1)
                    lat = cT[g % 2][:, i * P:(i + 1) * P]
                    pe.matmul(ps[n % 2][:, :], lat, w_uk[:, :], start=True, stop=True).then_inc(S("keys_made"), 1)
                    o = ps[SB[u]][:, (n % 8) * NS:(n % 8 + 1) * NS]
                    pe.matmul(o, lat, qa[:, sl], start=True, stop=False)
                    pe.matmul(o, krT[u][:, (n % 8 // 4) * P:(n % 8 // 4 + 1) * P],
                              qrs[par][:, NS * i:NS * (i + 1)], start=False, stop=True).then_inc(S("scored"), 1)
                    if t is not None and n in PE_TAIL:
                        pe_tail(pe, t, 1 - par, PE_TAIL[n])

            transposes(0)
            transposes(1)
            keys_scores(0)
            transposes(2)
            keys_scores(1)
            transposes(3)
            keys_scores(2)
            keys_scores(3)

        def pe_tail(pe, t, par, part):
            if part == 0:
                wait(pe, "max_ready", t, 1)
                wait(pe, "lat_copied", t, 0)
                pe.transpose(ps[MB][:, 0:P], soft[:, 0:P], ident).then_inc(S("max_T"), 1)
            if part == 1:
                wait(pe, "diag_ready", t, 1)
                pe.matmul(ps[MB][:, 128:128 + NS], C("ones", NS), sdiag, start=True, stop=True).then_inc(S("max_row"), 1)
            if part == 2:
                wait(pe, "exp_done", t, 1)
                wait(pe, "lat_scaled", t, 0)
                for n in range(16):
                    slot, c = 2 * par + n // 8, (n % 8) * P
                    pe.matmul(ps[AB][0:NS, 0:KR], Ssb[par][:, n * NS:(n + 1) * NS], cache[slot][:, c:c + P],
                              start=(n == 0), stop=False)
                pe.matmul(ps[AB][0:NS, 0:KR], Ssb[par][:, 1024:1088], ckvn[:, 2 * KR:3 * KR], start=False, stop=True)
                wait(pe, "exp_summed", t, 1)
                pe.matmul(ps[AB][0:NS, KR:KR + 1], ssum, C("ones")[:, 0:1], start=True, stop=True).then_inc(S("values_done"), 1)
            if part == 3:
                wait(pe, "lat_scaled", t, 1)
                pe.transpose(ps[MB][:, 256:384], olat[:, :], ident).then_inc(S("lat_T"), 1)

        def act_seq_(act, b, par, t):
            def copy_latents(g):
                wait(act, "c_transposed", b, g + 1)
                wait(act, "scored", b, 4 * (g - 1))
                act.activation(cT[g % 2], ps[TB][:, :], ACT.Copy).then_inc(S("c_copied"), 1)

            def square(n):
                wait(act, "keys_made", b, n + 1)
                wait(act, "summed", b, n - 1)
                act.activation(sq[n % 2], ps[n % 2][:, :], ACT.Square, scale=QK ** -0.5).then_inc(S("squared"), 1)

            def key_rsqrt(s, u, parity):
                ap = n2[:, parity * P + u * 64:parity * P + (u + 1) * 64]
                wait(act, "sums_ready", s, u + 1)
                act.activation(ap, ap, ACT.Ln, bias=EPS).then_inc(S("act_rs"), 1)
                act.wait_ge(S("act_rs"), s * 2 + (u + 1))
                act.activation(ap, ap, ACT.Exp, scale=-0.5).then_inc(S("rs_key"), 1)

            def turns():
                wait(act, "states", b, 0)
                for i in range(2):
                    ins = act.activation(f_t[:, i * T:(i + 1) * T], C("step"), ACT.Copy, scale=p_f[:, bass.ds(b * 2 + i, 1)])
                ins.then_inc(S("turns"), 1)

            def trig():
                wait(act, "fractions", b, 1)
                act.activation(f_1, f_f, ACT.Abs).then_inc(S("act_trig"), 1)
                act.activation(f_sin, f_f, ACT.Sin, scale=TWO_PI)
                act.wait_ge(S("act_trig"), b + 1)
                act.activation(f_cos, f_1, ACT.Sin, scale=-TWO_PI, bias=math.pi / 2).then_inc(S("trig"), 1)
                act.preload_act_table_set(LN_EXP)
                for i in range(2):
                    ins = act.activation(f_t[:, i * T:(i + 1) * T], C("carry"), ACT.Copy, scale=p_mag[:, bass.ds(b * 2 + i, 1)])
                ins.then_inc(S("carried"), 1)

            copy_latents(0)
            if t is not None:
                key_rsqrt(t, 1, 1 - par)
            copy_latents(1)
            for n in range(16):
                square(n)
                if n == ACT_AT["turns"]:
                    turns()
                if n == ACT_AT["trig"]:
                    trig()
                if n == ACT_AT["latents 2"]:
                    copy_latents(2)
                if n == ACT_AT["latents 3"]:
                    copy_latents(3)
                if n == ACT_AT["exp"] and t is not None:
                    act_tail(act, t, 1 - par)
                if n == ACT_AT["rsqrt"]:
                    key_rsqrt(b, 0, par)
            if t is not None:
                act_olat(act, t)

        def act_tail(act, t, par):
            wait(act, "centred", t, 1)
            act.activation(Ssb[par], Ssb[par], ACT.Exp).then_inc(S("exp_done"), 1)

        def act_olat(act, t):
            wait(act, "lat_T", t, 1)
            o = olT.rearrange("p (h b q) -> p h b q", h=H, b=NB)[:, :, bass.ds(t, 1), :]
            act.activation(o, ps[MB][:, 256:256 + NS].rearrange("p (h o q) -> p h o q", h=H, o=1), ACT.Copy).then_inc(S("lat_copied"), 1)

        def scale_scores(ve, s, u, par):
            wait(ve, "rs_key", s, u + 1)
            wait(ve, "scored", s, 8 * (u + 1))
            rs = n2[:, par * P + u * 64:par * P + (u + 1) * 64]
            ve.tensor_tensor(v3(Ssb[par][:, u * 512:(u + 1) * 512], 64), v3(ps[SB[u]][:, :], 64), bc(rs, 2, NQ),
                             ALU.mult).then_inc(S("scaled"), 1)

        def ve_tail(ve, t, par, part):
            s64 = Ssb[par][0:NS, 1024:1088]
            if part == 0:
                scale_scores(ve, t, 1, par)
                ve.tensor_tensor(v3(s64, H), v3(s_new[0:NS, bass.ds(t * NS, NS)], H),
                                 bc(C("smask", NS)[:, bass.ds(t * NQ, NQ)], 1, H), ALU.add).then_inc(S("tail_dve"), 1)
            if part == 1:
                ve.wait_ge(S("tail_dve"), t * 3 + 1)
                wait(ve, "scaled", t, 2)
                ve.tensor_reduce(smx, Ssb[par].rearrange("p (n j) -> p j n", j=NS), AX, ALU.max).then_inc(S("max_ready"), 1)
            if part == 2:
                wait(ve, "max_T", t, 1)
                ve.tensor_reduce(m64, ps[MB][0:NS, 0:P], AX, ALU.max).then_inc(S("tail_dve"), 1)
                ve.wait_ge(S("tail_dve"), t * 3 + 2)
                ve.tensor_scalar(sdiag, ident[0:NS, 0:NS], m64, None, ALU.mult).then_inc(S("diag_ready"), 1)
            if part == 3:
                wait(ve, "max_row", t, 1)
                s = v3(Ssb[par], 17)
                ve.tensor_tensor(s, s, bc(ps[MB][:, 128:128 + NS], 1, 17), ALU.subtract).then_inc(S("centred"), 1)
            if part == 4:
                wait(ve, "exp_done", t, 1)
                ve.tensor_reduce(ssum, Ssb[par].rearrange("p (n j) -> p j n", j=NS), AX, ALU.add).then_inc(S("exp_summed"), 1)
            if part == 5:
                wait(ve, "values_done", t, 1)
                ve.reciprocal(rl, ps[AB][0:NS, KR:KR + 1]).then_inc(S("tail_dve"), 1)
                ve.wait_ge(S("tail_dve"), t * 3 + 3)
                wait(ve, "lat_T", t, 0)
                ve.tensor_scalar(olat[0:NS, :], ps[AB][0:NS, 0:KR], rl, None, ALU.mult).then_inc(S("lat_scaled"), 1)

        def ve_seq(ve, b, half, par, t):
            sl, til, tsl = seq_slices(b)

            def copy_rope(u):
                wait(ve, "kr_transposed", b, u + 1)
                wait(ve, "scored", b, 8 * (u - 1))
                ve.tensor_copy(krT[u], ps[KRB][:, 0:256]).then_inc(S("kr_copied"), 1)

            def rope_squares(u):
                slot = 2 * par + u
                ve.scalar_tensor_tensor(out=krsq, in0=cachr[slot], scalar=1 / QK, in1=cachr[slot], op0=ALU.mult,
                                        op1=ALU.mult).then_inc(S("dve_seq"), 1)
                ve.wait_ge(S("dve_seq"), b * 4 + (2 * u + 1))
                ve.tensor_reduce(kr2[:, :], v3(krsq, 8), AX, ALU.add).then_inc(S("dve_seq"), 1)

            def add_rope(u):
                ap = v3(n2[:, par * P + u * 64:par * P + (u + 1) * 64], 8)
                ve.wait_ge(S("dve_seq"), b * 4 + (2 * u + 2))
                wait(ve, "summed", b, 8 * (u + 1))
                ve.tensor_tensor(ap, ap, bc(kr2[:, :], 2, H), ALU.add).then_inc(S("sums_ready"), 1)

            def fractions():
                wait(ve, "turns", b, 1)
                ve.tensor_scalar(f_2, f_t, MAGIC, MAGIC, ALU.add, ALU.subtract).then_inc(S("dve_f"), 1)
                ve.wait_ge(S("dve_f"), b + 1)
                ve.tensor_tensor(f_f, f_t, f_2, ALU.subtract).then_inc(S("fractions"), 1)

            def scan_inputs():
                wait(ve, "rotated", b, 1)
                ve.tensor_tensor(f_1, f_1, f_2, ALU.add).then_inc(S("dve_ssm"), 1)
                ve.tensor_tensor(f_3, f_3, f_4, ALU.subtract).then_inc(S("dve_ssm"), 1)
                ve.wait_ge(S("dve_ssm"), b * 5 + 2)
                for a, f in ((0, f_1), (1, f_3)):
                    start = two(f)[:, :, SEQ:T].rearrange("p i (b q) -> p i b q", b=NB)[:, :, :, 0]
                    h0 = st0[:, a * P:(a + 1) * P].rearrange("p (b i) -> p i b", b=NB)[:, til, :]
                    ve.tensor_tensor(start, start, h0, ALU.add).then_inc(S("dve_ssm"), 1)

            def scan(a):
                if a == 0:
                    wait(ve, "carried", b, 1)
                    ve.wait_ge(S("dve_ssm"), b * 5 + 4)
                    ve.tensor_tensor_scan(f_2, f_t, f_1, 0.0, ALU.mult, ALU.add).then_inc(S("dve_ssm"), 1)
                else:
                    ve.tensor_tensor_scan(f_4, f_t, f_3, 0.0, ALU.mult, ALU.add).then_inc(S("scanned"), 1)

            wait(ve, "scored", b, -16)
            ve.tensor_tensor(qrs[par].rearrange("p (s j) -> p s j", s=4), bc(qrp[:, sl], 1, 4), bc(C("quad"), 2, NS), ALU.mult)
            copy_rope(0)
            def add_side(n, step):
                side.setdefault(n, []).append(step)

            side = {}
            if t is not None:
                add_side(DVE_AT["states"], lambda: ve_states(ve, t))
                for part in range(6):
                    add_side(DVE_AT["tail"][part], lambda part=part: ve_tail(ve, t, 1 - par, part))
            add_side(DVE_AT["fractions"], fractions)
            add_side(DVE_AT["rope 0"], lambda: rope_squares(0))
            add_side(DVE_AT["copy rope"], lambda: copy_rope(1))
            add_side(7, lambda: add_rope(0))
            add_side(DVE_AT["scan inputs"], scan_inputs)
            add_side(DVE_AT["scan 0"], lambda: scan(0))
            add_side(DVE_AT["scan 1"], lambda: scan(1))
            add_side(DVE_AT["scale"], lambda: scale_scores(ve, b, 0, par))
            add_side(DVE_AT["rope 1"], lambda: rope_squares(1))
            add_side(15, lambda: add_rope(1))
            for step in side.get(-1, []):
                step()
            for n in range(16):
                wait(ve, "squared", b, n + 1)
                ve.tensor_reduce(n2[:, par * P + n * H:par * P + (n + 1) * H], v3(sq[n % 2], H), AX, ALU.add).then_inc(S("summed"), 1)
                for step in side.get(n, []):
                    step()

        def ve_states(ve, b):
            tsl = seq_slices(b)[2]
            wait(ve, "products", b, 1)
            ve.tensor_tensor(bre[:, tsl], f_1, f_3, ALU.subtract)
            ve.tensor_tensor(bim[:, tsl], f_t, f_f, ALU.add).then_inc(S("states"), 1)

        def pairs_from(eng, n, body):
            body(0)
            with eng.Fori(1, n) as i:
                body(i)

        def rounds(eng, seq):
            seq(0, 0, 0, None)

            def two_sequences(i):
                seq(i * 2 + 1, i, 1, i * 2)
                seq(i * 2 + 2, i + 1, 0, i * 2 + 1)

            pairs_from(eng, (NB - 2) // 2, two_sequences)
            seq(NB - 1, NB // 2 - 1, 1, NB - 2)

        def pool_loop(pool):
            pool.wait_ge(S("pole_exps_ready"), 2)
            used(pool, "bu30")
            used(pool, "bu31")
            used(pool, "qr")
            rounds(pool, lambda b, half, par, t: pool_seq(pool, b, par, t is not None and not (isinstance(b, int) and b == NB - 1)))
            post_pool(pool)

        def pe_loop(pe):
            rounds(pe, lambda b, half, par, t: pe_seq(pe, b, half, par, t))
            post_pe(pe)

        def act_loop(act):
            def seq(b, half, par, t):
                act_seq_(act, b, par, t)
            rounds(act, seq)
            ap = n2[:, P + 64:2 * P]
            wait(act, "sums_ready", NB - 1, 2)
            act.activation(ap, ap, ACT.Ln, bias=EPS).then_inc(S("act_rs"), 1)
            act.wait_ge(S("act_rs"), 2 * NB)
            act.activation(ap, ap, ACT.Exp, scale=-0.5).then_inc(S("rs_key"), 1)
            act_tail(act, NB - 1, 1)
            act_olat(act, NB - 1)
            post_act(act)

        def ve_loop(ve):
            for name in ("qr", "qa", "sn"):
                used(ve, name)
            rounds(ve, lambda b, half, par, t: ve_seq(ve, b, half, par, t))
            ve_states(ve, NB - 1)
            for part in range(4):
                ve_tail(ve, NB - 1, 1, part)
            post_ve(ve)
        qrs = [ckvT[:, 0:256], g_row[:, 0:256]]
        page_idx = sb("page_row_index", 4, U32)
        page_all = sb("page_row_indices", 2 * NB, U32)
        sraw = R[:, 10240:10496]
        craw = R[:, 10496:11520].rearrange("p (a m e s) -> p a m e s", a=2, m=4, e=2)
        xst = R[:, 11520:12544].rearrange("p (a i e c) -> p a i e c", a=2, i=LT, e=2)
        junk = R[:, 14080:15104]
        rt = [R[:, 12544 + 384 * i:12544 + 384 * (i + 1)] for i in range(4)]
        qr4 = R[:, 14080:15104].rearrange("p (h e d) -> p h e d", h=H, e=4)
        ldt = small[:, 0:2]
        ms1, ms2, msq, msk = small[:, 2:5], small[:, 5:11], small[:, 16:40], small[:, 40:64]
        msA, msS, msH = small[:, 64:67], small[:, 67:70], small[:, 70:73]

        def prm(k):
            return par[:, 16 * k:16 * k + 16]

        (p_dt, p_mag, p_ang, p_k, p_th, p_f, p_sin, p_cos, p_lr, p_li, p_den, p_cr, p_ci, p_a, p_b,
         p_ab) = [prm(k) for k in range(16)]

        def vcol(name):
            a, b = ROW[name]
            return vec[:, a:b]

        order = [("vec", 6), ("xT0", 0), ("xT1", 1), ("xT2", 2), ("xT3", 3), ("xT4", 4), ("xT5", 5),
                 ("page", 7), ("u0", 0), ("u1", 1), ("u2", 2), ("u3", 3), ("ct0", 6), ("ct1", 7),
                 ("z0", 4), ("z1", 5), ("z2", 0), ("bd0", 1), ("bd1", 2)]

        def bu_groups(m):
            return [f"bu{2 * (4 * m + j) + a}" for j in range(4) for a in range(2)]

        order += [(name, n) for n, name in enumerate(bu_groups(0))]
        order += [("cq0", 2), ("cq1", 3), ("ckvT", 4)]
        order += [(name, n) for m in range(1, 4) for n, name in enumerate(bu_groups(m))]
        order += [("q00", 5), ("q01", 6), ("q10", 7), ("q11", 0), ("q20", 1), ("q21", 2),
                  ("k0", 3), ("k1", 4), ("k2", 5), ("v0", 6), ("v1", 7)]
        order += [(f"qT{h}", h) for h in range(8)] + [(f"kT{h}", h) for h in range(8)]
        order += [("uk0", 0), ("uk1", 1), ("qr", 2), ("qa", 3), ("sn", 4)]
        nth, uses = {}, [0] * 8
        for name, b in order:
            nth[name] = (b, uses[b])
            uses[b] += 1
        pre_uses = list(uses)

        def fill(eng, name):
            b, n = nth[name]
            if n:
                eng.wait_ge(S(f"free{b}"), n)
            return ps[b]

        def filled(ins, name):
            ins.then_inc(S(f"full{nth[name][0]}"), 1)

        def read(eng, name):
            b, n = nth[name]
            eng.wait_ge(S(f"full{b}"), n + 1)
            return ps[b]

        def was_read(ins, name):
            return ins.then_inc(S(f"free{nth[name][0]}"), 1)

        def used(eng, name):
            b, n = nth[name]
            eng.wait_ge(S(f"free{b}"), n + 1)

        w_glu = LP[:, 0:2048].rearrange("p (k n) -> p k n", k=4)
        hstates = LP[:, 2048:2560]
        hlast = tmp[0][:, 0:2 * P]
        yT, g1 = R[:, 12288:13568], R[:, 13568:14848]
        soT = R[:, 16128:17664].rearrange("p (m t) -> p m t", m=4)
        sqT = KT[:, 0:1536].rearrange("p (m t) -> p m t", m=4)
        junk_a, junk_h = KT[:, 1536:2048], R[:, 13568:14592]
        Sp = CA[:, 0:3072].rearrange("p (h t) -> p h t", h=H)
        PT = [CA[:, 3072 + 384 * i:3072 + 384 * (i + 1)] for i in range(2)]
        g2row = CA[:, 3840:4864]
        att = QT[:, 0:1536]
        attT = QT[:, 1536:3072].rearrange("p (k t) -> p k t", k=4)
        xs = KT
        xsT = O1[:, 0:3072].rearrange("p (k t) -> p k t", k=KD)
        pm = [small[:, 80 + 16 * i:96 + 16 * i] for i in range(4)]
        nbg = small[:, 144:148]
        gain4 = small[:, 152:156]
        post = [(f"y{m}", m) for m in range(4)] + [("hf0", 4), ("hf1", 5)]
        post += [(f"s{h}", (4, 5, 6, 7)[h % 4]) for h in range(H)] + [("as", 3)]
        post += [(f"g{m}", m) for m in range(4)]
        post += [("o0", 0), ("o1", 1)]
        post += [(f"p{h}", 4 + h % 4) for h in range(H)]
        post += [("ss", 2)]
        post += [(f"w{i}{a}", (3, 4, 5, 6, 7, 2)[2 * i + a]) for i in range(TT) for a in range(2)]
        post += [("at0", 0), ("at1", 1), ("at2", 3)]
        post += [("w02", 4), ("w03", 5), ("w12", 6), ("w13", 7), ("xt0", 3), ("xt1", 5), ("rt", 2), ("w22", 0), ("w23", 1),
                 ("xt2", 4), ("xt3", 6), ("xt4", 7), ("xt5", 3), ("cum", 0)]
        for name, b in post:
            nth[name] = (b, uses[b])
            uses[b] += 1

        _off = [0]

        def rv(n):
            a = _off[0]
            _off[0] += n
            return QT[:, a:a + n]

        lgt, mask4, mask8a, mask8b = rv(108), rv(12), rv(24), rv(24)
        le8, work8, pairs, one = rv(24), rv(24), rv(192), rv(96)
        m4, m8, e4, w12, psel, tsum = rv(3), rv(6), rv(12), rv(6), rv(3), rv(3)
        first, second, routed, where, prod = rv(96), rv(96), rv(96), rv(96), rv(96)
        rows = rv(6 * 4)
        tgt, cnt, lst, gates = rv(6), rv(1), rv(4 * NE), rv(NE)
        assert _off[0] <= 3072
        gall, sall = sb("gather_rows", NE, U32), sb("scatter_rows", NE, U32)
        gsi = sb("expert_row_index", 4, U32)
        tgi = sb("list_row_index", 6, U32)
        most = sb("most_tokens", 1, I32)
        ring = [R[:, 6144 * i:6144 * (i + 1)] for i in range(2)]
        Xg = [R[:, 12288 + HD * i:12288 + HD * (i + 1)] for i in range(2)]
        XgT = [R[:, 13312 + HD * i:13312 + HD * (i + 1)] for i in range(2)]
        Yo = [R[:, 14336 + HD * i:14336 + HD * (i + 1)] for i in range(2)]
        thb, hmb, hS, hTb = [O1[:, P * i + 3072:P * (i + 1) + 3072] for i in range(4)]
        xs_halves = xs_dram.rearrange("t (a d) -> (t a) d", a=2)
        y2_halves = y2_dram.rearrange("t (a d) -> (t a) d", a=2)
        outs_total = 6 + 4 + 3

        def load_expert(sp, r, e, eh, s):
            sl = bass.ds(e, 1)
            need(sp, "gate_up_done", r * NE + e - 1)
            for a, name in enumerate(("w_gate", "w_up")):
                sp.dma_start(ring[s][:, 2048 * a:2048 * (a + 1)].rearrange("p (h x) -> p h x", h=2),
                             I[name][0][sl].rearrange("e (h p c) f -> (e p) h (c f)", h=2, c=4)).then_inc(S(f"gate_up_loaded{s}"), 16)
            need(sp, "down_done", r * NE + e - 1)
            sp.dma_start(ring[s][:, 4096:6144].rearrange("p (j n) -> p j n", j=2),
                         I["w_down"][0][sl].rearrange("e (j p) n -> (e p) j n", j=2)).then_inc(S(f"down_loaded{s}"), 16)

        def more_rounds(eng, round_):
            eng.wait_ge(S("counts_ready"), 1)
            n = eng.value_load(most[0:1, 0:1], min_val=0, max_val=T)
            with eng.Fori(1, ROUNDS) as r:
                with eng.If(n > r * SLOTS):
                    round_(r)
                eng.nop()

        def post_sync(sp):
            wait(sp, "scored", NB - 1, 16)
            wait(sp, "summed", NB - 1, 16)
            sp.dma_start(w_glu, I["ssm_w_glu"][0].rearrange("(k p) n -> p k n", p=P)).then_inc(S("w_glu_loaded"), 16)
            wait(sp, "values_done", NB - 1, 1)
            sp.dma_start(g2row, I["norm2_g"].to_broadcast([P, D])).then_inc(S("g2_loaded"), 16)
            with nc.allow_non_contiguous_dma(reason="router weights"):
                used(sp, "y3")
                sp.dma_start(w_r[:, :].rearrange("p (k n) -> p k n", k=KD)[:, :, 0:NG],
                             I["w_router_group"][0].rearrange("(k p) n -> p k n", p=P)).then_inc(S("router_loaded"), 16)
                sp.dma_start(w_r[:, :].rearrange("p (k n) -> p k n", k=KD)[:, :, NG:],
                             I["w_router_expert"][0].rearrange("(k p) n -> p k n", p=P)).then_inc(S("router_loaded"), 16)
                sp.dma_start(b_r[:, 0:NG], I["b_router_group"].to_broadcast([P, NG])).then_inc(S("router_loaded"), 16)
                sp.dma_start(b_r[:, NG:], I["b_router_expert"].to_broadcast([P, NE])).then_inc(S("router_loaded"), 16)
            used(sp, "hf0")
            used(sp, "hf1")
            for a, (pn, sn) in enumerate((("re_p", "re_s"), ("im_p", "im_s"))):
                sp.dma_start(O[pn].rearrange("o (i e) p -> (o i) (e p)", e=2), hstates[0:LT, 256 * a:256 * a + P]).then_inc(S("outputs_stored"), 16)
                sp.dma_start(O[sn].rearrange("o b (i e) p -> (o b i) (e p)", e=2), hstates[:, 256 * a + P:256 * (a + 1)]).then_inc(S("outputs_stored"), 16)
            for s in range(2):
                load_expert(sp, 0, s, 0, s)
            for i in range(TT):
                n = P if i < 2 else NS
                sp.wait_ge(S("xs_ready"), i + 1)
                sp.dma_start(xs_dram[i * P:i * P + n, :], xs[0:n, i * D:(i + 1) * D]).then_inc(S("xs_stored"), 16)

            def load_lists(r):
                src = lists_dram.rearrange("(s e) c -> s (e c)", e=NE)[bass.ds(r * SLOTS, SLOTS)]
                for a in range(2):
                    sp.dma_start(lst[SLOTS * a:SLOTS * (a + 1), :], src).then_inc(S("lists_loaded"), 16)

            def round_(r):
                load_lists(r)
                load_expert(sp, r, 2, 1, 0)

                def two_experts(i):
                    load_expert(sp, r, i * 2 + 3, i + 1, 1)
                    load_expert(sp, r, i * 2 + 4, i + 2, 0)

                pairs_from(sp, (NE - 4) // 2, two_experts)
                load_expert(sp, r, NE - 1, NE // 2 - 1, 1)

            sp.wait_ge(S("list_rows_written"), 16 * 6)
            round_(0)

            def later(r):
                for s in range(2):
                    load_expert(sp, r, s, 0, s)
                round_(r)

            more_rounds(sp, later)
            sp.wait_ge(S("moe_done"), 1)
            for i in range(TT):
                n = P if i < 2 else NS
                for a in range(2):
                    sp.dma_start(R[0:n, 3072 * a + i * D:3072 * a + (i + 1) * D],
                                 y2_dram[a * T + i * P:a * T + i * P + n, :]).then_inc(S(f"rows{i}_back"), 16)
            for i in range(TT):
                sp.wait_ge(S("y_ready"), i + 1)
                if i < 2:
                    sp.dma_start(O["y_p"][0, i * P:(i + 1) * P, :], x[:, i * D:(i + 1) * D]).then_inc(S("outputs_stored"), 16)
                else:
                    sp.dma_start(O["y_s"].rearrange("b t d -> (b t) d"), x[0:NS, 2 * D:]).then_inc(S("outputs_stored"), 16)
            sp.wait_ge(S("outputs_stored"), 16 * outs_total)

        def post_pool(pool):
            wait(pool, "centred", NB - 1, 1)
            wait(pool, "values_done", NB - 1, 1)
            pool.memset(soT[:, :, T:TP], 0.0).then_inc(S("post_pads"), 1)
            used(pool, "s7")
            pool.memset(sqT[:, :, T:TP], 0.0).then_inc(S("post_pads"), 1)
            pool.wait_ge(S("post_pads"), 2)
            pool.memset(att[NS:P, 1024:1536], 0.0).then_inc(S("post_pads"), 1)
            pool.wait_ge(S("post_pads"), 3)
            pool.wait_ge(S("xs_ready"), TT)
            for i in range(2):
                pool.memset(Xg[i], 0.0).then_inc(S("gather_cleared"), 1)
            pool.wait_ge(S("gather_cleared"), 2)
            pool.wait_ge(S("xs_stored"), 16 * TT)

            column = pool.alloc_register("expert_column")

            def column_of(r, e):
                if not isinstance(e, int):
                    return bass.ds(e, 1)
                if isinstance(r, int):
                    return slice(e, e + 1)
                pool.reg_add(column, r, e)
                pool.reg_alu(column, column, e, ALU.min)
                return bass.ds(pool.snap(column, min_val=0, max_val=NE - 1), 1)

            pool.wait_ge(S("list_rows_ready"), 1)
            pool.wait_ge(S("lists_emptied"), 16)
            for n in range(6):
                pool.indirect_dma_start(out=lists_dram, out_offset=bass.IndirectOffsetOnAxis(ap=tgi[:, n:n + 1], axis=0),
                                        in_=rows[:, 4 * n:4 * n + 4], in_offset=None,
                                        bounds_check=ROUNDS * SLOTS * NE - 1, oob_is_err=False).then_inc(S("list_rows_written"), 16)

            def gather(r, e, eh, s):
                need(pool, "x_T", r * NE + e - 1)
                pool.tensor_copy(gsi[:, s:s + 1], gall[:, column_of(r, e)]).then_inc(S("gather_index"), 1)
                pool.wait_ge(S("gather_index"), r * NE + e + 1)
                last = limit(pool, 2 * T - 1, r * NE + e)
                pool.indirect_dma_start(out=Xg[s], out_offset=None, in_=xs_halves,
                                        in_offset=bass.IndirectOffsetOnAxis(ap=gsi[:, s:s + 1], axis=0),
                                        bounds_check=last, oob_is_err=False).then_inc(S(f"tokens{s}"), 16)

            def scatter(r, e, eh, s):
                pool.wait_ge(S("y_copied"), r * NE + e + 1)
                value = (r * (NE // 2) + eh) * 16
                need(pool, f"scattered{s}", value)
                pool.tensor_copy(gsi[:, 2 + s:3 + s], sall[:, column_of(r, e)]).then_inc(S("scatter_index"), 1)
                pool.wait_ge(S("scatter_index"), r * NE + e + 1)
                last = limit(pool, 4 * T - 1, r * NE + e)
                pool.indirect_dma_start(out=y2_halves, out_offset=bass.IndirectOffsetOnAxis(ap=gsi[:, 2 + s:3 + s], axis=0),
                                        in_=Yo[s], in_offset=None, bounds_check=last, oob_is_err=False).then_inc(S(f"scattered{s}"), 16)

            def round_(r):
                pool.wait_ge(S("lists_ready"), r + 1)
                gather(r, 0, 0, 0)
                gather(r, 1, 0, 1)
                gather(r, 2, 1, 0)
                def two_experts(i):
                    gather(r, i * 2 + 3, i + 1, 1)
                    scatter(r, i * 2, i, 0)
                    gather(r, i * 2 + 4, i + 2, 0)
                    scatter(r, i * 2 + 1, i, 1)

                pairs_from(pool, (NE - 4) // 2, two_experts)
                gather(r, NE - 1, NE // 2 - 1, 1)
                for e in range(NE - 4, NE):
                    scatter(r, e, e // 2, e % 2)
                for s in range(2):
                    pool.wait_ge(S(f"scattered{s}"), (r + 1) * (16 * NE // 2))

            round_(0)
            more_rounds(pool, round_)
            pool.memset(small[0:1, 150:151], 0.0).then_inc(S("moe_done"), 1)

        def post_pe(pe):
            wait(pe, "squared", NB - 1, 16)
            wait(pe, "c_copied", NB - 1, 4)
            wait(pe, "kr_copied", NB - 1, 2)
            wait(pe, "states", NB - 1, 1)
            for m in range(4):
                b = fill(pe, f"y{m}")
                for a, src in enumerate((bre, bim)):
                    for j in range(4):
                        i, c = 4 * m + j, 512 * a + m * P + 32 * j
                        ins = pe.matmul(b[32 * j:32 * j + 32, 0:T], CT[:, c:c + 32], src[:, i * T:(i + 1) * T],
                                        start=(a == 0), stop=(a == 1))
                filled(ins, f"y{m}")
                if m in (1, 2):
                    pe_tail(pe, NB - 1, 1, m - 1)
            pe_tail(pe, NB - 1, 1, 2)
            pe_tail(pe, NB - 1, 1, 3)
            wait(pe, "scaled", NB - 1, 2)
            for a, src in enumerate((bre, bim)):
                b = fill(pe, f"hf{a}")
                per_tile = v3(src, LT)
                pe.transpose(b[0:LT, 0:P], per_tile[:, :, SEQ - 1], ident)
                pe.wait_ge(S("last_states"), a + 1)
                filled(pe.transpose(b[:, P:2 * P], hlast[:, a * P:(a + 1) * P], ident), f"hf{a}")
            wait(pe, "lat_copied", NB - 1, 1)
            for h in range(H):
                b = fill(pe, f"s{h}")
                pe.matmul(b[:, 0:P], qT[0:QK, h, 0:P], kT[0:QK, h, 0:P], start=True, stop=True)
                filled(pe.matmul(b[:, P:3 * P], qT[0:QK, h, P:2 * P], kT[0:QK, h, 0:2 * P], start=True, stop=True), f"s{h}")
            b = fill(pe, "as")
            for h in range(H):
                ins = pe.matmul(b[0:NS, h * VD:(h + 1) * VD], olT[:, h * NS:(h + 1) * NS], w_uv[:, h * VD:(h + 1) * VD],
                                start=True, stop=True)
            filled(ins, "as")
            pe.wait_ge(S("gelu_ready"), 1)
            pe.wait_ge(S("w_glu_loaded"), 16)
            for m in range(4):
                b = fill(pe, f"g{m}")
                for k in range(4):
                    ins = pe.matmul(b[:, 0:T], w_glu[:, k, m * P:(m + 1) * P], yT[:, k * T:(k + 1) * T],
                                    start=(k == 0), stop=(k == 3))
                filled(ins, f"g{m}")
            pe.wait_ge(S("prompt_exp_ready"), 1)
            o0, o1 = fill(pe, "o0"), fill(pe, "o1")

            def prompt_T(h):
                b = fill(pe, f"p{h}")
                for j in range(3):
                    ins = pe.transpose(b[:, j * P:(j + 1) * P], Sp[:, h, j * P:(j + 1) * P], ident)
                filled(ins, f"p{h}")

            prompt_T(0)
            for h in range(H):
                if h + 1 < H:
                    prompt_T(h + 1)
                used(pe, f"p{h}")
                pt, c = PT[h % 2], slice(h * VD, (h + 1) * VD)
                v0, v1 = v[:, h * VD:(h + 1) * VD], v[:, 512 + h * VD:512 + (h + 1) * VD]
                i0 = pe.matmul(o0[:, c], pt[:, 0:P], v0, start=True, stop=True)
                if h == H - 1:
                    filled(i0, "o0")
                pe.matmul(o1[:, c], pt[:, P:2 * P], v0, start=True, stop=False)
                i1 = pe.matmul(o1[:, c], pt[:, 2 * P:3 * P], v1, start=False, stop=True)
                if h == H - 1:
                    filled(i1, "o1")
                else:
                    i1.then_inc(S("prompt_values"), 1)
            pe.wait_ge(S("post_pads"), 3)
            pe.wait_ge(S("ssm_squared"), 1)
            b = fill(pe, "ss")
            for i in range(TT):
                for m in range(4):
                    ins = pe.matmul(b[:, i:i + 1], sqT[:, m, i * P:(i + 1) * P], C("ones")[:, 0:1], start=(m == 0), stop=(m == 3))
            filled(ins, "ss")
            pe.wait_ge(S("w_out_loaded"), 16)
            pe.wait_ge(S("so_ready"), 1)

            def out_proj(i, a):
                src, k0, n0 = (soT, 0, 512 * a) if a < 2 else (attT, 4, 512 * (a - 2))
                b = fill(pe, f"w{i}{a}")
                for k in range(4):
                    ins = pe.matmul(b[:, :], src[:, k, i * P:(i + 1) * P], w_out[:, k0 + k, n0:n0 + 512],
                                    start=(k == 0), stop=(k == 3))
                filled(ins, f"w{i}{a}")

            for i in range(TT):
                out_proj(i, 0)
                out_proj(i, 1)
            pe.wait_ge(S("att_ready"), 3)
            for i in range(TT):
                b = fill(pe, f"at{i}")
                for k in range(4):
                    ins = pe.transpose(b[:, k * P:(k + 1) * P], att[:, i * 512 + k * P:i * 512 + (k + 1) * P], ident)
                filled(ins, f"at{i}")

            def normed_T(i):
                pe.wait_ge(S("xs_ready"), i + 1)
                for g in range(2):
                    b = fill(pe, f"xt{2 * i + g}")
                    for k in range(4):
                        c = i * D + (4 * g + k) * P
                        ins = pe.transpose(b[:, k * P:(k + 1) * P], xs[:, c:c + P], ident)
                    filled(ins, f"xt{2 * i + g}")

            wr = w_r[:, :].rearrange("p (k n) -> p k n", k=KD)

            def router(i, b):
                for g in range(2):
                    used(pe, f"xt{2 * i + g}")
                for k in range(KD):
                    ins = pe.matmul(b[:, i * 36:(i + 1) * 36], xsT[:, k, i * P:(i + 1) * P], wr[:, k, :],
                                    start=(k == 0), stop=(k == KD - 1))
                return ins

            for i in range(2):
                used(pe, f"at{i}")
                out_proj(i, 2)
                out_proj(i, 3)
            normed_T(0)
            used(pe, "at2")
            out_proj(2, 2)
            pe.wait_ge(S("router_loaded"), 64)
            rt = fill(pe, "rt")
            router(0, rt)
            out_proj(2, 3)
            normed_T(1)
            router(1, rt)
            normed_T(2)
            filled(router(2, rt), "rt")
            pe.wait_ge(S("routed_ready"), 1)
            b = fill(pe, "cum")
            for i in range(TT + 1):
                before = range(min(i + 1, TT))
                for j in before:
                    ins = pe.matmul(b[:, i * NE:(i + 1) * NE], C("tri") if j == i else C("ones"), routed[:, j * NE:(j + 1) * NE],
                                    start=(j == 0), stop=(j == before[-1]))
            filled(ins, "cum")
            for i in range(8):
                pe.wait_ge(S(f"free{i}"), uses[i])

            def xT(r, e, eh, s):
                pe.wait_ge(S(f"tokens{s}"), (r * (NE // 2) + eh + 1) * 16)
                need(pe, "x_copied", r * NE + e - 1)
                view = Xg[s].rearrange("p (d c) -> p c d", c=4)
                for c in range(4):
                    ins = pe.transpose(ps[s][:, c * P:(c + 1) * P], view[:, c, :], ident)
                ins.then_inc(S("x_T"), 1)

            def gate_up(r, e, eh, s):
                pe.wait_ge(S(f"gate_up_loaded{s}"), (r * (NE // 2) + eh + 1) * 32)
                pe.wait_ge(S("x_copied"), r * NE + e + 1)
                need(pe, "act_ready", r * NE + e - 1)
                w = ring[s][:, 0:4096].rearrange("p (a k f) -> p k a f", a=2, k=KD)
                for k in range(KD):
                    c = (k % 4) * P + (k // 4) * SLOTS
                    for g in range(2):
                        o = ps[2 + s][g * SLOTS:(g + 1) * SLOTS, 0:FE].rearrange("p (a f) -> p a f", a=2)
                        ins = pe.matmul(o, XgT[s][:, c:c + SLOTS], w[:, k, :, g * P:(g + 1) * P], start=(k == 0), stop=(k == KD - 1))
                ins.then_inc(S("gate_up_done"), 1)

            def h_T(r, e, eh, s):
                pe.wait_ge(S("act_ready"), r * NE + e + 1)
                need(pe, "h_copied", r * NE + e)
                pe.transpose(ps[4][:, 0:P], hS, ident).then_inc(S("h_T"), 1)

            def down(r, e, eh, s):
                pe.wait_ge(S("h_copied"), r * NE + e + 1)
                pe.wait_ge(S(f"down_loaded{s}"), (r * (NE // 2) + eh + 1) * 16)
                need(pe, "y_copied", r * NE + e - 1)
                w = ring[s][:, 4096:6144].rearrange("p (j n) -> p j n", j=2)
                for j in range(2):
                    for g in range(2):
                        ins = pe.matmul(ps[5 + s][g * SLOTS:(g + 1) * SLOTS, :], hTb[:, j * SLOTS:(j + 1) * SLOTS],
                                        w[:, j, g * HD:(g + 1) * HD], start=(j == 0), stop=(j == 1))
                ins.then_inc(S("down_done"), 1)

            def round_(r):
                xT(r, 0, 0, 0)
                gate_up(r, 0, 0, 0)
                xT(r, 1, 0, 1)
                h_T(r, 0, 0, 0)
                def two_experts(i):
                    gate_up(r, i * 2 + 1, i, 1)
                    xT(r, i * 2 + 2, i + 1, 0)
                    down(r, i * 2, i, 0)
                    h_T(r, i * 2 + 1, i, 1)
                    gate_up(r, i * 2 + 2, i + 1, 0)
                    xT(r, i * 2 + 3, i + 1, 1)
                    down(r, i * 2 + 1, i, 1)
                    h_T(r, i * 2 + 2, i + 1, 0)

                pairs_from(pe, (NE - 2) // 2, two_experts)
                e = NE - 1
                gate_up(r, e, e // 2, 1)
                down(r, e - 1, (e - 1) // 2, 0)
                h_T(r, e, e // 2, 1)
                down(r, e, e // 2, 1)

            round_(0)
            more_rounds(pe, round_)

        def post_act(act):
            st = chain(act, "act_steps")

            def rsqrt(ap, src, scale):
                st.link(act.activation(ap, src, ACT.Ln, bias=EPS, scale=scale))
                return act.activation(ap, ap, ACT.Exp, scale=-0.5)

            wait(act, "states", NB - 1, 1)
            for a, src in enumerate((bre, bim)):
                last = v3(src, LT)[:, :, SEQ:T].rearrange("p i (b q) -> p b i q", b=NB)[:, :, :, NQ - 1]
                act.activation(v3(hlast[:, a * P:(a + 1) * P], NB), last, ACT.Copy).then_inc(S("last_states"), 1)
            act.wait_ge(S("gelu_inner"), 1)
            act.activation(g1, g1, ACT.Tanh, scale=math.sqrt(2 / math.pi)).then_inc(S("gelu_tanh"), 1)
            for a in range(2):
                b = read(act, f"hf{a}")
                st.inc(act.activation(hstates[0:LT, 256 * a:256 * a + P], b[0:LT, 0:P], ACT.Copy))
                st.sync()
                was_read(act.activation(hstates[:, 256 * a + P:256 * (a + 1)], b[:, P:2 * P], ACT.Copy), f"hf{a}")
            act.wait_ge(S("gelu_ready"), 1)
            for m in range(4):
                b = read(act, f"g{m}")
                was_read(act.activation(g1[:, m * T:(m + 1) * T], b[:, 0:T], ACT.Tanh, scale=0.25, bias=nbg[:, m:m + 1]), f"g{m}")
            act.wait_ge(S("prompt_centred"), 1)
            act.activation(CA[:, 0:3072], CA[:, 0:3072], ACT.Exp).then_inc(S("prompt_exp_ready"), 1)
            for h in range(H):
                if h >= 2:
                    act.wait_ge(S("prompt_values"), h - 1)
                b = read(act, f"p{h}")
                was_read(act.activation(PT[h % 2], b[:, 0:384], ACT.Copy), f"p{h}")
                if h == 3:
                    act.wait_ge(S("glu_out"), 1)
                    used(act, "s7")
                    act.activation(sqT[:, :, 0:T], v3(yT, 4), ACT.Square, scale=0.25).then_inc(S("ssm_squared"), 1)
            act.preload_act_table_set(LN_EXP)
            b = read(act, "ss")
            st.link(act.activation(msS, b[:, 0:TT], ACT.Ln, bias=EPS, scale=1 / 512))
            was_read(act.activation(msS, msS, ACT.Exp, scale=-0.5), "ss")
            act.wait_ge(S("att_ready"), 3)
            act.wait_ge(S("post_pads"), 3)
            for i in range(TT):
                st.link(act.activation(junk_a, att[:, i * 512:(i + 1) * 512], ACT.Square, scale=512 ** -0.5, accum_out=msA[:, i:i + 1]))
            rsqrt(msA, msA, 1.0).then_inc(S("rs_att_ready"), 1)

            def normed_T_copy(i):
                b = read(act, f"xt{2 * i + 1}")
                was_read(act.activation(xsT[:, 4:8, i * P:(i + 1) * P], v3(b[:, :], 4), ACT.Copy), f"xt{2 * i + 1}")

            for i in range(TT):
                act.wait_ge(S("h_ready"), i + 1)
                st.link(act.activation(junk_h, x[:, i * D:(i + 1) * D], ACT.Square, scale=1 / 32, accum_out=msH[:, i:i + 1]))
                rsqrt(msH[:, i:i + 1], msH[:, i:i + 1], 1.0).then_inc(S("rs2_ready"), 1)
                if i:
                    normed_T_copy(i - 1)
            normed_T_copy(TT - 1)
            act.wait_ge(S("router_diffs"), 1)
            st.link(act.activation(e4, e4, ACT.Exp))
            act.activation(w12[:, 0:3], w12[:, 0:3], ACT.Exp).then_inc(S("router_exp"), 1)

            def x_copy(r, e, s):
                act.wait_ge(S("x_T"), r * NE + e + 1)
                need(act, "gate_up_done", r * NE + e - 1)
                act.activation(XgT[s], ps[s][:, :], ACT.Copy).then_inc(S("x_copied"), 1)

            def tanh_(r, e, s):
                act.wait_ge(S("gate_up_done"), r * NE + e + 1)
                need(act, "act_ready", r * NE + e)
                act.activation(thb, ps[2 + s][:, 0:P], ACT.Tanh, scale=0.5).then_inc(S("gate_tanh"), 1)

            def y_copy(r, e, eh, s):
                act.wait_ge(S("down_done"), r * NE + e + 1)
                need(act, f"scattered{s}", (r * (NE // 2) + eh) * 16)
                act.activation(Yo[s], ps[5 + s][:, :], ACT.Copy).then_inc(S("y_copied"), 1)

            def round_(r):
                x_copy(r, 0, 0)
                tanh_(r, 0, 0)
                x_copy(r, 1, 1)
                def two_experts(i):
                    tanh_(r, i * 2 + 1, 1)
                    x_copy(r, i * 2 + 2, 0)
                    y_copy(r, i * 2, i, 0)
                    tanh_(r, i * 2 + 2, 0)
                    x_copy(r, i * 2 + 3, 1)
                    y_copy(r, i * 2 + 1, i, 1)

                pairs_from(act, (NE - 2) // 2, two_experts)
                e = NE - 1
                tanh_(r, e, 1)
                y_copy(r, e - 1, (e - 1) // 2, 0)
                y_copy(r, e, e // 2, 1)

            round_(0)
            more_rounds(act, round_)

        def post_ve(ve):
            st = chain(ve, "dve_steps")
            tt = ve.tensor_tensor
            for m in range(4):
                b = read(ve, f"y{m}")
                was_read(ve.scalar_tensor_tensor(out=yT[:, m * T:(m + 1) * T], in0=uT[:, m * T:(m + 1) * T],
                                                 scalar=vcol("ssm_d")[:, m:m + 1], in1=b[:, 0:T], op0=ALU.mult, op1=ALU.add), f"y{m}")
            for m in range(4):
                used(ve, f"y{m}")
            st.link(tt(g1, yT, yT, ALU.mult))
            st.link(ve.tensor_scalar(g1, g1, 0.044715, 1.0, ALU.mult, ALU.add))
            tt(g1, g1, yT, ALU.mult).then_inc(S("gelu_inner"), 1)
            st.inc(ve.tensor_scalar(nbg, vcol("ssm_b_glu"), 0.5, None, ALU.mult))
            st.inc(ve.tensor_scalar(gain4, vcol("out_norm_ssm"), 0.25, None, ALU.mult))
            for part in (4, 5):
                ve_tail(ve, NB - 1, 1, part)
            ve.wait_ge(S("gelu_tanh"), 1)
            ve.scalar_tensor_tensor(out=yT, in0=g1, scalar=1.0, in1=yT, op0=ALU.add, op1=ALU.mult).then_inc(S("gelu_ready"), 1)
            for h in range(H):
                b = read(ve, f"s{h}")
                was_read(tt(Sp[:, h, :], b[:, 0:384], C("causal"), ALU.add), f"s{h}")
            for h in range(H):
                used(ve, f"s{h}")
            b = read(ve, "as")
            was_read(ve.tensor_copy(att[0:NS, 1024:1536], b[0:NS, :]), "as")
            blocks = (Sp[:, :, 0:P], Sp[:, :, P:3 * P])
            for i, s in enumerate(blocks):
                st.link(ve.tensor_reduce(pm[0][:, 8 * i:8 * i + 8], s, AX, ALU.max))
            for i, s in enumerate(blocks):
                ins = tt(s, s, bc(pm[0][:, 8 * i:8 * i + 8], 2, (i + 1) * P), ALU.subtract)
                if i == 0:
                    st.inc(ins)
            ins.then_inc(S("prompt_centred"), 1)
            for m in range(4):
                used(ve, f"g{m}")
            ve.wait_ge(S("gelu_ready"), 1)
            ve.scalar_tensor_tensor(out=yT, in0=g1, scalar=1.0, in1=yT, op0=ALU.add, op1=ALU.mult).then_inc(S("glu_out"), 1)
            ve.wait_ge(S("glu_out"), 1)
            tt(soT[:, :, 0:T], v3(yT, 4), bc(gain4, 2, T), ALU.mult).then_inc(S("so_ready"), 1)
            ve.wait_ge(S("prompt_exp_ready"), 1)
            for i, s in enumerate(blocks):
                st.link(ve.tensor_reduce(pm[1][:, 8 * i:8 * i + 8], s, AX, ALU.add))
            st.link(ve.reciprocal(pm[1], pm[1]))
            used(ve, "as")
            for i in range(2):
                b = read(ve, f"o{i}")
                was_read(tt(v3(att[:, i * 512:(i + 1) * 512], H), v3(b[:, :], H), bc(pm[1][:, 8 * i:8 * i + 8], 2, VD), ALU.mult), f"o{i}")
            used(ve, "o0")
            used(ve, "o1")
            st.link(ve.tensor_copy(pm[2][:, 0:1], pm[1][:, 0:1]))
            ve.tensor_copy(pm[2][:, 1:2], pm[2][:, 0:1]).then_inc(S("att_ready"), 3)

            def add_to_x(i, a):
                b = read(ve, f"w{i}{a}")
                o = x[:, i * D + 512 * (a % 2):i * D + 512 * (a % 2 + 1)]
                rs = (msS if a < 2 else msA)[:, i:i + 1]
                was_read(ve.scalar_tensor_tensor(out=o, in0=b[:, :], scalar=rs, in1=o, op0=ALU.mult, op1=ALU.add), f"w{i}{a}")

            used(ve, "ss")
            for i in range(TT):
                add_to_x(i, 0)
                add_to_x(i, 1)
            for i in range(TT):
                b = read(ve, f"at{i}")
                was_read(tt(attT[:, :, i * P:(i + 1) * P], v3(b[:, :], 4), bc(vcol("out_norm_attn"), 2, P), ALU.mult), f"at{i}")
            ve.wait_ge(S("rs_att_ready"), 1)
            ve.wait_ge(S("g2_loaded"), 16)

            def norm_2(i):
                ve.wait_ge(S("rs2_ready"), i + 1)
                ve.scalar_tensor_tensor(out=xs[:, i * D:(i + 1) * D], in0=x[:, i * D:(i + 1) * D], scalar=msH[:, i:i + 1],
                                        in1=g2row, op0=ALU.mult, op1=ALU.mult).then_inc(S("xs_ready"), 1)

            def normed_T_copy(i):
                b = read(ve, f"xt{2 * i}")
                was_read(ve.tensor_copy(xsT[:, 0:4, i * P:(i + 1) * P], v3(b[:, :], 4)), f"xt{2 * i}")

            for i in range(TT):
                used(ve, f"w{i}0")
                used(ve, f"w{i}1")
                add_to_x(i, 2)
                add_to_x(i, 3)
                used(ve, f"w{i}2")
                used(ve, f"w{i}3")
                ve.tensor_copy(pm[2][:, 2 + i:3 + i], pm[2][:, 0:1]).then_inc(S("h_ready"), 1)
                norm_2(i)
                if i:
                    normed_T_copy(i - 1)
            normed_T_copy(TT - 1)
            b = read(ve, "rt")
            lg = v3(lgt, TT)
            was_read(tt(lg, v3(b[:, 0:108], TT), bc(b_r[:, :], 1, TT), ALU.add), "rt")
            used(ve, "rt")

            def first_max(src, n, m, mask):
                st.link(ve.tensor_reduce(m, src, AX, ALU.max))
                eq = v3(one[:, 0:TT * n], TT)
                st.link(tt(eq, src, bc(m, 2, n), ALU.is_equal))
                prs = pairs[:, 0:TT * n * n].rearrange("p (i a b) -> p i a b", i=TT, a=n)
                early = C("early8" if n == 8 else "early4").rearrange("p (a b) -> p a b", a=n)
                st.link(tt(prs, bc(eq, 2, n), bc(early, 1, TT), ALU.mult))
                st.link(ve.tensor_reduce(work8[:, 0:TT * n], prs.rearrange("p i a b -> p (i a) b"), AX, ALU.add))
                st.link(ve.scalar_tensor_tensor(out=mask, in0=work8[:, 0:TT * n], scalar=0.0, in1=one[:, 0:TT * n],
                                                op0=ALU.is_equal, op1=ALU.mult))

            first_max(lg[:, :, 0:NG], NG, m4, mask4)
            st.inc(tt(v3(e4, TT), lg[:, :, 0:NG], bc(m4, 2, NG), ALU.subtract))
            grp = mask4.rearrange("p (i g) -> p i g", i=TT)
            t32 = one.rearrange("p (i g e) -> p i g e", i=TT, g=NG)
            st.link(tt(t32, lg[:, :, NG:].rearrange("p i (g e) -> p i g e", g=NG), bc(grp, 3, EG), ALU.mult))
            st.link(ve.tensor_reduce(v3(le8, TT), t32.rearrange("p i g e -> p i e g"), AX, ALU.add))
            first_max(v3(le8, TT), EG, m8[:, 0:3], mask8a)
            st.link(ve.scalar_tensor_tensor(out=le8, in0=mask8a, scalar=NEG, in1=le8, op0=ALU.mult, op1=ALU.add))
            first_max(v3(le8, TT), EG, m8[:, 3:6], mask8b)
            tt(w12[:, 0:3], m8[:, 3:6], m8[:, 0:3], ALU.subtract).then_inc(S("router_diffs"), 1)
            ve.wait_ge(S("router_exp"), 1)
            st.link(ve.tensor_reduce(psel, v3(e4, TT), AX, ALU.add))
            st.link(ve.tensor_scalar(tsum, w12[:, 0:3], 1.0, None, ALU.add))
            st.link(tt(psel, psel, tsum, ALU.mult))
            st.link(ve.reciprocal(psel, psel))
            st.link(tt(w12[:, 3:6], w12[:, 0:3], psel, ALU.mult))
            m8a, m8b = v3(mask8a, TT), v3(mask8b, TT)
            def spread(dst, src8):
                return tt(dst, bc(src8, 2, NG), bc(grp, 3, EG), ALU.mult)

            def four(ap):
                return ap.rearrange("p (i g e) -> p i g e", i=TT, g=NG)

            st.link(spread(four(first), m8a))
            st.link(spread(four(second), m8b))
            st.link(tt(routed, first, second, ALU.add))
            tt(v3(routed, TT), v3(routed, TT), bc(C("valid"), 2, NE), ALU.mult).then_inc(S("routed_ready"), 1)
            r4 = rows.rearrange("p (k i c) -> p k i c", k=2, i=TT)
            for k, gate in enumerate((psel, w12[:, 3:6])):
                st.link(ve.tensor_copy(r4[:, k, :, 0], C("tok")))
                st.link(ve.tensor_scalar(r4[:, k, :, 1], C("tok"), float(k * T), None, ALU.add))
                st.link(ve.tensor_copy(r4[:, k, :, 2], gate))
                st.link(ve.tensor_copy(r4[:, k, :, 3], C("tok")))
            b = read(ve, "cum")
            st.link(ve.scalar_tensor_tensor(out=v3(where, TT), in0=v3(b[:, 0:3 * NE], TT), scalar=float(NE),
                                            in1=bc(C("ramp"), 1, TT), op0=ALU.mult, op1=ALU.add))
            for k, mask in enumerate((first, second)):
                st.link(tt(prod, where, mask, ALU.mult))
                st.link(ve.tensor_reduce(tgt[:, 3 * k:3 * k + 3], v3(prod, TT), AX, ALU.add))
            tt(v3(tgi[:, :], 2), v3(tgt, 2), bc(C("beyond"), 1, 2), ALU.add).then_inc(S("list_rows_ready"), 1)
            st.link(ve.tensor_reduce(cnt, b[:, 3 * NE:4 * NE], AX, ALU.max))
            st.inc(ve.tensor_copy(most[:, :], cnt))
            was_read(ve.tensor_copy(pm[2][:, 6:7], cnt), "cum")
            used(ve, "cum")
            ve.tensor_copy(pm[2][:, 7:8], cnt).then_inc(S("counts_ready"), 1)

            def lists(r):
                need(ve, "gather_index", r * NE)
                need(ve, "scatter_index", r * NE)
                ve.wait_ge(S("lists_loaded"), r * 32 + 32)
                l3 = lst.rearrange("p (e c) -> p c e", c=4)
                ve.tensor_scalar(gall[:, :], l3[:, 0, :], 2.0, C("half"), ALU.mult, ALU.add)
                ve.tensor_scalar(sall[:, :], l3[:, 1, :], 2.0, C("half"), ALU.mult, ALU.add)
                ve.tensor_scalar(gates, l3[:, 2, :], 0.5, None, ALU.mult).then_inc(S("lists_ready"), 1)
                ve.wait_ge(S("lists_ready"), r + 1)

            def silu(r, e, s):
                G = r * NE + e
                ve.wait_ge(S("gate_tanh"), G + 1)
                ve.scalar_tensor_tensor(out=hmb, in0=thb, scalar=1.0, in1=ps[2 + s][:, 0:P], op0=ALU.add,
                                        op1=ALU.mult).then_inc(S("silu_steps"), 1)
                ve.wait_ge(S("silu_steps"), G + 1)
                need(ve, "h_T", G)
                ve.scalar_tensor_tensor(out=hS, in0=hmb, scalar=gates[:, bass.ds(e, 1)], in1=ps[2 + s][:, P:2 * P], op0=ALU.mult,
                                        op1=ALU.mult).then_inc(S("act_ready"), 1)

            def h_copy(r, e, s):
                G = r * NE + e
                ve.wait_ge(S("h_T"), G + 1)
                need(ve, "down_done", G)
                ve.tensor_copy(hTb, ps[4][:, 0:P]).then_inc(S("h_copied"), 1)

            def round_(r):
                lists(r)
                silu(r, 0, 0)
                h_copy(r, 0, 0)

                def two_experts(i):
                    silu(r, i * 2 + 1, 1)
                    h_copy(r, i * 2 + 1, 1)
                    silu(r, i * 2 + 2, 0)
                    h_copy(r, i * 2 + 2, 0)

                pairs_from(ve, (NE - 2) // 2, two_experts)
                silu(r, NE - 1, 1)
                h_copy(r, NE - 1, 1)

            round_(0)
            more_rounds(ve, round_)
            for i in range(TT):
                n = P if i < 2 else NS
                ve.wait_ge(S(f"rows{i}_back"), 32)
                h = x[0:n, i * D:(i + 1) * D]
                st.link(tt(h, h, R[0:n, i * D:(i + 1) * D], ALU.add))
                tt(h, h, R[0:n, 3072 + i * D:3072 + (i + 1) * D], ALU.add).then_inc(S("y_ready"), 1)

        block = ctx.enter_context(nc.Block())

        def v3(ap, a):
            return ap.rearrange("p (a b) -> p a b", a=a)

        @block.sync
        def _(sp):
            sp.dma_start(x[:, 0:D], I["x_prompt"][0, 0:P, :]).then_inc(S("x0_loaded"), 16)
            sp.dma_start(x[:, D:2 * D], I["x_prompt"][0, P:2 * P, :]).then_inc(S("x1_loaded"), 16)
            sp.dma_start(x[0:NS, 2 * D:3 * D], I["x_sample"].rearrange("b t d -> (b t) d")).then_inc(S("x2_loaded"), 16)
            sp.dma_start(cst[:, :], I["shape_constants"][:, 0:LASTING]).then_inc(S("constants_loaded"), 16)
            sp.dma_start(cst_early, I["shape_constants"][:, LASTING:]).then_inc(S("constants_loaded"), 16)
            with nc.allow_non_contiguous_dma(reason="small tables"):
                sp.dma_start(ldt[0:LT, :], I["ssm_log_dt"].rearrange("o (i e) -> (o i) e", e=2)).then_inc(S("log_dt_loaded"), 16)
                sp.dma_start(pgt[0:UP, :], I["page_table"].rearrange("b (h g) -> g (b h)", g=UP)).then_inc(S("pages_loaded"), 16)
            for name in ("norm1_g", "ssm_d", "ssm_b_glu", "q_norm_g", "out_norm_ssm", "out_norm_attn"):
                a, b = ROW[name]
                sp.dma_start(vrow[a:b, :], I[name].rearrange("o (r p) -> (o r) p", p=P)).then_inc(S("rows_loaded"), 16)
            for name in ("qk_norm_q", "qk_norm_k"):
                a, b = ROW[name]
                sp.dma_start(vrow[a:b, 0:QK], I[name]).then_inc(S("rows_loaded"), 16)
                sp.dma_start(vrow[a:b, QK:P], I[name][:, 0:P - QK]).then_inc(S("rows_loaded"), 16)
            for name in ("ssm_a_re", "ssm_a_im"):
                a, b = ROW[name]
                sp.dma_start(vrow[a:b, :], I[name].rearrange("o (i e) p -> (o i) (e p)", e=2)).then_inc(S("rows_loaded"), 16)
            for a, name in enumerate(("state_ssm_re", "state_ssm_im")):
                sp.dma_start(sraw[:, a * P:(a + 1) * P],
                             I[name].rearrange("o b (i e) p -> (o b i) (e p)", e=2)).then_inc(S("rows_loaded"), 16)
            for k0 in (0, 4):
                sp.dma_start(w_in[:, k0:k0 + 4, :],
                             I["w_in"][0, k0 * P:(k0 + 4) * P, :].rearrange("(k p) n -> p k n", p=P)).then_inc(S(f"w_in_loaded{k0 // 4}"), 16)
            with nc.allow_non_contiguous_dma(reason="64-byte rows of the input matrices"):
                for a, name in enumerate(("ssm_b_re", "ssm_b_im")):
                    sp.dma_start(braw[:, a], I[name].rearrange("o (i e) p c -> (o e p) i c", e=2)).then_inc(S("b_loaded"), 16)
                for a, name in enumerate(("ssm_c_re", "ssm_c_im")):
                    for e in range(2):
                        sp.dma_start(craw[:, a, :, e, :],
                                     I[name].rearrange("o (m g) c p -> (o g c) m p", m=4)).then_inc(S("c_loaded"), 16)
            sp.dma_start(g_row[:, 0:KR], I["kv_norm_g"].to_broadcast([P, KR])).then_inc(S("gains_loaded"), 16)
            sp.dma_start(g_row[:, KR:KR + QK], I["qk_norm_q"].to_broadcast([P, QK])).then_inc(S("gains_loaded"), 16)
            sp.dma_start(g_row[:, KR + QK:], I["qk_norm_k"].to_broadcast([P, QK])).then_inc(S("gains_loaded"), 16)
            sp.dma_start(w_uq[:, :, :], I["w_uq"][0].rearrange("(k p) h d -> p k (h d)", p=P)).then_inc(S("w_uq_loaded"), 16)
            sp.dma_start(w_uk[:, :], I["w_uk"][0].rearrange("r h d -> r (h d)")).then_inc(S("w_kv_loaded"), 16)
            sp.dma_start(w_uv[:, :], I["w_uv"][0].rearrange("r h d -> r (h d)")).then_inc(S("w_kv_loaded"), 16)
            sp.dma_start(lists_dram, I["empty_lists"]).then_inc(S("lists_emptied"), 16)
            sp.wait_ge(S("latents_ready"), 2)
            for i in range(2):
                sp.dma_start(O["ckv_p"][0, i], ckvn[:, i * KR:(i + 1) * KR]).then_inc(S("outputs_stored"), 16)
                sp.dma_start(O["kr_p"][0, i], krn[:, i * ROPE:(i + 1) * ROPE]).then_inc(S("outputs_stored"), 16)
            sp.dma_start(O["ckv_s"].rearrange("o b t r -> (o b t) r"), ckvn[0:NS, 2 * KR:]).then_inc(S("outputs_stored"), 16)
            sp.dma_start(O["kr_s"].rearrange("o b t r -> (o b t) r"), krn[0:NS, 2 * ROPE:]).then_inc(S("outputs_stored"), 16)
            used(sp, "qT7")
            used(sp, "kT7")
            used(sp, "qr")
            sp.dma_start(w_out, I["w_out"][0].rearrange("(k p) n -> p k n", p=P)).then_inc(S("w_out_loaded"), 16)
            post_sync(sp)

        @block.gpsimd
        def _(pool):
            pool.memset(x[64:P, 2 * D:3 * D], 0.0).then_inc(S("pads_set"), 1)
            pool.wait_ge(S("pads_set"), 1)
            pool.memset(R[:, 11520:12544], 0.0).then_inc(S("pads_set"), 1)
            for i in range(2):
                pool.wait_ge(S("pads_set"), 2 + i)
                pool.memset(Ssb[i][64:P, 1024:1088], NEG).then_inc(S("pads_set"), 1)
            pool.wait_ge(S("pads_set"), 4)
            pool.memset(soft[:, NS:P], 0.0).then_inc(S("pads_set"), 1)
            used(pool, "vec")
            pool.wait_ge(S("pads_set"), 5)
            pool.memset(vrow[NS:P, :], 0.0).then_inc(S("pads_set"), 1)
            pool.wait_ge(S("pads_set"), 6)
            pool.wait_ge(S("page_rows_ready"), 1)
            for u in range(4):
                gather_unit(pool, u, 0)
            pool_loop(pool)

        @block.tensor
        def _(pe):
            pe.wait_ge(S("constants_loaded"), 32)
            pe.wait_ge(S("rows_loaded"), 16 * 14)
            pe.wait_ge(S("log_dt_spread"), 1)
            b = fill(pe, "vec")
            pe.transpose(b[:, 0:NROW], vrow[0:NROW, :], ident[0:NROW, 0:NROW])
            pe.transpose(b[:, 128:256], sraw[:, 0:P], ident)
            filled(pe.transpose(b[:, 256:384], sraw[:, P:2 * P], ident), "vec")
            for i in range(TT):
                pe.wait_ge(S("xn_ready"), i + 1)
                for g in range(2):
                    b = fill(pe, f"xT{2 * i + g}")
                    for k in range(4):
                        c = i * D + (4 * g + k) * P
                        ins = pe.transpose(b[:, k * P:(k + 1) * P], xn[:, c:c + P], ident)
                    filled(ins, f"xT{2 * i + g}")
            pe.wait_ge(S("page_table_ready"), 1)
            b = fill(pe, "page")
            filled(pe.matmul(b[:, 0:16], C("pgsel", UP), pgf[0:UP, 0:16], start=True, stop=True), "page")
            for i in range(6):
                used(pe, f"xT{i}")
            for m in range(4):
                b = fill(pe, f"u{m}")
                for k in range(KD):
                    if m == 0 and k % 4 == 0:
                        pe.wait_ge(S(f"w_in_loaded{k // 4}"), 16)
                    ins = pe.matmul(b[:, 0:T], w_in[:, k, m * P:(m + 1) * P], nT[:, k, 0:T],
                                    start=(k == 0), stop=(k == KD - 1))
                filled(ins, f"u{m}")
            pe.wait_ge(S("c_loaded"), 64)
            for a in range(2):
                b = fill(pe, f"ct{a}")
                for m in range(4):
                    ins = pe.transpose(b[:, m * P:(m + 1) * P], craw[:, a, m].rearrange("p e s -> p (e s)"), ident)
                filled(ins, f"ct{a}")
            for i in range(TT):
                b = fill(pe, f"z{i}")
                for k in range(KD):
                    ins = pe.matmul(b[:, 0:ZW], nT[:, k, i * P:(i + 1) * P], w_in[:, k, SSM_W:DIN],
                                    start=(k == 0), stop=(k == KD - 1))
                filled(ins, f"z{i}")
            pe.wait_ge(S("b_spread"), 4)
            for a in range(2):
                b = fill(pe, f"bd{a}")
                for m in range(4):
                    ins = pe.transpose(b[:, m * P:(m + 1) * P],
                                       xst[:, a, 4 * m:4 * m + 4].rearrange("p i e c -> p (i e c)"), ident)
                filled(ins, f"bd{a}")
            used(pe, "bd0")
            used(pe, "bd1")
            used(pe, "u3")

            def input_products(m):
                for n, name in enumerate(bu_groups(m)):
                    bd = bd4[n % 2][:, n // 2]
                    b = fill(pe, name)
                    filled(pe.matmul(b[:, 0:T], bd[:, m * P:(m + 1) * P], uT[:, m * T:(m + 1) * T],
                                     start=True, stop=True), name)

            input_products(0)
            pe.wait_ge(S("cq_ready"), 3)
            for k in range(2):
                b = fill(pe, f"cq{k}")
                for i in range(TT):
                    ins = pe.transpose(b[:, i * P:(i + 1) * P], cqn[:, i, k * P:(k + 1) * P], ident)
                filled(ins, f"cq{k}")
            pe.wait_ge(S("latents_ready"), 2)
            b = fill(pe, "ckvT")
            for i in range(TT):
                ins = pe.transpose(b[:, i * P:(i + 1) * P], ckvn[:, i * KR:(i + 1) * KR], ident)
            filled(ins, "ckvT")
            for m in range(1, 4):
                input_products(m)
            used(pe, "cq0")
            used(pe, "cq1")
            pe.wait_ge(S("w_uq_loaded"), 16)
            for i in range(TT):
                for g, (lo, hi) in enumerate(((0, 512), (512, 768))):
                    b = fill(pe, f"q{i}{g}")
                    for k in range(2):
                        ins = pe.matmul(b[:, 0:hi - lo], cqT[:, k, i * P:(i + 1) * P], w_uq[:, k, lo:hi],
                                        start=(k == 0), stop=(k == 1))
                    filled(ins, f"q{i}{g}")
            pe.wait_ge(S("w_kv_loaded"), 32)
            used(pe, "ckvT")
            for i in range(TT):
                b = fill(pe, f"k{i}")
                filled(pe.matmul(b[:, :], ckvT[:, i * P:(i + 1) * P], w_uk[:, :], start=True, stop=True), f"k{i}")
            for i in range(2):
                b = fill(pe, f"v{i}")
                filled(pe.matmul(b[:, :], ckvT[:, i * P:(i + 1) * P], w_uv[:, :], start=True, stop=True), f"v{i}")
            for what, src, ready in (("qT", q, "q_ready"), ("kT", kk, "k_ready")):
                pe.wait_ge(S(ready), 1)
                for h in range(H):
                    b = fill(pe, f"{what}{h}")
                    for i in range(TT):
                        ins = pe.transpose(b[0:QK, i * P:(i + 1) * P], src[:, i, h, :], ident)
                    filled(ins, f"{what}{h}")
            for g in range(2):
                b = fill(pe, f"uk{g}")
                for h in range(4):
                    c = (4 * g + h) * NOPE
                    ins = pe.transpose(b[0:NOPE, h * P:(h + 1) * P], w_uk[:, c:c + NOPE], ident)
                filled(ins, f"uk{g}")
            b = fill(pe, "qr")
            pe.wait_ge(S("q_rope_spread"), 1)
            for h in range(H):
                ins = pe.transpose(b[:, h * NS:(h + 1) * NS], qr4[0:NS, h].rearrange("p e d -> p (e d)"), ident[0:NS, 0:NS])
            filled(ins, "qr")
            used(pe, "uk1")
            used(pe, "uk0")
            for h in range(H):
                used(pe, f"qT{h}")
                used(pe, f"kT{h}")
            b = fill(pe, "qa")
            for h in range(H):
                ins = pe.matmul(b[:, h * NS:(h + 1) * NS], w_ukT[0:NOPE, h, :], qT[0:NOPE, h, SEQ:T], start=True, stop=True)
            filled(ins, "qa")
            b = fill(pe, "sn")
            for h in range(H):
                ins = pe.matmul(b[0:NS, h * NS:(h + 1) * NS], kT[0:QK, h, SEQ:T], qT[0:QK, h, SEQ:T], start=True, stop=True)
            filled(ins, "sn")
            for i in range(8):
                pe.wait_ge(S(f"free{i}"), pre_uses[i])
            pe_loop(pe)

        @block.scalar
        def _(act):
            st = chain(act, "act_steps")

            def rsqrt(ap, scale=1.0):
                st.link(act.activation(ap, ap, ACT.Ln, bias=EPS, scale=scale))
                return act.activation(ap, ap, ACT.Exp, scale=-0.5)

            act.wait_ge(S("pads_set"), 1)
            for i in range(TT):
                act.wait_ge(S(f"x{i}_loaded"), 16)
                st.link(act.activation(junk, x[:, i * D:(i + 1) * D], ACT.Square, scale=1 / 32, accum_out=ms1[:, i:i + 1]))
            rsqrt(ms1).then_inc(S("rs1_ready"), 1)
            used(act, "vec")
            act.activation(p_dt, vcol("log_dt"), ACT.Exp).then_inc(S("pole_exps_ready"), 1)
            act.wait_ge(S("angles_ready"), 1)
            act.activation(p_mag, p_b, ACT.Exp).then_inc(S("pole_exps_ready"), 1)
            st.link(act.activation(p_ab, p_f, ACT.Abs))
            act.activation(p_sin, p_f, ACT.Sin, scale=TWO_PI).then_inc(S("trig0_ready"), 1)
            act.activation(p_cos, p_ab, ACT.Sin, scale=-TWO_PI, bias=math.pi / 2).then_inc(S("trig0_ready"), 1)
            for m in range(4):
                b = read(act, f"u{m}")
                was_read(act.activation(uT[:, m * T:(m + 1) * T], b[:, 0:T], ACT.Copy), f"u{m}")
            for i in range(TT):
                b = read(act, f"z{i}")
                was_read(act.activation(z[:, i, :], b[:, 0:ZW], ACT.Copy), f"z{i}")
                used(act, f"z{i}")
                st.inc(act.activation(junk[:, 0:QR], z[:, i, 0:QR], ACT.Square, scale=1 / 16, accum_out=ms2[:, i:i + 1]))
                st.inc(act.activation(junk[:, QR:QR + KR], z[:, i, QR:QR + KR], ACT.Square, scale=KR ** -0.5,
                                      accum_out=ms2[:, 3 + i:4 + i]))
                st.sync()
            rsqrt(ms2).then_inc(S("rs_latent_ready"), 1)
            for i in range(LT):
                b = read(act, f"bu{2 * i}")
                was_read(act.activation(bre[:, i * T:(i + 1) * T], b[:, 0:T], ACT.Copy), f"bu{2 * i}")
            for i in range(TT):
                for g, (lo, hi) in enumerate(((0, 512), (512, 768))):
                    b = read(act, f"q{i}{g}")
                    o = O1[:, i * 768 + lo:i * 768 + hi]
                    was_read(act.activation(o, b[:, 0:hi - lo], ACT.Copy), f"q{i}{g}")
            for i in range(TT):
                b = read(act, f"k{i}")
                was_read(act.activation(kk[:, i, :, 0:NOPE], v3(b[:, :], H), ACT.Copy), f"k{i}")
            for i in range(2):
                b = read(act, f"v{i}")
                was_read(act.activation(v[:, i * 512:(i + 1) * 512], b[:, :], ACT.Copy), f"v{i}")
            act.wait_ge(S("q_rotated"), 1)
            act.activation(QT[:, 0:2304], O1[:, 0:2304], ACT.Square, scale=QK ** -0.5).then_inc(S("qk_squared"), 1)
            act.wait_ge(S("k_filled"), 1)
            for i in range(TT):
                used(act, f"k{i}")
            act.activation(KT[:, 0:2304], O1[:, 2304:4608], ACT.Square, scale=QK ** -0.5).then_inc(S("qk_squared"), 1)
            act.wait_ge(S("qk_sums_ready"), 2)
            rsqrt(small[:, 16:64]).then_inc(S("rs_qk_ready"), 1)
            for h in range(H):
                b = read(act, f"kT{h}")
                was_read(act.activation(kT[0:QK, h, :], b[0:QK, 0:T], ACT.Copy), f"kT{h}")
            act_loop(act)

        @block.vector
        def _(ve):
            st = chain(ve, "dve_steps")
            ve.wait_ge(S("log_dt_loaded"), 16)
            ve.tensor_copy(v3(vrow[0:LT, :], 2), bc(ldt[0:LT, :], 2, SP)).then_inc(S("log_dt_spread"), 1)
            ve.wait_ge(S("pages_loaded"), 16)
            ve.tensor_copy(pgf[0:UP, 0:16], pgt[0:UP, :]).then_inc(S("page_table_ready"), 1)
            ve.wait_ge(S("rs1_ready"), 1)
            for i in range(TT):
                ve.tensor_scalar(xn[:, i * D:(i + 1) * D], x[:, i * D:(i + 1) * D], ms1[:, i:i + 1], None,
                                 ALU.mult).then_inc(S("xn_ready"), 1)
            b = read(ve, "vec")
            st.inc(ve.tensor_copy(st0[:, :], b[:, 128:384]))
            was_read(ve.tensor_copy(vec[:, :], b[:, 0:NROW]), "vec")
            used(ve, "vec")
            for i in range(6):
                b = read(ve, f"xT{i}")
                k0, t0 = 4 * (i % 2), (i // 2) * P
                was_read(ve.tensor_tensor(nT[:, k0:k0 + 4, t0:t0 + P], v3(b[:, :], 4),
                                          bc(vcol("norm1_g")[:, k0:k0 + 4], 2, P), ALU.mult), f"xT{i}")
            b = read(ve, "page")
            was_read(ve.tensor_scalar(page_all[:, :], b[:, 0:16], float(PAGE // RUN), C("pgrow"), ALU.mult, ALU.add), "page")
            used(ve, "page")
            ve.tensor_copy(page_idx[:, :], page_all[:, 0:4]).then_inc(S("page_rows_ready"), 1)
            ar, ai = vcol("ssm_a_re"), vcol("ssm_a_im")
            c1 = 6.28125
            ve.wait_ge(S("pole_exps_ready"), 1)
            st.inc(ve.tensor_tensor(p_ang, ai, p_dt, ALU.mult))
            st.link(ve.tensor_tensor(p_b, ar, p_dt, ALU.mult))
            st.link(ve.tensor_scalar(p_k, p_ang, 1 / (2 * math.pi), MAGIC, ALU.mult, ALU.add))
            st.link(ve.tensor_scalar(p_k, p_k, MAGIC, None, ALU.subtract))
            st.link(ve.scalar_tensor_tensor(out=p_th, in0=p_k, scalar=-c1, in1=p_ang, op0=ALU.mult, op1=ALU.add))
            st.link(ve.scalar_tensor_tensor(out=p_th, in0=p_k, scalar=-(2 * math.pi - c1), in1=p_th, op0=ALU.mult, op1=ALU.add))
            st.link(ve.tensor_scalar(p_f, p_th, 1 / (2 * math.pi), 0.5, ALU.mult, ALU.min))
            ve.tensor_scalar(p_f, p_f, -0.5, None, ALU.max).then_inc(S("angles_ready"), 1)
            ve.wait_ge(S("pole_exps_ready"), 2)
            ve.wait_ge(S("trig0_ready"), 2)
            ve.wait_ge(S("b_loaded"), 32)
            ve.wait_ge(S("pads_set"), 4)
            st.inc(ve.tensor_tensor(p_lr, p_mag, p_cos, ALU.mult))
            st.inc(ve.tensor_tensor(p_li, p_mag, p_sin, ALU.mult))
            st.inc(ve.tensor_tensor(p_a, ar, ar, ALU.mult))
            st.inc(ve.tensor_tensor(p_den, ai, ai, ALU.mult))
            st.sync()
            st.inc(ve.tensor_scalar(p_lr, p_lr, -1.0, None, ALU.add))
            st.link(ve.tensor_tensor(p_den, p_den, p_a, ALU.add))
            st.inc(ve.reciprocal(p_den, p_den))
            st.inc(ve.tensor_tensor(p_a, p_lr, ar, ALU.mult))
            st.inc(ve.tensor_tensor(p_b, p_li, ai, ALU.mult))
            st.inc(ve.tensor_tensor(p_k, p_li, ar, ALU.mult))
            st.inc(ve.tensor_tensor(p_th, p_lr, ai, ALU.mult))
            st.sync()
            st.inc(ve.tensor_tensor(p_cr, p_a, p_b, ALU.add))
            st.inc(ve.tensor_tensor(p_ci, p_k, p_th, ALU.subtract))
            st.sync()
            st.inc(ve.tensor_tensor(p_cr, p_cr, p_den, ALU.mult))
            st.inc(ve.tensor_tensor(p_ci, p_ci, p_den, ALU.mult))
            st.sync()
            t = [v3(rt[i][:, 0:256], LT) for i in range(4)]
            crb, cib = bc(p_cr, 2, CH), bc(p_ci, 2, CH)
            st.inc(ve.tensor_tensor(t[0], crb, braw[:, 0], ALU.mult))
            st.inc(ve.tensor_tensor(t[1], cib, braw[:, 1], ALU.mult))
            st.inc(ve.tensor_tensor(t[2], crb, braw[:, 1], ALU.mult))
            st.inc(ve.tensor_tensor(t[3], cib, braw[:, 0], ALU.mult))
            st.sync()
            for e in range(2):
                r = slice(64 * e, 64 * e + 64)
                ve.tensor_tensor(xst[r, 0, :, e, :], t[0][r], t[1][r], ALU.subtract).then_inc(S("b_spread"), 1)
                ve.tensor_tensor(xst[r, 1, :, e, :], t[2][r], t[3][r], ALU.add).then_inc(S("b_spread"), 1)
            for a in range(2):
                b = read(ve, f"bd{a}")
                for j in range(4):
                    ins = ve.tensor_scalar(bd4[a][:, j], b[:, :], C("quad")[:, j:j + 1], None, ALU.mult)
                was_read(ins, f"bd{a}")
            for a in range(2):
                s = v3(st0[:, a * P:(a + 1) * P], NB)
                st.inc(ve.tensor_tensor(s, s, bc(p_mag, 1, NB), ALU.mult))
            b = read(ve, "ct0")
            was_read(ve.tensor_tensor(v3(CT[:, 0:512], 4), v3(b[:, :], 4), bc(C("even"), 1, 4), ALU.mult), "ct0")
            b = read(ve, "ct1")
            was_read(ve.scalar_tensor_tensor(out=v3(CT[:, 512:1024], 4), in0=v3(b[:, :], 4), scalar=-1.0,
                                             in1=bc(C("even"), 1, 4), op0=ALU.mult, op1=ALU.mult), "ct1")

            def input_copies(first, last):
                for i in range(4 * first, 4 * last):
                    b = read(ve, f"bu{2 * i + 1}")
                    was_read(ve.tensor_copy(bim[:, i * T:(i + 1) * T], b[:, 0:T]), f"bu{2 * i + 1}")

            input_copies(0, 1)
            ve.wait_ge(S("rs_latent_ready"), 1)
            ve.wait_ge(S("gains_loaded"), 48)
            for i in range(TT):
                ve.tensor_scalar(cqn[:, i, :], z[:, i, 0:QR], ms2[:, i:i + 1], None, ALU.mult).then_inc(S("cq_ready"), 1)
            for i in range(TT):
                ins = ve.scalar_tensor_tensor(out=ckvn[:, i * KR:(i + 1) * KR], in0=z[:, i, QR:QR + KR],
                                              scalar=ms2[:, 3 + i:4 + i], in1=g_row[:, 0:KR], op0=ALU.mult, op1=ALU.mult)
                if i < 2:
                    st.inc(ins)
            ins.then_inc(S("latents_ready"), 1)
            cos3, sin3 = v3(C("cos"), TT), v3(C("sin"), TT)

            def rotate(x1, x2, cos, sin, t, out1, out2, sem):
                st.inc(ve.tensor_tensor(t[0], x1, cos, ALU.mult))
                st.inc(ve.tensor_tensor(t[1], x2, sin, ALU.mult))
                st.inc(ve.tensor_tensor(t[2], x1, sin, ALU.mult))
                st.inc(ve.tensor_tensor(t[3], x2, cos, ALU.mult))
                st.sync()
                st.inc(ve.tensor_tensor(out1, t[0], t[1], ALU.subtract))
                ve.tensor_tensor(out2, t[2], t[3], ALU.add).then_inc(sem, 1)

            kr3 = v3(krn[:, :], TT)
            zr = z[:, :, QR + KR:ZW]
            ve.wait_ge(S("b_spread"), 4)
            rotate(zr[:, :, 0:HR], zr[:, :, HR:ROPE], cos3, sin3, [v3(r[:, 0:TT * HR], TT) for r in rt],
                   kr3[:, :, 0:HR], kr3[:, :, HR:], S("latents_ready"))
            for o, gq, gk in ((g_row[:, KR:KR + QK], g_row[:, KR:KR + QK], g_row[:, KR + QK:]),
                              (vcol("qk_norm_q"), vcol("qk_norm_q"), vcol("qk_norm_k"))):
                st.link(ve.scalar_tensor_tensor(out=o, in0=gq, scalar=QK ** -0.5, in1=gk, op0=ALU.mult, op1=ALU.mult))
            for k in range(2):
                b = read(ve, f"cq{k}")
                was_read(ve.tensor_scalar(cqT[:, k, :], b[:, 0:TP], vcol("q_norm_g")[:, k:k + 1], None, ALU.mult), f"cq{k}")
            b = read(ve, "ckvT")
            was_read(ve.tensor_copy(ckvT[:, :], b[:, 0:TP]), "ckvT")
            input_copies(1, 4)
            for i in range(TT):
                used(ve, f"q{i}1")
            ve.wait_ge(S("latents_ready"), 2)
            t = [r.rearrange("p (i h d) -> p i h d", i=TT, h=H) for r in rt]
            rotate(q[:, :, :, NOPE:NOPE + HR], q[:, :, :, NOPE + HR:], bc(cos3, 2, H), bc(sin3, 2, H), t,
                   q[:, :, :, NOPE:NOPE + HR], q[:, :, :, NOPE + HR:], S("q_rotated"))
            ve.tensor_copy(kk[:, :, :, NOPE:], bc(kr3, 2, H)).then_inc(S("k_filled"), 1)
            ve.wait_ge(S("qk_squared"), 1)
            ve.tensor_reduce(msq, v3(QT[:, 0:2304], 24), AX, ALU.add).then_inc(S("qk_sums_ready"), 1)
            ve.wait_ge(S("qk_squared"), 2)
            ve.tensor_reduce(msk, v3(KT[:, 0:2304], 24), AX, ALU.add).then_inc(S("qk_sums_ready"), 1)
            ve.wait_ge(S("rs_qk_ready"), 1)
            qf, kf = v3(O1[:, 0:2304], 24), v3(O1[:, 2304:4608], 24)
            ve.tensor_tensor(qf, qf, bc(msq, 2, QK), ALU.mult).then_inc(S("q_ready"), 1)
            ve.wait_ge(S("q_ready"), 1)
            rope_gain = g_row[0:NS, KR + NOPE:KR + QK]
            for e in range(4):
                ins = ve.tensor_tensor(qr4[0:NS, :, e], q[0:NS, 2, :, NOPE:], bc(rope_gain, 1, H), ALU.mult)
            ins.then_inc(S("q_rope_spread"), 1)
            ve.tensor_tensor(kf, kf, bc(msk, 2, QK), ALU.mult).then_inc(S("k_ready"), 1)
            for h in range(H):
                b = read(ve, f"qT{h}")
                was_read(ve.tensor_scalar(qT[0:QK, h, :], b[0:QK, 0:T], vcol("qk_norm_q")[0:QK], None, ALU.mult), f"qT{h}")
            for g in range(2):
                b = read(ve, f"uk{g}")
                was_read(ve.tensor_copy(w_ukT[0:NOPE, 4 * g:4 * g + 4, :], v3(b[0:NOPE, :], 4)), f"uk{g}")
            for name, dst, rows in (("qr", qrp, P), ("qa", qa, P), ("sn", s_new, NS)):
                b = read(ve, name)
                o = dst[0:rows, :].rearrange("p (b h t) -> p h b t", b=NB, h=H)
                was_read(ve.tensor_copy(o, b[0:rows, :].rearrange("p (h b t) -> p h b t", h=H, b=NB)), name)
            ve_loop(ve)


_INS = ["x_prompt", "x_sample", "cache_ckv", "cache_krope", "state_ssm_re", "state_ssm_im", "page_table", "norm1_g",
        "w_in", "ssm_a_re", "ssm_a_im", "ssm_log_dt", "ssm_b_re", "ssm_b_im", "ssm_c_re", "ssm_c_im", "ssm_d",
        "ssm_w_glu", "ssm_b_glu", "q_norm_g", "w_uq", "kv_norm_g", "w_uk", "w_uv", "qk_norm_q", "qk_norm_k",
        "out_norm_ssm", "out_norm_attn", "w_out", "norm2_g", "w_router_group", "b_router_group", "w_router_expert",
        "b_router_expert", "w_gate", "w_up", "w_down"]
_OUTS = [("y_p", (1, SEQ, D)), ("y_s", (NB, NQ, D)), ("ckv_p", (1, 1, SEQ // PAGE, PAGE, KR)),
         ("kr_p", (1, 1, SEQ // PAGE, PAGE, ROPE)), ("re_p", (1, 1, GROUPS, SP)), ("im_p", (1, 1, GROUPS, SP)),
         ("ckv_s", (1, NB, NQ, KR)), ("kr_s", (1, NB, NQ, ROPE)), ("re_s", (1, NB, GROUPS, SP)), ("im_s", (1, NB, GROUPS, SP))]


def program_outputs(O):
    views = dict(O)
    for name in ("ckv_p", "kr_p"):
        views[name] = O[name][0]
    for name in ("re_p", "im_p"):
        views[name] = O[name][0]
    return views


def kernel(**inputs):
    import numpy as _np
    import concourse.bacc as _bacc
    from concourse import mybir as _mybir
    from concourse.bass_utils import run_bass_kernel_spmd as _run

    nc = _bacc.Bacc("TRN2", target_bir_lowering=False, num_devices=1)
    arrays, I, O = {}, {}, {}
    for name in _INS:
        a = _np.ascontiguousarray(inputs[name])
        arrays[f"in_{name}"] = a
        I[name] = nc.dram_tensor(f"in_{name}", a.shape, _mybir.dt.from_np(a.dtype), kind="ExternalInput").ap()
    a = shape_constants()
    arrays["in_shape_constants"] = a
    I["shape_constants"] = nc.dram_tensor("in_shape_constants", a.shape, _mybir.dt.from_np(a.dtype), kind="ExternalInput").ap()
    a = empty_lists()
    arrays["in_empty_lists"] = a
    I["empty_lists"] = nc.dram_tensor("in_empty_lists", a.shape, _mybir.dt.from_np(a.dtype), kind="ExternalInput").ap()
    for name, shape in _OUTS:
        O[name] = nc.dram_tensor(f"out_{name}", shape, F32, kind="ExternalOutput").ap()
    build_program(nc, I, program_outputs(O))
    r = _run(nc, [arrays], core_ids=[0])
    return tuple(r.results[0][f"out_{name}"] for name, _ in _OUTS)
```

```python
import math
from contextlib import ExitStack

import numpy as np

import concourse.bass as bass
from concourse import mybir

ALU = mybir.AluOpType
ACT = mybir.ActivationFunctionType
AX = mybir.AxisListType.X
F32 = mybir.dt.float32
U32 = mybir.dt.uint32
I32 = mybir.dt.int32

P = 128
D = 1024
SEQ = 256
NB, NQ = 8, 8
NS = NB * NQ
T = SEQ + NS
TT = 3
TP = TT * P
KD = D // P
SSM_W, CH, GROUPS, SP = 512, 16, 32, 64
LT = GROUPS * SP // P
H, VD, NOPE, ROPE = 8, 64, 64, 32
HR = ROPE // 2
QK = NOPE + ROPE
QR, KR = 256, 128
ZW = QR + KR + ROPE
DIN = SSM_W + ZW
PAGE, NPG, POOL = 128, 16, 160
UP = 8
RUN = 8
NG, EG, NE, FE = 4, 8, 32, 256
EPS = 1e-6
NEG = -1e30
MAGIC = 1.5 * 2.0 ** 23
TWO_PI = 6.283185
SLOTS = 64
HD = D // 2
LN_EXP = "natural_log_exp_and_others"
ROUNDS = -(-T // SLOTS)
FAR = 65536.0

_COLS = [("ident", P), ("tri", P), ("ones", P), ("causal", 3 * P), ("smask", NS), ("ramp", NE),
         ("step", T), ("carry", T), ("tok", TT), ("valid", TT), ("beyond", TT), ("half", 1), ("early8", 64), ("early4", 16), ("quad", 4),
         ("cos", TT * HR), ("sin", TT * HR), ("pgsel", P), ("pgrow", 1), ("even", P)]
COL = {}
_at = 0
for _n, _w in _COLS:
    COL[_n] = (_at, _w)
    _at += _w
NCONST = _at
LASTING = COL["cos"][0]


def shape_constants():
    c = np.zeros((P, NCONST), np.float32)

    def col(name):
        a, w = COL[name]
        return c[:, a:a + w]

    p = np.arange(P)
    col("ident")[:] = np.eye(P)
    col("tri")[:] = p[:, None] < p[None, :]
    col("ones")[:] = 1.0
    col("causal")[:, 0:P] = col("causal")[:, 2 * P:] = np.where(p[None, :] <= p[:, None], 0.0, NEG)
    key_b, key_t = p // NQ, p % NQ
    for b in range(NB):
        for q in range(NQ):
            col("smask")[:, b * NQ + q] = np.where((key_b == b) & (key_t <= q), 0.0, NEG)
    col("ramp")[:] = np.arange(NE)[None, :]
    step = np.concatenate([np.arange(1, SEQ + 1), np.tile(np.arange(1, NQ + 1), NB)])
    col("step")[:] = step[None, :]
    col("carry")[:] = (step != 1)[None, :]
    inv = (np.float32(10000.0) ** (-np.arange(0, ROPE, 2, dtype=np.float32) / np.float32(ROPE))).astype(np.float32)
    pos = np.zeros((TT, P), np.float32)
    pos[0], pos[1] = np.arange(P), np.arange(P, 2 * P)
    pos[2, :NS] = NPG * PAGE + np.arange(NS) % NQ
    ang = (pos[:, :, None] * inv[None, None, :]).astype(np.float32).transpose(1, 0, 2).reshape(P, -1)
    col("cos")[:], col("sin")[:] = np.cos(ang), np.sin(ang)
    col("pgsel")[:UP] = (p[None, :] // (P // UP)) == np.arange(UP)[:, None]
    col("pgrow")[:, 0] = p % (PAGE // RUN)
    col("tok")[:] = p[:, None] + P * np.arange(TT)[None, :]
    col("valid")[:] = col("tok") < T
    col("beyond")[:] = np.where(col("tok") < T, 0.0, FAR)
    col("half")[:, 0] = p // SLOTS
    e = np.arange(8)
    col("early8")[:] = (e[None, :] < e[:, None]).reshape(1, 64)
    col("early4")[:] = (e[None, :4] < e[:4, None]).reshape(1, 16)
    col("even")[:] = (p[:, None] // SP) == ((p[None, :] // CH) % 2)
    col("quad")[:] = (p[:, None] // 32) == np.arange(4)[None, :]
    return c


def empty_lists():
    return np.full((ROUNDS * SLOTS * NE, 4), FAR, np.float32)


_ROWS = [("log_dt", 16), ("norm1_g", 8), ("ssm_d", 4), ("ssm_b_glu", 4), ("q_norm_g", 2), ("out_norm_ssm", 4),
         ("out_norm_attn", 4), ("ssm_a_re", 16), ("ssm_a_im", 16),
         ("qk_norm_q", 1), ("qk_norm_k", 1)]
ROW = {}
_at = 0
for _n, _w in _ROWS:
    ROW[_n] = (_at, _at + _w)
    _at += _w
NROW = _at


RING = 4
STEPS = 4


ROWS = 4


class Expert:

    def __init__(self, k, i=0):
        self.e = i * STEPS + k
        self.buf = k % 2
        self.rows, self.turn = k % ROWS, i * (STEPS // ROWS) + k // ROWS
        self.slot, self.lap = k % RING, i * (STEPS // RING) + k // RING
        if k == NE - 1:
            self.slot = RING

    def loaded(self, r, n):
        return n if self.slot == RING else (r * LAPS[self.slot] + self.lap + 1) * n


LAPS = [len(range(s, NE - 1, RING)) for s in range(RING)]


def experts(eng, first, count, step):
    whole = count // STEPS

    def steps(i):
        for k in range(first, first + STEPS):
            step(k, i)

    steps(0)
    with eng.Fori(1, whole) as i:
        steps(i)
    for k in range(first + STEPS * whole, first + count):
        step(k, 0)


class Chain:

    def __init__(self, eng, sem):
        self.eng, self.sem, self.n = eng, sem, 0

    def inc(self, ins):
        ins.then_inc(self.sem, 1)
        self.n += 1
        return ins

    def sync(self):
        self.eng.wait_ge(self.sem, self.n)

    def link(self, ins):
        self.inc(ins)
        self.sync()
        return ins


def build_program(nc, I, O):
    with ExitStack() as ctx:
        def sb(name, n, dt=F32):
            return ctx.enter_context(nc.sbuf_tensor(name, [P, n], dt))

        sems = {}

        def S(name):
            if name not in sems:
                sems[name] = ctx.enter_context(nc.semaphore(name))
            return sems[name]

        chains = {}

        def chain(eng, name):
            if name not in chains:
                chains[name] = Chain(eng, S(name))
            return chains[name]

        ps = [ctx.enter_context(nc.psum_tensor(f"bank{i}", [P, 512], F32)) for i in range(8)]

        xs_dram = nc.dram_tensor("normed_tokens", [T, D], F32).ap()
        lists_dram = nc.dram_tensor("slot_lists", [ROUNDS * SLOTS * NE, 4], F32).ap()
        y2_dram = nc.dram_tensor("expert_rows", [2 * T, D], F32).ap()

        cst = sb("constants", LASTING)

        def C(name, rows=P):
            a, w = COL[name]
            if a >= LASTING:
                return cst_early[0:rows, a - LASTING:a - LASTING + w]
            return cst[0:rows, a:a + w]

        x = sb("x", TT * D)
        R = sb("region_ssm_then_ring", 18432)
        O1 = sb("region_projection_then_w_out", 8192)
        cst_early = O1[:, 7392:7392 + NCONST - LASTING]
        ident = C("ident")
        QT = sb("region_qT", 3072)
        KT = sb("region_kT", 3072)
        CA = sb("region_cache_then_prompt", 5120)
        UQ = sb("region_w_uq", 1536)
        LP = sb("region_loop", 2560)
        uT = sb("uT", 4 * T)
        w_uk = sb("w_uk", H * NOPE)
        w_uv = sb("w_uv", H * VD)
        v = sb("v_prompt", 2 * 512)
        CT = sb("ssm_c_T", 1024)
        vrow = sb("vector_rows", P)
        vec = sb("vector_columns", NROW)
        ckvn = sb("ckv_normed", TT * KR)
        krn = sb("k_rope", TT * ROPE)
        ckvT = sb("ckv_new_T", TP)
        g_row = sb("gain_rows", KR + 2 * QK)
        par = sb("ssm_params", 16 * 16)
        small = sb("small", 160)
        st0 = QT[:, 2560:2816]
        n2 = QT[:, 2816:3072]
        soft = KT[:, 2560:2824]
        kr2 = KT[:, 2824:2832]
        w_r = uT[:, 0:KD * 36]
        b_r = uT[:, KD * 36:(KD + 1) * 36]
        pgf = sb("page_table_f", 2 * 16)
        pgt = sb("page_table_i", 16, I32)
        olat = vrow

        w_in = R[:, 0:KD * DIN].rearrange("p (k n) -> p k n", k=KD)
        bre, bim = R[:, 0:5120], R[:, 5120:10240]
        tmp = [R[:, 10240 + 640 * i:10240 + 640 * (i + 1)] for i in range(8)]
        Ssb = [R[:, 15360 + 1088 * i:15360 + 1088 * (i + 1)] for i in range(2)]
        xn = O1[:, 0:3072]
        nT = O1[:, 3072:6144].rearrange("p (k t) -> p k t", k=KD)
        z = O1[:, 6144:6144 + TT * ZW].rearrange("p (i n) -> p i n", i=TT)
        q = O1[:, 0:2304].rearrange("p (i h d) -> p i h d", i=TT, h=H)
        kk = O1[:, 2304:4608].rearrange("p (i h d) -> p i h d", i=TT, h=H)
        cqn = O1[:, 4608:4608 + TT * QR].rearrange("p (i n) -> p i n", i=TT)
        cqT = O1[:, 5376:5376 + 768].rearrange("p (k t) -> p k t", k=2)
        w_out = O1[:, 0:8192].rearrange("p (k n) -> p k n", k=8)
        qT = QT[:, 0:H * T].rearrange("p (h t) -> p h t", h=H)
        kT = KT[:, 0:H * T].rearrange("p (h t) -> p h t", h=H)
        w_uq = UQ[:, :].rearrange("p (k n) -> p k n", k=2)
        w_ukT = UQ[:, 0:1024].rearrange("p (h r) -> p h r", h=H)
        olT = UQ[:, 0:512]
        qa = UQ[:, 512:1024]
        s_new = UQ[:, 1024:1536]
        qrp = R[:, 17792:18304]
        bd4 = [r[:, 0:2048].rearrange("p (j c) -> p j c", j=4) for r in (QT, KT)]
        braw = LP[:, 1024:1536].rearrange("p (a i c) -> p a i c", a=2, i=LT)
        cT = [LP[:, 0:512], LP[:, 512:1024]]
        krT = [LP[:, 1024:1280], LP[:, 1280:1536]]
        sq = [LP[:, 1536:2048], LP[:, 2048:2560]]
        cache = [CA[:, 1280 * i:1280 * i + 1024] for i in range(4)]
        cachr = [CA[:, 1280 * i + 1024:1280 * (i + 1)] for i in range(4)]

        limits = {}

        def limit(pool, last_row, count):
            if isinstance(count, int):
                return last_row
            if last_row not in limits:
                limits[last_row] = pool.alloc_register(f"last_row_{last_row}")
            reg = limits[last_row]
            pool.reg_add(reg, count, last_row)
            pool.reg_alu(reg, reg, last_row, ALU.min)
            return reg

        def bc(ap, dim, n):
            shape = list(ap.shape)
            shape.insert(dim, n)
            return ap.unsqueeze(dim).to_broadcast(shape)

        def v3(ap, a):
            return ap.rearrange("p (a b) -> p a b", a=a)

        PER = dict(kr_transposed=2, kr_copied=2, c_transposed=4, c_copied=4, keys_made=16, squared=16,
                   summed=16, scored=16, sums_ready=2, rs_key=2, scaled=2, dve_seq=4, carried=1,
                   tail_dve=3, max_ready=1, max_T=1, diag_ready=1, max_row=1, centred=1, exp_done=1,
                   exp_summed=1, values_done=1, lat_scaled=1, lat_T=1, lat_copied=1,
                   turns=1, fractions=1, trig=1, rotated=1, scanned=1, products=1, states=1)

        def at(name, b, k):
            return b * PER[name] + k

        def need(eng, name, value):
            if not isinstance(value, int) or value > 0:
                eng.wait_ge(S(name), value)

        def wait(eng, name, b, k):
            need(eng, name, at(name, b, k))

        TB, KRB, SB, AB, MB = 2, 3, (4, 5), 6, 7
        smx, ssum = soft[:, 0:NS], soft[:, NS:2 * NS]
        sdiag = soft[0:NS, 2 * NS:3 * NS]
        m64, rl = soft[0:NS, 4 * NS:4 * NS + 1], soft[0:NS, 4 * NS + 1:4 * NS + 2]
        cache_rows = I["cache_ckv"][0].rearrange("n (r s) d -> (n r) (s d)", s=RUN)
        rope_rows = I["cache_krope"][0].rearrange("n (r s) d -> (n r) (s d)", s=RUN)
        far_row = POOL * (PAGE // RUN) - 1

        krsq = R[:, 17536:17792]

        def gather_unit(pool, slot, b):
            off = bass.IndirectOffsetOnAxis(ap=page_idx[:, slot:slot + 1], axis=0)
            last = limit(pool, far_row, b)
            pool.indirect_dma_start(out=cache[slot], out_offset=None, in_=cache_rows, in_offset=off,
                                    bounds_check=last, oob_is_err=False).then_inc(S(f"pages{slot}"), 16)
            pool.indirect_dma_start(out=cachr[slot], out_offset=None, in_=rope_rows, in_offset=off,
                                    bounds_check=last, oob_is_err=False).then_inc(S(f"pages{slot}"), 16)

        def seq_slices(b):
            return bass.ds(b * NS, NS), bass.ds(b * 2, 2), bass.ds(b * (2 * T), 2 * T)

        def two(ap):
            return v3(ap, 2)

        f_t, f_f, f_cos, f_sin, f_1, f_2, f_3, f_4 = tmp

        def pool_seq(pool, b, par, gather):
            _, til, sl = seq_slices(b)
            wait(pool, "trig", b, 1)
            pool.tensor_tensor(f_1, bre[:, sl], f_cos, ALU.mult)
            pool.tensor_tensor(f_2, bim[:, sl], f_sin, ALU.mult)
            pool.tensor_tensor(f_3, bim[:, sl], f_cos, ALU.mult)
            pool.tensor_tensor(f_4, bre[:, sl], f_sin, ALU.mult).then_inc(S("rotated"), 1)
            def gather_next(u):
                wait(pool, "values_done", b, 0)
                slot = 2 * (1 - par) + u
                pool.tensor_copy(page_idx[:, slot:slot + 1], page_all[:, bass.ds(b * 2 + (2 + u), 1)]).then_inc(S("index_copied"), 1)
                pool.wait_ge(S("index_copied"), b * 2 + (u - 1))
                gather_unit(pool, slot, b)

            if gather:
                gather_next(0)
            wait(pool, "scanned", b, 1)
            pool.tensor_tensor(f_1, f_2, f_cos, ALU.mult)
            pool.tensor_tensor(f_3, f_4, f_sin, ALU.mult)
            pool.tensor_tensor(f_t, f_2, f_sin, ALU.mult)
            pool.tensor_tensor(f_f, f_4, f_cos, ALU.mult).then_inc(S("products"), 1)
            if gather:
                gather_next(1)

        PE_TAIL = {2: 0, 6: 1, 10: 2, 15: 3}
        DVE_AT = {"states": -1, "tail": (-1, 1, 3, 6, 8, 12), "fractions": 0, "rope 0": 2, "copy rope": 4, "scan inputs": 7,
                  "scan 0": 9, "scan 1": 10, "scale": 12, "rope 1": 13}
        ACT_AT = {"turns": 0, "trig": 2, "latents 2": 3, "exp": 7, "latents 3": 7, "rsqrt": 9}

        def pe_seq(pe, b, half, par, t):
            sl, _, _ = seq_slices(b)

            def transposes(g):
                u, slot = g // 2, 2 * par + g // 2
                if g % 2 == 0:
                    pe.wait_ge(S(f"pages{slot}"), half * 32 + 32)
                    wait(pe, "kr_copied", b, u)
                    for j in range(2):
                        ins = pe.transpose(ps[KRB][:, j * P:(j + 1) * P], cachr[slot][:, j * P:(j + 1) * P], ident)
                    ins.then_inc(S("kr_transposed"), 1)
                wait(pe, "c_copied", b, g)
                for i in range(4):
                    c = (4 * (g % 2) + i) * P
                    ins = pe.transpose(ps[TB][:, i * P:(i + 1) * P], cache[slot][:, c:c + P], ident)
                ins.then_inc(S("c_transposed"), 1)

            def keys_scores(g):
                u = g // 2
                wait(pe, "c_copied", b, g + 1)
                if g % 2 == 0:
                    wait(pe, "kr_copied", b, u + 1)
                    wait(pe, "scaled", b, u - 1)
                for i in range(4):
                    n = 4 * g + i
                    wait(pe, "squared", b, n - 1)
                    lat = cT[g % 2][:, i * P:(i + 1) * P]
                    pe.matmul(ps[n % 2][:, :], lat, w_uk[:, :], start=True, stop=True).then_inc(S("keys_made"), 1)
                    o = ps[SB[u]][:, (n % 8) * NS:(n % 8 + 1) * NS]
                    pe.matmul(o, lat, qa[:, sl], start=True, stop=False)
                    pe.matmul(o, krT[u][:, (n % 8 // 4) * P:(n % 8 // 4 + 1) * P],
                              qrs[par][:, NS * i:NS * (i + 1)], start=False, stop=True).then_inc(S("scored"), 1)
                    if t is not None and n in PE_TAIL:
                        pe_tail(pe, t, 1 - par, PE_TAIL[n])

            transposes(0)
            transposes(1)
            keys_scores(0)
            transposes(2)
            keys_scores(1)
            transposes(3)
            keys_scores(2)
            keys_scores(3)

        def pe_tail(pe, t, par, part):
            if part == 0:
                wait(pe, "max_ready", t, 1)
                wait(pe, "lat_copied", t, 0)
                pe.transpose(ps[MB][:, 0:P], soft[:, 0:P], ident).then_inc(S("max_T"), 1)
            if part == 1:
                wait(pe, "diag_ready", t, 1)
                pe.matmul(ps[MB][:, 128:128 + NS], C("ones", NS), sdiag, start=True, stop=True).then_inc(S("max_row"), 1)
            if part == 2:
                wait(pe, "exp_done", t, 1)
                wait(pe, "lat_scaled", t, 0)
                for n in range(16):
                    slot, c = 2 * par + n // 8, (n % 8) * P
                    pe.matmul(ps[AB][0:NS, 0:KR], Ssb[par][:, n * NS:(n + 1) * NS], cache[slot][:, c:c + P],
                              start=(n == 0), stop=False)
                pe.matmul(ps[AB][0:NS, 0:KR], Ssb[par][:, 1024:1088], ckvn[:, 2 * KR:3 * KR], start=False, stop=True)
                wait(pe, "exp_summed", t, 1)
                pe.matmul(ps[AB][0:NS, KR:KR + 1], ssum, C("ones")[:, 0:1], start=True, stop=True).then_inc(S("values_done"), 1)
            if part == 3:
                wait(pe, "lat_scaled", t, 1)
                pe.transpose(ps[MB][:, 256:384], olat[:, :], ident).then_inc(S("lat_T"), 1)

        def act_seq_(act, b, par, t):
            def copy_latents(g):
                wait(act, "c_transposed", b, g + 1)
                wait(act, "scored", b, 4 * (g - 1))
                act.activation(cT[g % 2], ps[TB][:, :], ACT.Copy).then_inc(S("c_copied"), 1)

            def square(n):
                wait(act, "keys_made", b, n + 1)
                wait(act, "summed", b, n - 1)
                act.activation(sq[n % 2], ps[n % 2][:, :], ACT.Square, scale=QK ** -0.5).then_inc(S("squared"), 1)

            def key_rsqrt(s, u, parity):
                ap = n2[:, parity * P + u * 64:parity * P + (u + 1) * 64]
                wait(act, "sums_ready", s, u + 1)
                act.activation(ap, ap, ACT.Ln, bias=EPS).then_inc(S("act_rs"), 1)
                act.wait_ge(S("act_rs"), s * 2 + (u + 1))
                act.activation(ap, ap, ACT.Exp, scale=-0.5).then_inc(S("rs_key"), 1)

            def turns():
                wait(act, "states", b, 0)
                for i in range(2):
                    ins = act.activation(f_t[:, i * T:(i + 1) * T], C("step"), ACT.Copy, scale=p_f[:, bass.ds(b * 2 + i, 1)])
                ins.then_inc(S("turns"), 1)

            def trig():
                wait(act, "fractions", b, 1)
                act.activation(f_1, f_f, ACT.Abs).then_inc(S("act_trig"), 1)
                act.activation(f_sin, f_f, ACT.Sin, scale=TWO_PI)
                act.wait_ge(S("act_trig"), b + 1)
                act.activation(f_cos, f_1, ACT.Sin, scale=-TWO_PI, bias=math.pi / 2).then_inc(S("trig"), 1)
                act.preload_act_table_set(LN_EXP)
                for i in range(2):
                    ins = act.activation(f_t[:, i * T:(i + 1) * T], C("carry"), ACT.Copy, scale=p_mag[:, bass.ds(b * 2 + i, 1)])
                ins.then_inc(S("carried"), 1)

            copy_latents(0)
            if t is not None:
                key_rsqrt(t, 1, 1 - par)
            copy_latents(1)
            for n in range(16):
                square(n)
                if n == ACT_AT["turns"]:
                    turns()
                if n == ACT_AT["trig"]:
                    trig()
                if n == ACT_AT["latents 2"]:
                    copy_latents(2)
                if n == ACT_AT["latents 3"]:
                    copy_latents(3)
                if n == ACT_AT["exp"] and t is not None:
                    act_tail(act, t, 1 - par)
                if n == ACT_AT["rsqrt"]:
                    key_rsqrt(b, 0, par)
            if t is not None:
                act_olat(act, t)

        def act_tail(act, t, par):
            wait(act, "centred", t, 1)
            act.activation(Ssb[par], Ssb[par], ACT.Exp).then_inc(S("exp_done"), 1)

        def act_olat(act, t):
            wait(act, "lat_T", t, 1)
            o = olT.rearrange("p (h b q) -> p h b q", h=H, b=NB)[:, :, bass.ds(t, 1), :]
            act.activation(o, ps[MB][:, 256:256 + NS].rearrange("p (h o q) -> p h o q", h=H, o=1), ACT.Copy).then_inc(S("lat_copied"), 1)

        def scale_scores(ve, s, u, par):
            wait(ve, "rs_key", s, u + 1)
            wait(ve, "scored", s, 8 * (u + 1))
            rs = n2[:, par * P + u * 64:par * P + (u + 1) * 64]
            ve.tensor_tensor(v3(Ssb[par][:, u * 512:(u + 1) * 512], 64), v3(ps[SB[u]][:, :], 64), bc(rs, 2, NQ),
                             ALU.mult).then_inc(S("scaled"), 1)

        def ve_tail(ve, t, par, part):
            s64 = Ssb[par][0:NS, 1024:1088]
            if part == 0:
                scale_scores(ve, t, 1, par)
                ve.tensor_tensor(v3(s64, H), v3(s_new[0:NS, bass.ds(t * NS, NS)], H),
                                 bc(C("smask", NS)[:, bass.ds(t * NQ, NQ)], 1, H), ALU.add).then_inc(S("tail_dve"), 1)
            if part == 1:
                ve.wait_ge(S("tail_dve"), t * 3 + 1)
                wait(ve, "scaled", t, 2)
                ve.tensor_reduce(smx, Ssb[par].rearrange("p (n j) -> p j n", j=NS), AX, ALU.max).then_inc(S("max_ready"), 1)
            if part == 2:
                wait(ve, "max_T", t, 1)
                ve.tensor_reduce(m64, ps[MB][0:NS, 0:P], AX, ALU.max).then_inc(S("tail_dve"), 1)
                ve.wait_ge(S("tail_dve"), t * 3 + 2)
                ve.tensor_scalar(sdiag, ident[0:NS, 0:NS], m64, None, ALU.mult).then_inc(S("diag_ready"), 1)
            if part == 3:
                wait(ve, "max_row", t, 1)
                s = v3(Ssb[par], 17)
                ve.tensor_tensor(s, s, bc(ps[MB][:, 128:128 + NS], 1, 17), ALU.subtract).then_inc(S("centred"), 1)
            if part == 4:
                wait(ve, "exp_done", t, 1)
                ve.tensor_reduce(ssum, Ssb[par].rearrange("p (n j) -> p j n", j=NS), AX, ALU.add).then_inc(S("exp_summed"), 1)
            if part == 5:
                wait(ve, "values_done", t, 1)
                ve.reciprocal(rl, ps[AB][0:NS, KR:KR + 1]).then_inc(S("tail_dve"), 1)
                ve.wait_ge(S("tail_dve"), t * 3 + 3)
                wait(ve, "lat_T", t, 0)
                ve.tensor_scalar(olat[0:NS, :], ps[AB][0:NS, 0:KR], rl, None, ALU.mult).then_inc(S("lat_scaled"), 1)

        def ve_seq(ve, b, half, par, t):
            sl, til, tsl = seq_slices(b)

            def copy_rope(u):
                wait(ve, "kr_transposed", b, u + 1)
                wait(ve, "scored", b, 8 * (u - 1))
                ve.tensor_copy(krT[u], ps[KRB][:, 0:256]).then_inc(S("kr_copied"), 1)

            def rope_squares(u):
                slot = 2 * par + u
                ve.scalar_tensor_tensor(out=krsq, in0=cachr[slot], scalar=1 / QK, in1=cachr[slot], op0=ALU.mult,
                                        op1=ALU.mult).then_inc(S("dve_seq"), 1)
                ve.wait_ge(S("dve_seq"), b * 4 + (2 * u + 1))
                ve.tensor_reduce(kr2[:, :], v3(krsq, 8), AX, ALU.add).then_inc(S("dve_seq"), 1)

            def add_rope(u):
                ap = v3(n2[:, par * P + u * 64:par * P + (u + 1) * 64], 8)
                ve.wait_ge(S("dve_seq"), b * 4 + (2 * u + 2))
                wait(ve, "summed", b, 8 * (u + 1))
                ve.tensor_tensor(ap, ap, bc(kr2[:, :], 2, H), ALU.add).then_inc(S("sums_ready"), 1)

            def fractions():
                wait(ve, "turns", b, 1)
                ve.tensor_scalar(f_2, f_t, MAGIC, MAGIC, ALU.add, ALU.subtract).then_inc(S("dve_f"), 1)
                ve.wait_ge(S("dve_f"), b + 1)
                ve.tensor_tensor(f_f, f_t, f_2, ALU.subtract).then_inc(S("fractions"), 1)

            def scan_inputs():
                wait(ve, "rotated", b, 1)
                ve.tensor_tensor(f_1, f_1, f_2, ALU.add).then_inc(S("dve_ssm"), 1)
                ve.tensor_tensor(f_3, f_3, f_4, ALU.subtract).then_inc(S("dve_ssm"), 1)
                ve.wait_ge(S("dve_ssm"), b * 5 + 2)
                for a, f in ((0, f_1), (1, f_3)):
                    start = two(f)[:, :, SEQ:T].rearrange("p i (b q) -> p i b q", b=NB)[:, :, :, 0]
                    h0 = st0[:, a * P:(a + 1) * P].rearrange("p (b i) -> p i b", b=NB)[:, til, :]
                    ve.tensor_tensor(start, start, h0, ALU.add).then_inc(S("dve_ssm"), 1)

            def scan(a):
                if a == 0:
                    wait(ve, "carried", b, 1)
                    ve.wait_ge(S("dve_ssm"), b * 5 + 4)
                    ve.tensor_tensor_scan(f_2, f_t, f_1, 0.0, ALU.mult, ALU.add).then_inc(S("dve_ssm"), 1)
                else:
                    ve.tensor_tensor_scan(f_4, f_t, f_3, 0.0, ALU.mult, ALU.add).then_inc(S("scanned"), 1)

            wait(ve, "scored", b, -16)
            ve.tensor_tensor(qrs[par].rearrange("p (s j) -> p s j", s=4), bc(qrp[:, sl], 1, 4), bc(C("quad"), 2, NS), ALU.mult)
            copy_rope(0)
            def add_side(n, step):
                side.setdefault(n, []).append(step)

            side = {}
            if t is not None:
                add_side(DVE_AT["states"], lambda: ve_states(ve, t))
                for part in range(6):
                    add_side(DVE_AT["tail"][part], lambda part=part: ve_tail(ve, t, 1 - par, part))
            add_side(DVE_AT["fractions"], fractions)
            add_side(DVE_AT["rope 0"], lambda: rope_squares(0))
            add_side(DVE_AT["copy rope"], lambda: copy_rope(1))
            add_side(7, lambda: add_rope(0))
            add_side(DVE_AT["scan inputs"], scan_inputs)
            add_side(DVE_AT["scan 0"], lambda: scan(0))
            add_side(DVE_AT["scan 1"], lambda: scan(1))
            add_side(DVE_AT["scale"], lambda: scale_scores(ve, b, 0, par))
            add_side(DVE_AT["rope 1"], lambda: rope_squares(1))
            add_side(15, lambda: add_rope(1))
            for step in side.get(-1, []):
                step()
            for n in range(16):
                wait(ve, "squared", b, n + 1)
                ve.tensor_reduce(n2[:, par * P + n * H:par * P + (n + 1) * H], v3(sq[n % 2], H), AX, ALU.add).then_inc(S("summed"), 1)
                for step in side.get(n, []):
                    step()

        def ve_states(ve, b):
            tsl = seq_slices(b)[2]
            wait(ve, "products", b, 1)
            ve.tensor_tensor(bre[:, tsl], f_1, f_3, ALU.subtract)
            ve.tensor_tensor(bim[:, tsl], f_t, f_f, ALU.add).then_inc(S("states"), 1)

        def pairs_from(eng, n, body):
            body(0)
            with eng.Fori(1, n) as i:
                body(i)

        def rounds(eng, seq):
            seq(0, 0, 0, None)

            def two_sequences(i):
                seq(i * 2 + 1, i, 1, i * 2)
                seq(i * 2 + 2, i + 1, 0, i * 2 + 1)

            pairs_from(eng, (NB - 2) // 2, two_sequences)
            seq(NB - 1, NB // 2 - 1, 1, NB - 2)

        def pool_loop(pool):
            pool.wait_ge(S("pole_exps_ready"), 2)
            used(pool, "bu30")
            used(pool, "bu31")
            used(pool, "qr")
            rounds(pool, lambda b, half, par, t: pool_seq(pool, b, par, t is not None and not (isinstance(b, int) and b == NB - 1)))
            post_pool(pool)

        def pe_loop(pe):
            rounds(pe, lambda b, half, par, t: pe_seq(pe, b, half, par, t))
            post_pe(pe)

        def act_loop(act):
            def seq(b, half, par, t):
                act_seq_(act, b, par, t)
            rounds(act, seq)
            ap = n2[:, P + 64:2 * P]
            wait(act, "sums_ready", NB - 1, 2)
            act.activation(ap, ap, ACT.Ln, bias=EPS).then_inc(S("act_rs"), 1)
            act.wait_ge(S("act_rs"), 2 * NB)
            act.activation(ap, ap, ACT.Exp, scale=-0.5).then_inc(S("rs_key"), 1)
            act_tail(act, NB - 1, 1)
            act_olat(act, NB - 1)
            post_act(act)

        def ve_loop(ve):
            for name in ("qr", "qa", "sn"):
                used(ve, name)
            rounds(ve, lambda b, half, par, t: ve_seq(ve, b, half, par, t))
            ve_states(ve, NB - 1)
            for part in range(4):
                ve_tail(ve, NB - 1, 1, part)
            post_ve(ve)
        qrs = [ckvT[:, 0:256], g_row[:, 0:256]]
        page_idx = sb("page_row_index", 4, U32)
        page_all = sb("page_row_indices", 2 * NB, U32)
        sraw = R[:, 10240:10496]
        craw = R[:, 10496:11520].rearrange("p (a m e s) -> p a m e s", a=2, m=4, e=2)
        xst = R[:, 11520:12544].rearrange("p (a i e c) -> p a i e c", a=2, i=LT, e=2)
        junk = R[:, 14080:15104]
        rt = [R[:, 12544 + 384 * i:12544 + 384 * (i + 1)] for i in range(4)]
        qr4 = R[:, 14080:15104].rearrange("p (h e d) -> p h e d", h=H, e=4)
        ldt = small[:, 0:2]
        ms1, ms2, msq, msk = small[:, 2:5], small[:, 5:11], small[:, 16:40], small[:, 40:64]
        msA, msS, msH = small[:, 64:67], small[:, 67:70], small[:, 70:73]

        def prm(k):
            return par[:, 16 * k:16 * k + 16]

        (p_dt, p_mag, p_ang, p_k, p_th, p_f, p_sin, p_cos, p_lr, p_li, p_den, p_cr, p_ci, p_a, p_b,
         p_ab) = [prm(k) for k in range(16)]

        def vcol(name):
            a, b = ROW[name]
            return vec[:, a:b]

        order = [("vec", 6), ("xT0", 0), ("xT1", 1), ("xT2", 2), ("xT3", 3), ("xT4", 4), ("xT5", 5),
                 ("page", 7), ("u0", 0), ("u1", 1), ("u2", 2), ("u3", 3), ("ct0", 6), ("ct1", 7),
                 ("z0", 4), ("z1", 5), ("z2", 0), ("bd0", 1), ("bd1", 2)]

        def bu_groups(m):
            return [f"bu{2 * (4 * m + j) + a}" for j in range(4) for a in range(2)]

        order += [(name, n) for n, name in enumerate(bu_groups(0))]
        order += [("cq0", 2), ("cq1", 3), ("ckvT", 4)]
        order += [(name, n) for m in range(1, 4) for n, name in enumerate(bu_groups(m))]
        order += [("q00", 5), ("q01", 6), ("q10", 7), ("q11", 0), ("q20", 1), ("q21", 2),
                  ("k0", 3), ("k1", 4), ("k2", 5), ("v0", 6), ("v1", 7)]
        order += [(f"qT{h}", h) for h in range(8)] + [(f"kT{h}", h) for h in range(8)]
        order += [("uk0", 0), ("uk1", 1), ("qr", 2), ("qa", 3), ("sn", 4)]
        nth, uses = {}, [0] * 8
        for name, b in order:
            nth[name] = (b, uses[b])
            uses[b] += 1
        pre_uses = list(uses)

        def fill(eng, name):
            b, n = nth[name]
            if n:
                eng.wait_ge(S(f"free{b}"), n)
            return ps[b]

        def filled(ins, name):
            ins.then_inc(S(f"full{nth[name][0]}"), 1)

        def read(eng, name):
            b, n = nth[name]
            eng.wait_ge(S(f"full{b}"), n + 1)
            return ps[b]

        def was_read(ins, name):
            return ins.then_inc(S(f"free{nth[name][0]}"), 1)

        def used(eng, name):
            b, n = nth[name]
            eng.wait_ge(S(f"free{b}"), n + 1)

        w_glu = LP[:, 0:2048].rearrange("p (k n) -> p k n", k=4)
        hstates = LP[:, 2048:2560]
        hlast = tmp[0][:, 0:2 * P]
        yT, g1 = R[:, 12288:13568], R[:, 13568:14848]
        soT = R[:, 16128:17664].rearrange("p (m t) -> p m t", m=4)
        sqT = KT[:, 0:1536].rearrange("p (m t) -> p m t", m=4)
        junk_a, junk_h = KT[:, 1536:2048], CA[:, 4096:5120]
        Sp = CA[:, 0:3072].rearrange("p (h t) -> p h t", h=H)
        PT = [CA[:, 3072 + 384 * i:3072 + 384 * (i + 1)] for i in range(2)]
        g2row = UQ[:, 0:D]
        att = QT[:, 0:1536]
        attT = QT[:, 1536:3072].rearrange("p (k t) -> p k t", k=4)
        xs = KT
        xsT = O1[:, 0:3072].rearrange("p (k t) -> p k t", k=KD)
        pm = [small[:, 80 + 16 * i:96 + 16 * i] for i in range(4)]
        nbg = small[:, 144:148]
        gain4 = small[:, 152:156]
        post = [(f"y{m}", m) for m in range(4)] + [("hf0", 4), ("hf1", 5)]
        post += [(f"s{h}", (4, 5, 6, 7)[h % 4]) for h in range(H)] + [("as", 3)]
        post += [(f"g{m}", m) for m in range(4)]
        post += [("o0", 0), ("o1", 1)]
        post += [(f"p{h}", 6 + h % 2) for h in range(H)]
        post += [("ss", 2)]
        ssm_part = ["w00", "w01", "w10", "w11", "w20"]
        post += [(name, 3 + i % 3) for i, name in enumerate(ssm_part)]
        post += [("at0", 0), ("at1", 1), ("at2", 3)]
        post += [("w02", 4), ("w03", 5), ("w12", 6), ("w13", 7), ("xt0", 3), ("xt1", 5), ("rt", 2), ("w22", 0),
                 ("xt2", 4), ("xt3", 6), ("xt4", 7), ("xt5", 3), ("cum", 0)]
        for name, b in post:
            nth[name] = (b, uses[b])
            uses[b] += 1

        _off = [0]

        def rv(n):
            a = _off[0]
            _off[0] += n
            return QT[:, a:a + n]

        lgt, mask4, mask8a, mask8b = rv(108), rv(12), rv(24), rv(24)
        le8, work8, pairs, one = rv(24), rv(24), rv(192), rv(96)
        m4, m8, e4, w12, psel, tsum = rv(3), rv(6), rv(12), rv(6), rv(3), rv(3)
        first, second, routed, where, prod = rv(96), rv(96), rv(4 * NE), rv(96), rv(96)
        rows = rv(6 * 4)
        tgt, cnt, lst, gates = rv(6), rv(1), rv(4 * NE), rv(NE)
        assert _off[0] <= 3072
        gall, sall = sb("gather_rows", NE, U32), sb("scatter_rows", NE, U32)
        gsi, ssi = sb("gather_index_columns", ROWS, U32), sb("scatter_index_columns", ROWS, U32)
        tgi = sb("list_row_index", 6, U32)
        most = sb("most_tokens", 1, I32)
        gu_ring = [R[:, 6144 * i:6144 * i + 4096] for i in range(3)] + [CA[:, 0:4096], O1[:, 0:4096]]
        down_ring = [R[:, 6144 * i + 4096:6144 * (i + 1)] for i in range(3)] + [LP[:, 0:2048], KT[:, 0:2048]]
        Xg = [r[:, HD * i:HD * (i + 1)] for r in (O1[:, 4608:5632], CA[:, 4096:5120]) for i in range(2)]
        XgT = [O1[:, 5632 + HD * i:5632 + HD * (i + 1)] for i in range(2)]
        Yo = [r[:, HD * i:HD * (i + 1)] for r in (O1[:, 6656:7680], UQ[:, 0:D]) for i in range(2)]
        thb, hmb, hS, hTb = [O1[:, P * i + 4096:P * (i + 1) + 4096] for i in range(4)]
        xs_halves = xs_dram.rearrange("t (a d) -> (t a) d", a=2)
        y2_halves = y2_dram.rearrange("t (a d) -> (t a) d", a=2)
        outs_total = 6 + 4 + 3

        def load_expert(sp, r, k, i=0):
            ex = Expert(k, i)
            e, s = ex.e, ex.slot
            sl = bass.ds(e, 1)
            done = r * NE + (e - (RING - 1) if RING <= k < NE - 1 else 0)
            need(sp, "gate_up_done", done)
            for a, name in enumerate(("w_gate", "w_up")):
                sp.dma_start(gu_ring[s][:, 2048 * a:2048 * (a + 1)].rearrange("p (h x) -> p h x", h=2),
                             I[name][0][sl].rearrange("e (h p c) f -> (e p) h (c f)", h=2, c=4)).then_inc(S(f"gate_up_loaded{s}"), 16)
            need(sp, "down_done", done)
            sp.dma_start(down_ring[s].rearrange("p (j n) -> p j n", j=2),
                         I["w_down"][0][sl].rearrange("e (j p) n -> (e p) j n", j=2)).then_inc(S(f"down_loaded{s}"), 16)

        def more_rounds(eng, round_):
            eng.wait_ge(S("routing_ready"), 2)
            n = eng.value_load(most[0:1, 0:1], min_val=0, max_val=T)
            with eng.Fori(1, ROUNDS) as r:
                with eng.If(n > r * SLOTS):
                    round_(r)
                eng.nop()

        def post_sync(sp):
            wait(sp, "scored", NB - 1, 16)
            wait(sp, "summed", NB - 1, 16)
            sp.dma_start(w_glu, I["ssm_w_glu"][0].rearrange("(k p) n -> p k n", p=P)).then_inc(S("w_glu_loaded"), 16)
            used(sp, "as")
            sp.dma_start(g2row, I["norm2_g"].to_broadcast([P, D])).then_inc(S("route_inputs_loaded"), 16)
            with nc.allow_non_contiguous_dma(reason="router weights"):
                used(sp, "y3")
                sp.dma_start(w_r[:, :].rearrange("p (k n) -> p k n", k=KD)[:, :, 0:NG],
                             I["w_router_group"][0].rearrange("(k p) n -> p k n", p=P)).then_inc(S("route_inputs_loaded"), 16)
                sp.dma_start(w_r[:, :].rearrange("p (k n) -> p k n", k=KD)[:, :, NG:],
                             I["w_router_expert"][0].rearrange("(k p) n -> p k n", p=P)).then_inc(S("route_inputs_loaded"), 16)
                sp.dma_start(b_r[:, 0:NG], I["b_router_group"].to_broadcast([P, NG])).then_inc(S("route_inputs_loaded"), 16)
                sp.dma_start(b_r[:, NG:], I["b_router_expert"].to_broadcast([P, NE])).then_inc(S("route_inputs_loaded"), 16)
            used(sp, "hf0")
            used(sp, "hf1")
            for a, (pn, sn) in enumerate((("re_p", "re_s"), ("im_p", "im_s"))):
                sp.dma_start(O[pn].rearrange("o (i e) p -> (o i) (e p)", e=2), hstates[0:LT, 256 * a:256 * a + P]).then_inc(S("outputs_stored"), 16)
                sp.dma_start(O[sn].rearrange("o b (i e) p -> (o b i) (e p)", e=2), hstates[:, 256 * a + P:256 * (a + 1)]).then_inc(S("outputs_stored"), 16)
            load_expert(sp, 0, 0)
            load_expert(sp, 0, 1)
            used(sp, "w20")
            load_expert(sp, 0, 2)
            sp.wait_ge(S("att_ready"), 3)
            load_expert(sp, 0, 3)
            for i in range(TT):
                n = P if i < 2 else NS
                sp.wait_ge(S("xs_ready"), i + 1)
                sp.dma_start(xs_dram[i * P:i * P + n, :], xs[0:n, i * D:(i + 1) * D]).then_inc(S("xs_stored"), 16)

            used(sp, "rt")
            sp.wait_ge(S("xs_stored"), 16 * TT)
            load_expert(sp, 0, NE - 1)

            def load_lists(r):
                src = lists_dram.rearrange("(s e) c -> s (e c)", e=NE)[bass.ds(r * SLOTS, SLOTS)]
                for a in range(2):
                    sp.dma_start(lst[SLOTS * a:SLOTS * (a + 1), :], src).then_inc(S("lists_loaded"), 16)

            def round_(r):
                load_lists(r)
                experts(sp, RING, NE - 1 - RING, lambda k, i: load_expert(sp, r, k, i))

            sp.wait_ge(S("list_rows_written"), 16 * 6)
            round_(0)

            def later(r):
                for k in range(RING):
                    load_expert(sp, r, k)
                round_(r)

            more_rounds(sp, later)
            sp.wait_ge(S("pool_steps"), 3 + ROWS)
            for i in range(TT):
                n = P if i < 2 else NS
                for a in range(2):
                    sp.dma_start(R[0:n, 3072 * a + i * D:3072 * a + (i + 1) * D],
                                 y2_dram[a * T + i * P:a * T + i * P + n, :]).then_inc(S(f"rows{i}_back"), 16)
            for i in range(TT):
                sp.wait_ge(S("y_ready"), i + 1)
                if i < 2:
                    sp.dma_start(O["y_p"][0, i * P:(i + 1) * P, :], x[:, i * D:(i + 1) * D]).then_inc(S("outputs_stored"), 16)
                else:
                    sp.dma_start(O["y_s"].rearrange("b t d -> (b t) d"), x[0:NS, 2 * D:]).then_inc(S("outputs_stored"), 16)
            sp.wait_ge(S("outputs_stored"), 16 * outs_total)

        def post_pool(pool):
            wait(pool, "centred", NB - 1, 1)
            wait(pool, "values_done", NB - 1, 1)
            used(pool, "s7")
            pool.memset(sqT[:, :, T:TP], 0.0).then_inc(S("pool_steps"), 1)
            pool.wait_ge(S("pool_steps"), 1)
            pool.memset(att[NS:P, 1024:1536], 0.0).then_inc(S("pool_steps"), 1)
            pool.wait_ge(S("pool_steps"), 2)
            pool.wait_ge(S("xs_ready"), TT)
            for i in range(ROWS):
                pool.memset(Xg[i], 0.0).then_inc(S("pool_steps"), 1)
            pool.wait_ge(S("pool_steps"), 2 + ROWS)
            pool.wait_ge(S("xs_stored"), 16 * TT)

            column = pool.alloc_register("expert_column")

            def column_of(r, e):
                if not isinstance(e, int):
                    return bass.ds(e, 1)
                if isinstance(r, int):
                    return slice(e, e + 1)
                pool.reg_add(column, r, e)
                pool.reg_alu(column, column, e, ALU.min)
                return bass.ds(pool.snap(column, min_val=0, max_val=NE - 1), 1)

            pool.wait_ge(S("routing_ready"), 1)
            pool.wait_ge(S("lists_emptied"), 16)
            for n in range(6):
                pool.indirect_dma_start(out=lists_dram, out_offset=bass.IndirectOffsetOnAxis(ap=tgi[:, n:n + 1], axis=0),
                                        in_=rows[:, 4 * n:4 * n + 4], in_offset=None,
                                        bounds_check=ROUNDS * SLOTS * NE - 1, oob_is_err=False).then_inc(S("list_rows_written"), 16)

            AHEAD = ROWS + 1

            def gather(r, k, i=0):
                ex = Expert(k, i)
                e, s = ex.e, ex.rows
                need(pool, "x_T", r * NE + e - (ROWS - 1))
                pool.tensor_copy(gsi[:, s:s + 1], gall[:, column_of(r, e)]).then_inc(S("gather_index"), 1)
                pool.wait_ge(S("gather_index"), r * NE + e + 1)
                last = limit(pool, 2 * T - 1, r * NE + e)
                pool.indirect_dma_start(out=Xg[s], out_offset=None, in_=xs_halves,
                                        in_offset=bass.IndirectOffsetOnAxis(ap=gsi[:, s:s + 1], axis=0),
                                        bounds_check=last, oob_is_err=False).then_inc(S(f"tokens{s}"), 16)

            def scatter(r, k, i=0):
                ex = Expert(k, i)
                e, s = ex.e, ex.rows
                pool.wait_ge(S("y_copied"), r * NE + e + 1)
                need(pool, f"scattered{s}", (r * (NE // ROWS) + ex.turn) * 16)
                pool.tensor_copy(ssi[:, s:s + 1], sall[:, column_of(r, e)]).then_inc(S("scatter_index"), 1)
                pool.wait_ge(S("scatter_index"), r * NE + e + 1)
                last = limit(pool, 4 * T - 1, r * NE + e)
                pool.indirect_dma_start(out=y2_halves, out_offset=bass.IndirectOffsetOnAxis(ap=ssi[:, s:s + 1], axis=0),
                                        in_=Yo[s], in_offset=None, bounds_check=last, oob_is_err=False).then_inc(S(f"scattered{s}"), 16)

            def round_(r):
                pool.wait_ge(S("lists_ready"), r + 1)
                for k in range(AHEAD):
                    gather(r, k)

                def step(k, i):
                    gather(r, k + AHEAD, i)
                    scatter(r, k, i)

                experts(pool, 0, NE - AHEAD, step)
                for k in range(NE - AHEAD, NE):
                    scatter(r, k)
                for s in range(ROWS):
                    pool.wait_ge(S(f"scattered{s}"), (r + 1) * (16 * NE // ROWS))

            round_(0)
            more_rounds(pool, round_)
            pool.memset(small[0:1, 150:151], 0.0).then_inc(S("pool_steps"), 1)

        def post_pe(pe):
            wait(pe, "squared", NB - 1, 16)
            wait(pe, "c_copied", NB - 1, 4)
            wait(pe, "kr_copied", NB - 1, 2)
            wait(pe, "states", NB - 1, 1)
            for m in range(4):
                b = fill(pe, f"y{m}")
                for a, src in enumerate((bre, bim)):
                    for j in range(4):
                        i, c = 4 * m + j, 512 * a + m * P + 32 * j
                        ins = pe.matmul(b[32 * j:32 * j + 32, 0:T], CT[:, c:c + 32], src[:, i * T:(i + 1) * T],
                                        start=(a == 0), stop=(a == 1))
                filled(ins, f"y{m}")
                if m in (1, 2):
                    pe_tail(pe, NB - 1, 1, m - 1)
            pe_tail(pe, NB - 1, 1, 2)
            pe_tail(pe, NB - 1, 1, 3)
            wait(pe, "scaled", NB - 1, 2)
            for a, src in enumerate((bre, bim)):
                b = fill(pe, f"hf{a}")
                per_tile = v3(src, LT)
                pe.transpose(b[0:LT, 0:P], per_tile[:, :, SEQ - 1], ident)
                pe.wait_ge(S("last_states"), a + 1)
                filled(pe.transpose(b[:, P:2 * P], hlast[:, a * P:(a + 1) * P], ident), f"hf{a}")
            wait(pe, "lat_copied", NB - 1, 1)
            for h in range(H):
                b = fill(pe, f"s{h}")
                pe.matmul(b[:, 0:P], qT[0:QK, h, 0:P], kT[0:QK, h, 0:P], start=True, stop=True)
                filled(pe.matmul(b[:, P:3 * P], qT[0:QK, h, P:2 * P], kT[0:QK, h, 0:2 * P], start=True, stop=True), f"s{h}")
            b = fill(pe, "as")
            for h in range(H):
                ins = pe.matmul(b[0:NS, h * VD:(h + 1) * VD], olT[:, h * NS:(h + 1) * NS], w_uv[:, h * VD:(h + 1) * VD],
                                start=True, stop=True)
            filled(ins, "as")
            pe.wait_ge(S("gelu_ready"), 1)
            pe.wait_ge(S("w_glu_loaded"), 16)
            for m in range(4):
                b = fill(pe, f"g{m}")
                for k in range(4):
                    ins = pe.matmul(b[:, 0:T], w_glu[:, k, m * P:(m + 1) * P], yT[:, k * T:(k + 1) * T],
                                    start=(k == 0), stop=(k == 3))
                filled(ins, f"g{m}")
            o0, o1 = fill(pe, "o0"), fill(pe, "o1")

            def prompt_T(h):
                pe.wait_ge(S("prompt_exp_ready"), h // 4 + 1)
                b = fill(pe, f"p{h}")
                for j in range(3):
                    ins = pe.transpose(b[:, j * P:(j + 1) * P], Sp[:, h, j * P:(j + 1) * P], ident)
                filled(ins, f"p{h}")

            def out_proj(i, a):
                src, k0, n0 = (soT, 0, 512 * a) if a < 2 else (attT, 4, 512 * (a - 2))
                b = fill(pe, f"w{i}{a}")
                for k in range(4):
                    if i < 2:
                        ins = pe.matmul(b[:, :], src[:, k, i * P:(i + 1) * P], w_out[:, k0 + k, n0:n0 + 512],
                                        start=(k == 0), stop=(k == 3))
                    else:
                        for g in range(2):
                            ins = pe.matmul(b[g * NS:(g + 1) * NS, :], src[:, k, i * P:i * P + NS],
                                            w_out[:, k0 + k, 512 * g:512 * (g + 1)], start=(k == 0), stop=(k == 3))
                filled(ins, f"w{i}{a}")

            prompt_T(0)
            for h in range(H):
                if h + 1 < H:
                    prompt_T(h + 1)
                if h == 1:
                    pe.wait_ge(S("pool_steps"), 2)
                    pe.wait_ge(S("ssm_squared"), 1)
                    b = fill(pe, "ss")
                    for i in range(TT):
                        for m in range(4):
                            ins = pe.matmul(b[:, i:i + 1], sqT[:, m, i * P:(i + 1) * P], C("ones")[:, 0:1],
                                            start=(m == 0), stop=(m == 3))
                    filled(ins, "ss")
                    pe.wait_ge(S("w_out_loaded"), 16)
                    pe.wait_ge(S("so_ready"), 1)
                elif 2 <= h < 7:
                    out_proj(*divmod(h - 2, 2))
                used(pe, f"p{h}")
                pt, c = PT[h % 2], slice(h * VD, (h + 1) * VD)
                v0, v1 = v[:, h * VD:(h + 1) * VD], v[:, 512 + h * VD:512 + (h + 1) * VD]
                i0 = pe.matmul(o0[:, c], pt[:, 0:P], v0, start=True, stop=True)
                if h == H - 1:
                    filled(i0, "o0")
                pe.matmul(o1[:, c], pt[:, P:2 * P], v0, start=True, stop=False)
                i1 = pe.matmul(o1[:, c], pt[:, 2 * P:3 * P], v1, start=False, stop=True)
                if h == H - 1:
                    filled(i1, "o1")
                else:
                    i1.then_inc(S("prompt_values"), 1)
            pe.wait_ge(S("att_ready"), 3)
            for i in range(TT):
                b = fill(pe, f"at{i}")
                for k in range(4):
                    ins = pe.transpose(b[:, k * P:(k + 1) * P], att[:, i * 512 + k * P:i * 512 + (k + 1) * P], ident)
                filled(ins, f"at{i}")

            def normed_T(i):
                pe.wait_ge(S("xs_ready"), i + 1)
                for g in range(2):
                    b = fill(pe, f"xt{2 * i + g}")
                    for k in range(4):
                        c = i * D + (4 * g + k) * P
                        ins = pe.transpose(b[:, k * P:(k + 1) * P], xs[:, c:c + P], ident)
                    filled(ins, f"xt{2 * i + g}")

            wr = w_r[:, :].rearrange("p (k n) -> p k n", k=KD)

            def router(i, b):
                for g in range(2):
                    used(pe, f"xt{2 * i + g}")
                for k in range(KD):
                    ins = pe.matmul(b[:, i * 36:(i + 1) * 36], xsT[:, k, i * P:(i + 1) * P], wr[:, k, :],
                                    start=(k == 0), stop=(k == KD - 1))
                return ins

            for i in range(2):
                used(pe, f"at{i}")
                out_proj(i, 2)
                out_proj(i, 3)
            normed_T(0)
            used(pe, "at2")
            out_proj(2, 2)
            pe.wait_ge(S("route_inputs_loaded"), 80)
            rt = fill(pe, "rt")
            router(0, rt)
            normed_T(1)
            router(1, rt)
            normed_T(2)
            filled(router(2, rt), "rt")
            pe.wait_ge(S("routed_ready"), 1)
            b = fill(pe, "cum")
            pe.matmul(b[:, 0:4 * NE], C("tri"), routed, start=True, stop=False)
            for j in range(TT):
                ins = pe.matmul(b[:, (j + 1) * NE:4 * NE], C("ones"), routed[:, 0:(TT - j) * NE], start=False, stop=(j == TT - 1))
            filled(ins, "cum")
            for i in range(8):
                pe.wait_ge(S(f"free{i}"), uses[i])

            def xT(r, k, i=0):
                ex = Expert(k, i)
                e, s = ex.e, ex.buf
                pe.wait_ge(S(f"tokens{ex.rows}"), (r * (NE // ROWS) + ex.turn + 1) * 16)
                need(pe, "x_copied", r * NE + e - 1)
                view = Xg[ex.rows].rearrange("p (d c) -> p c d", c=4)
                for c in range(4):
                    ins = pe.transpose(ps[s][:, c * P:(c + 1) * P], view[:, c, :], ident)
                ins.then_inc(S("x_T"), 1)

            def gate_up(r, k, i=0):
                ex = Expert(k, i)
                e, s = ex.e, ex.buf
                pe.wait_ge(S(f"gate_up_loaded{ex.slot}"), ex.loaded(r, 32))
                pe.wait_ge(S("x_copied"), r * NE + e + 1)
                need(pe, "act_ready", r * NE + e - 1)
                w = gu_ring[ex.slot].rearrange("p (a k f) -> p k a f", a=2, k=KD)
                for d in range(KD):
                    c = (d % 4) * P + (d // 4) * SLOTS
                    for g in range(2):
                        o = ps[2 + s][g * SLOTS:(g + 1) * SLOTS, 0:FE].rearrange("p (a f) -> p a f", a=2)
                        ins = pe.matmul(o, XgT[s][:, c:c + SLOTS], w[:, d, :, g * P:(g + 1) * P], start=(d == 0), stop=(d == KD - 1))
                ins.then_inc(S("gate_up_done"), 1)

            def h_T(r, k, i=0):
                ex = Expert(k, i)
                e, s = ex.e, ex.buf
                pe.wait_ge(S("act_ready"), r * NE + e + 1)
                need(pe, "h_copied", r * NE + e)
                pe.transpose(ps[4][:, 0:P], hS, ident).then_inc(S("h_T"), 1)

            def down(r, k, i=0):
                ex = Expert(k, i)
                e, s = ex.e, ex.buf
                pe.wait_ge(S("h_copied"), r * NE + e + 1)
                pe.wait_ge(S(f"down_loaded{ex.slot}"), ex.loaded(r, 16))
                need(pe, "y_copied", r * NE + e - 1)
                w = down_ring[ex.slot].rearrange("p (j n) -> p j n", j=2)
                for j in range(2):
                    for g in range(2):
                        ins = pe.matmul(ps[5 + s][g * SLOTS:(g + 1) * SLOTS, :], hTb[:, j * SLOTS:(j + 1) * SLOTS],
                                        w[:, j, g * HD:(g + 1) * HD], start=(j == 0), stop=(j == 1))
                ins.then_inc(S("down_done"), 1)

            def round_(r):
                xT(r, 0)
                gate_up(r, 0)
                xT(r, 1)
                h_T(r, 0)

                def step(k, i):
                    gate_up(r, k, i)
                    xT(r, k + 1, i)
                    down(r, k - 1, i)
                    h_T(r, k, i)

                experts(pe, 1, NE - 2, step)
                gate_up(r, NE - 1)
                down(r, NE - 2)
                h_T(r, NE - 1)
                down(r, NE - 1)

            round_(0)
            more_rounds(pe, round_)

        def post_act(act):
            st = chain(act, "act_steps")

            def rsqrt(ap, src, scale):
                st.link(act.activation(ap, src, ACT.Ln, bias=EPS, scale=scale))
                return act.activation(ap, ap, ACT.Exp, scale=-0.5)

            wait(act, "states", NB - 1, 1)
            for a, src in enumerate((bre, bim)):
                last = v3(src, LT)[:, :, SEQ:T].rearrange("p i (b q) -> p b i q", b=NB)[:, :, :, NQ - 1]
                act.activation(v3(hlast[:, a * P:(a + 1) * P], NB), last, ACT.Copy).then_inc(S("last_states"), 1)
            act.wait_ge(S("gelu_inner"), 1)
            act.activation(g1, g1, ACT.Tanh, scale=math.sqrt(2 / math.pi)).then_inc(S("gelu_tanh"), 1)
            for a in range(2):
                b = read(act, f"hf{a}")
                st.inc(act.activation(hstates[0:LT, 256 * a:256 * a + P], b[0:LT, 0:P], ACT.Copy))
                st.sync()
                was_read(act.activation(hstates[:, 256 * a + P:256 * (a + 1)], b[:, P:2 * P], ACT.Copy), f"hf{a}")
            act.wait_ge(S("gelu_ready"), 1)
            for m in range(4):
                if m % 2 == 0:
                    c = slice(1536 * (m // 2), 1536 * (m // 2 + 1))
                    act.wait_ge(S("prompt_centred"), m + 2)
                    act.activation(CA[:, c], CA[:, c], ACT.Exp).then_inc(S("prompt_exp_ready"), 1)
                b = read(act, f"g{m}")
                was_read(act.activation(g1[:, m * T:(m + 1) * T], b[:, 0:T], ACT.Tanh, scale=0.25, bias=nbg[:, m:m + 1]), f"g{m}")
            act.preload_act_table_set(LN_EXP)
            for h in range(H):
                if h >= 2:
                    act.wait_ge(S("prompt_values"), h - 1)
                b = read(act, f"p{h}")
                was_read(act.activation(PT[h % 2], b[:, 0:384], ACT.Copy), f"p{h}")
                if h == 0:
                    act.wait_ge(S("glu_out"), 1)
                    used(act, "s7")
                    act.activation(sqT[:, :, 0:T], v3(yT, 4), ACT.Square, scale=0.25).then_inc(S("ssm_squared"), 1)
                if h == 2:
                    b = read(act, "ss")
                    st.link(act.activation(msS, b[:, 0:TT], ACT.Ln, bias=EPS, scale=1 / 512))
                    was_read(act.activation(msS, msS, ACT.Exp, scale=-0.5), "ss")
            act.wait_ge(S("att_ready"), 3)
            act.wait_ge(S("pool_steps"), 2)
            for i in range(TT):
                st.link(act.activation(junk_a, att[:, i * 512:(i + 1) * 512], ACT.Square, scale=512 ** -0.5, accum_out=msA[:, i:i + 1]))
            rsqrt(msA, msA, 1.0).then_inc(S("rs_att_ready"), 1)

            def normed_T_copy(i):
                b = read(act, f"xt{2 * i + 1}")
                was_read(act.activation(xsT[:, 4:8, i * P:(i + 1) * P], v3(b[:, :], 4), ACT.Copy), f"xt{2 * i + 1}")

            for i in range(TT):
                act.wait_ge(S("h_ready"), i + 1)
                st.link(act.activation(junk_h, x[:, i * D:(i + 1) * D], ACT.Square, scale=1 / 32, accum_out=msH[:, i:i + 1]))
                rsqrt(msH[:, i:i + 1], msH[:, i:i + 1], 1.0).then_inc(S("rs2_ready"), 1)
                if i:
                    normed_T_copy(i - 1)
            normed_T_copy(TT - 1)
            act.wait_ge(S("router_diffs"), 1)
            st.link(act.activation(e4, e4, ACT.Exp))
            act.activation(w12[:, 0:3], w12[:, 0:3], ACT.Exp).then_inc(S("router_exp"), 1)

            def x_copy(r, k, i=0):
                ex = Expert(k, i)
                e, s = ex.e, ex.buf
                act.wait_ge(S("x_T"), r * NE + e + 1)
                need(act, "gate_up_done", r * NE + e - 1)
                act.activation(XgT[s], ps[s][:, :], ACT.Copy).then_inc(S("x_copied"), 1)

            def tanh_(r, k, i=0):
                ex = Expert(k, i)
                e, s = ex.e, ex.buf
                act.wait_ge(S("gate_up_done"), r * NE + e + 1)
                need(act, "act_ready", r * NE + e)
                act.activation(thb, ps[2 + s][:, 0:P], ACT.Tanh, scale=0.5).then_inc(S("gate_tanh"), 1)

            def y_copy(r, k, i=0):
                ex = Expert(k, i)
                e, s = ex.e, ex.buf
                act.wait_ge(S("down_done"), r * NE + e + 1)
                need(act, f"scattered{ex.rows}", (r * (NE // ROWS) + ex.turn) * 16)
                act.activation(Yo[ex.rows], ps[5 + s][:, :], ACT.Copy).then_inc(S("y_copied"), 1)

            def round_(r):
                x_copy(r, 0)
                tanh_(r, 0)
                x_copy(r, 1)

                def step(k, i):
                    tanh_(r, k, i)
                    x_copy(r, k + 1, i)
                    y_copy(r, k - 1, i)

                experts(act, 1, NE - 2, step)
                tanh_(r, NE - 1)
                y_copy(r, NE - 2)
                y_copy(r, NE - 1)

            round_(0)
            more_rounds(act, round_)

        def post_ve(ve):
            st = chain(ve, "dve_steps")
            tt = ve.tensor_tensor
            for m in range(4):
                b = read(ve, f"y{m}")
                was_read(ve.scalar_tensor_tensor(out=yT[:, m * T:(m + 1) * T], in0=uT[:, m * T:(m + 1) * T],
                                                 scalar=vcol("ssm_d")[:, m:m + 1], in1=b[:, 0:T], op0=ALU.mult, op1=ALU.add), f"y{m}")
            for m in range(4):
                used(ve, f"y{m}")
            st.link(tt(g1, yT, yT, ALU.mult))
            st.link(ve.tensor_scalar(g1, g1, 0.044715, 1.0, ALU.mult, ALU.add))
            tt(g1, g1, yT, ALU.mult).then_inc(S("gelu_inner"), 1)
            st.inc(ve.tensor_scalar(nbg, vcol("ssm_b_glu"), 0.5, None, ALU.mult))
            st.inc(ve.tensor_scalar(gain4, vcol("out_norm_ssm"), 0.25, None, ALU.mult))
            for part in (4, 5):
                ve_tail(ve, NB - 1, 1, part)
            ve.wait_ge(S("gelu_tanh"), 1)
            ve.scalar_tensor_tensor(out=yT, in0=g1, scalar=1.0, in1=yT, op0=ALU.add, op1=ALU.mult).then_inc(S("gelu_ready"), 1)
            blocks = (Sp[:, :, 0:P], Sp[:, :, P:3 * P])
            for q in range(2):
                heads = range(4 * q, 4 * q + 4)
                for h in heads:
                    b = read(ve, f"s{h}")
                    was_read(tt(Sp[:, h, :], b[:, 0:384], C("causal"), ALU.add), f"s{h}")
                for h in heads:
                    used(ve, f"s{h}")
                maxima = [pm[0][:, 8 * i + 4 * q:8 * i + 4 * q + 4] for i in range(2)]
                for i, s in enumerate(blocks):
                    ins = ve.tensor_reduce(maxima[i], s[:, 4 * q:4 * q + 4], AX, ALU.max)
                    st.inc(ins)
                st.sync()
                for i, s in enumerate(blocks):
                    s4 = s[:, 4 * q:4 * q + 4]
                    tt(s4, s4, bc(maxima[i], 2, (i + 1) * P), ALU.subtract).then_inc(S("prompt_centred"), 1)
            b = read(ve, "as")
            was_read(ve.tensor_copy(att[0:NS, 1024:1536], b[0:NS, :]), "as")
            for m in range(4):
                used(ve, f"g{m}")
            ve.wait_ge(S("gelu_ready"), 1)
            ve.scalar_tensor_tensor(out=yT, in0=g1, scalar=1.0, in1=yT, op0=ALU.add, op1=ALU.mult).then_inc(S("glu_out"), 1)
            ve.wait_ge(S("glu_out"), 1)
            tt(soT[:, :, 0:T], v3(yT, 4), bc(gain4, 2, T), ALU.mult).then_inc(S("so_ready"), 1)
            ve.wait_ge(S("prompt_exp_ready"), 2)
            for i, s in enumerate(blocks):
                st.link(ve.tensor_reduce(pm[1][:, 8 * i:8 * i + 8], s, AX, ALU.add))
            st.link(ve.reciprocal(pm[1], pm[1]))
            def add_to_x(i, a):
                b = read(ve, f"w{i}{a}")
                n = P if i < 2 else NS
                rs = (msS if a < 2 else msA)[0:n, i:i + 1]
                for g in range(a % 2, a % 2 + 1) if i < 2 else range(2):
                    o = x[0:n, i * D + 512 * g:i * D + 512 * (g + 1)]
                    part = b[:, :] if i < 2 else b[g * NS:(g + 1) * NS, :]
                    ins = ve.scalar_tensor_tensor(out=o, in0=part, scalar=rs, in1=o, op0=ALU.mult, op1=ALU.add)
                was_read(ins, f"w{i}{a}")

            used(ve, "ss")
            for name in ssm_part:
                add_to_x(int(name[1]), int(name[2]))
            used(ve, "as")
            for i in range(2):
                b = read(ve, f"o{i}")
                was_read(tt(v3(att[:, i * 512:(i + 1) * 512], H), v3(b[:, :], H), bc(pm[1][:, 8 * i:8 * i + 8], 2, VD), ALU.mult), f"o{i}")
            used(ve, "o0")
            used(ve, "o1")
            st.link(ve.tensor_copy(pm[2][:, 0:1], pm[1][:, 0:1]))
            ve.tensor_copy(pm[2][:, 1:2], pm[2][:, 0:1]).then_inc(S("att_ready"), 3)

            for i in range(TT):
                b = read(ve, f"at{i}")
                was_read(tt(attT[:, :, i * P:(i + 1) * P], v3(b[:, :], 4), bc(vcol("out_norm_attn"), 2, P), ALU.mult), f"at{i}")
            ve.wait_ge(S("rs_att_ready"), 1)
            ve.wait_ge(S("route_inputs_loaded"), 80)

            def norm_2(i):
                ve.wait_ge(S("rs2_ready"), i + 1)
                ve.scalar_tensor_tensor(out=xs[:, i * D:(i + 1) * D], in0=x[:, i * D:(i + 1) * D], scalar=msH[:, i:i + 1],
                                        in1=g2row, op0=ALU.mult, op1=ALU.mult).then_inc(S("xs_ready"), 1)

            def normed_T_copy(i):
                b = read(ve, f"xt{2 * i}")
                was_read(ve.tensor_copy(xsT[:, 0:4, i * P:(i + 1) * P], v3(b[:, :], 4)), f"xt{2 * i}")

            for i in range(TT):
                parts = range(2) if i < 2 else (0,)
                for a in parts:
                    used(ve, f"w{i}{a}")
                for a in parts:
                    add_to_x(i, a + 2)
                for a in parts:
                    used(ve, f"w{i}{a + 2}")
                ve.tensor_copy(pm[2][:, 2 + i:3 + i], pm[2][:, 0:1]).then_inc(S("h_ready"), 1)
                norm_2(i)
                if i:
                    normed_T_copy(i - 1)
            normed_T_copy(TT - 1)
            ve.memset(routed[:, TT * NE:4 * NE], 0.0)
            b = read(ve, "rt")
            lg = v3(lgt, TT)
            was_read(tt(lg, v3(b[:, 0:108], TT), bc(b_r[:, :], 1, TT), ALU.add), "rt")
            used(ve, "rt")

            def first_max(src, n, m, mask):
                st.link(ve.tensor_reduce(m, src, AX, ALU.max))
                eq = v3(one[:, 0:TT * n], TT)
                st.link(tt(eq, src, bc(m, 2, n), ALU.is_equal))
                prs = pairs[:, 0:TT * n * n].rearrange("p (i a b) -> p i a b", i=TT, a=n)
                early = C("early8" if n == 8 else "early4").rearrange("p (a b) -> p a b", a=n)
                st.link(tt(prs, bc(eq, 2, n), bc(early, 1, TT), ALU.mult))
                st.link(ve.tensor_reduce(work8[:, 0:TT * n], prs.rearrange("p i a b -> p (i a) b"), AX, ALU.add))
                st.link(ve.scalar_tensor_tensor(out=mask, in0=work8[:, 0:TT * n], scalar=0.0, in1=one[:, 0:TT * n],
                                                op0=ALU.is_equal, op1=ALU.mult))

            first_max(lg[:, :, 0:NG], NG, m4, mask4)
            st.inc(tt(v3(e4, TT), lg[:, :, 0:NG], bc(m4, 2, NG), ALU.subtract))
            grp = mask4.rearrange("p (i g) -> p i g", i=TT)
            t32 = one.rearrange("p (i g e) -> p i g e", i=TT, g=NG)
            st.link(tt(t32, lg[:, :, NG:].rearrange("p i (g e) -> p i g e", g=NG), bc(grp, 3, EG), ALU.mult))
            st.link(ve.tensor_reduce(v3(le8, TT), t32.rearrange("p i g e -> p i e g"), AX, ALU.add))
            first_max(v3(le8, TT), EG, m8[:, 0:3], mask8a)
            st.link(ve.scalar_tensor_tensor(out=le8, in0=mask8a, scalar=NEG, in1=le8, op0=ALU.mult, op1=ALU.add))
            first_max(v3(le8, TT), EG, m8[:, 3:6], mask8b)
            tt(w12[:, 0:3], m8[:, 3:6], m8[:, 0:3], ALU.subtract).then_inc(S("router_diffs"), 1)
            m8a, m8b = v3(mask8a, TT), v3(mask8b, TT)
            def spread(dst, src8):
                return tt(dst, bc(src8, 2, NG), bc(grp, 3, EG), ALU.mult)

            def four(ap):
                return ap.rearrange("p (i g e) -> p i g e", i=TT, g=NG)

            st.link(spread(four(first), m8a))
            st.link(spread(four(second), m8b))
            r3 = routed[:, 0:TT * NE]
            st.link(tt(r3, first, second, ALU.add))
            tt(v3(r3, TT), v3(r3, TT), bc(C("valid"), 2, NE), ALU.mult).then_inc(S("routed_ready"), 1)
            ve.wait_ge(S("router_exp"), 1)
            st.link(ve.tensor_reduce(psel, v3(e4, TT), AX, ALU.add))
            st.link(ve.tensor_scalar(tsum, w12[:, 0:3], 1.0, None, ALU.add))
            st.link(tt(psel, psel, tsum, ALU.mult))
            st.link(ve.reciprocal(psel, psel))
            st.link(tt(w12[:, 3:6], w12[:, 0:3], psel, ALU.mult))
            r4 = rows.rearrange("p (k i c) -> p k i c", k=2, i=TT)
            for k, gate in enumerate((psel, w12[:, 3:6])):
                st.link(ve.tensor_copy(r4[:, k, :, 0], C("tok")))
                st.link(ve.tensor_scalar(r4[:, k, :, 1], C("tok"), float(k * T), None, ALU.add))
                st.link(ve.tensor_copy(r4[:, k, :, 2], gate))
                st.link(ve.tensor_copy(r4[:, k, :, 3], C("tok")))
            b = read(ve, "cum")
            st.link(ve.scalar_tensor_tensor(out=v3(where, TT), in0=v3(b[:, 0:3 * NE], TT), scalar=float(NE),
                                            in1=bc(C("ramp"), 1, TT), op0=ALU.mult, op1=ALU.add))
            for k, mask in enumerate((first, second)):
                st.link(tt(prod, where, mask, ALU.mult))
                st.link(ve.tensor_reduce(tgt[:, 3 * k:3 * k + 3], v3(prod, TT), AX, ALU.add))
            tt(v3(tgi[:, :], 2), v3(tgt, 2), bc(C("beyond"), 1, 2), ALU.add).then_inc(S("routing_ready"), 1)
            st.link(ve.tensor_reduce(cnt, b[:, 3 * NE:4 * NE], AX, ALU.max))
            st.inc(ve.tensor_copy(most[:, :], cnt))
            was_read(ve.tensor_copy(pm[2][:, 6:7], cnt), "cum")
            used(ve, "cum")
            ve.tensor_copy(pm[2][:, 7:8], cnt).then_inc(S("routing_ready"), 1)

            def lists(r):
                need(ve, "gather_index", r * NE)
                need(ve, "scatter_index", r * NE)
                ve.wait_ge(S("lists_loaded"), r * 32 + 32)
                l3 = lst.rearrange("p (e c) -> p c e", c=4)
                ve.tensor_scalar(gall[:, :], l3[:, 0, :], 2.0, C("half"), ALU.mult, ALU.add)
                ve.tensor_scalar(sall[:, :], l3[:, 1, :], 2.0, C("half"), ALU.mult, ALU.add)
                ve.tensor_scalar(gates, l3[:, 2, :], 0.5, None, ALU.mult).then_inc(S("lists_ready"), 1)
                ve.wait_ge(S("lists_ready"), r + 1)

            def silu(r, k, i=0):
                ex = Expert(k, i)
                e, s = ex.e, ex.buf
                G = r * NE + e
                ve.wait_ge(S("gate_tanh"), G + 1)
                ve.scalar_tensor_tensor(out=hmb, in0=thb, scalar=1.0, in1=ps[2 + s][:, 0:P], op0=ALU.add,
                                        op1=ALU.mult).then_inc(S("silu_steps"), 1)
                ve.wait_ge(S("silu_steps"), G + 1)
                need(ve, "h_T", G)
                ve.scalar_tensor_tensor(out=hS, in0=hmb, scalar=gates[:, bass.ds(e, 1)], in1=ps[2 + s][:, P:2 * P], op0=ALU.mult,
                                        op1=ALU.mult).then_inc(S("act_ready"), 1)

            def h_copy(r, k, i=0):
                ex = Expert(k, i)
                e, s = ex.e, ex.buf
                G = r * NE + e
                ve.wait_ge(S("h_T"), G + 1)
                need(ve, "down_done", G)
                ve.tensor_copy(hTb, ps[4][:, 0:P]).then_inc(S("h_copied"), 1)

            def round_(r):
                lists(r)
                silu(r, 0)
                h_copy(r, 0)

                def step(k, i):
                    silu(r, k, i)
                    h_copy(r, k, i)

                experts(ve, 1, NE - 2, step)
                silu(r, NE - 1)
                h_copy(r, NE - 1)

            round_(0)
            more_rounds(ve, round_)
            for i in range(TT):
                n = P if i < 2 else NS
                ve.wait_ge(S(f"rows{i}_back"), 32)
                h = x[0:n, i * D:(i + 1) * D]
                st.link(tt(h, h, R[0:n, i * D:(i + 1) * D], ALU.add))
                tt(h, h, R[0:n, 3072 + i * D:3072 + (i + 1) * D], ALU.add).then_inc(S("y_ready"), 1)

        block = ctx.enter_context(nc.Block())

        def v3(ap, a):
            return ap.rearrange("p (a b) -> p a b", a=a)

        @block.sync
        def _(sp):
            sp.dma_start(x[:, 0:D], I["x_prompt"][0, 0:P, :]).then_inc(S("x0_loaded"), 16)
            sp.dma_start(x[:, D:2 * D], I["x_prompt"][0, P:2 * P, :]).then_inc(S("x1_loaded"), 16)
            sp.dma_start(x[0:NS, 2 * D:3 * D], I["x_sample"].rearrange("b t d -> (b t) d")).then_inc(S("x2_loaded"), 16)
            sp.dma_start(cst[:, :], I["shape_constants"][:, 0:LASTING]).then_inc(S("constants_loaded"), 16)
            sp.dma_start(cst_early, I["shape_constants"][:, LASTING:]).then_inc(S("constants_loaded"), 16)
            with nc.allow_non_contiguous_dma(reason="small tables"):
                sp.dma_start(ldt[0:LT, :], I["ssm_log_dt"].rearrange("o (i e) -> (o i) e", e=2)).then_inc(S("log_dt_loaded"), 16)
                sp.dma_start(pgt[0:UP, :], I["page_table"].rearrange("b (h g) -> g (b h)", g=UP)).then_inc(S("pages_loaded"), 16)
            for name in ("norm1_g", "ssm_d", "ssm_b_glu", "q_norm_g", "out_norm_ssm", "out_norm_attn"):
                a, b = ROW[name]
                sp.dma_start(vrow[a:b, :], I[name].rearrange("o (r p) -> (o r) p", p=P)).then_inc(S("rows_loaded"), 16)
            for name in ("qk_norm_q", "qk_norm_k"):
                a, b = ROW[name]
                sp.dma_start(vrow[a:b, 0:QK], I[name]).then_inc(S("rows_loaded"), 16)
                sp.dma_start(vrow[a:b, QK:P], I[name][:, 0:P - QK]).then_inc(S("rows_loaded"), 16)
            for name in ("ssm_a_re", "ssm_a_im"):
                a, b = ROW[name]
                sp.dma_start(vrow[a:b, :], I[name].rearrange("o (i e) p -> (o i) (e p)", e=2)).then_inc(S("rows_loaded"), 16)
            for a, name in enumerate(("state_ssm_re", "state_ssm_im")):
                sp.dma_start(sraw[:, a * P:(a + 1) * P],
                             I[name].rearrange("o b (i e) p -> (o b i) (e p)", e=2)).then_inc(S("rows_loaded"), 16)
            for k0 in (0, 4):
                sp.dma_start(w_in[:, k0:k0 + 4, :],
                             I["w_in"][0, k0 * P:(k0 + 4) * P, :].rearrange("(k p) n -> p k n", p=P)).then_inc(S(f"w_in_loaded{k0 // 4}"), 16)
            with nc.allow_non_contiguous_dma(reason="64-byte rows of the input matrices"):
                for a, name in enumerate(("ssm_b_re", "ssm_b_im")):
                    sp.dma_start(braw[:, a], I[name].rearrange("o (i e) p c -> (o e p) i c", e=2)).then_inc(S("b_loaded"), 16)
                for a, name in enumerate(("ssm_c_re", "ssm_c_im")):
                    for e in range(2):
                        sp.dma_start(craw[:, a, :, e, :],
                                     I[name].rearrange("o (m g) c p -> (o g c) m p", m=4)).then_inc(S("c_loaded"), 16)
            sp.dma_start(g_row[:, 0:KR], I["kv_norm_g"].to_broadcast([P, KR])).then_inc(S("gains_loaded"), 16)
            sp.dma_start(g_row[:, KR:KR + QK], I["qk_norm_q"].to_broadcast([P, QK])).then_inc(S("gains_loaded"), 16)
            sp.dma_start(g_row[:, KR + QK:], I["qk_norm_k"].to_broadcast([P, QK])).then_inc(S("gains_loaded"), 16)
            sp.dma_start(w_uq[:, :, :], I["w_uq"][0].rearrange("(k p) h d -> p k (h d)", p=P)).then_inc(S("w_uq_loaded"), 16)
            sp.dma_start(w_uk[:, :], I["w_uk"][0].rearrange("r h d -> r (h d)")).then_inc(S("w_kv_loaded"), 16)
            sp.dma_start(w_uv[:, :], I["w_uv"][0].rearrange("r h d -> r (h d)")).then_inc(S("w_kv_loaded"), 16)
            sp.dma_start(lists_dram, I["empty_lists"]).then_inc(S("lists_emptied"), 16)
            sp.wait_ge(S("latents_ready"), 2)
            for i in range(2):
                sp.dma_start(O["ckv_p"][0, i], ckvn[:, i * KR:(i + 1) * KR]).then_inc(S("outputs_stored"), 16)
                sp.dma_start(O["kr_p"][0, i], krn[:, i * ROPE:(i + 1) * ROPE]).then_inc(S("outputs_stored"), 16)
            sp.dma_start(O["ckv_s"].rearrange("o b t r -> (o b t) r"), ckvn[0:NS, 2 * KR:]).then_inc(S("outputs_stored"), 16)
            sp.dma_start(O["kr_s"].rearrange("o b t r -> (o b t) r"), krn[0:NS, 2 * ROPE:]).then_inc(S("outputs_stored"), 16)
            used(sp, "qT7")
            used(sp, "kT7")
            used(sp, "qr")
            sp.dma_start(w_out, I["w_out"][0].rearrange("(k p) n -> p k n", p=P)).then_inc(S("w_out_loaded"), 16)
            post_sync(sp)

        @block.gpsimd
        def _(pool):
            pool.memset(x[64:P, 2 * D:3 * D], 0.0).then_inc(S("pads_set"), 1)
            pool.wait_ge(S("pads_set"), 1)
            pool.memset(R[:, 11520:12544], 0.0).then_inc(S("pads_set"), 1)
            for i in range(2):
                pool.wait_ge(S("pads_set"), 2 + i)
                pool.memset(Ssb[i][64:P, 1024:1088], NEG).then_inc(S("pads_set"), 1)
            pool.wait_ge(S("pads_set"), 4)
            pool.memset(soft[:, NS:P], 0.0).then_inc(S("pads_set"), 1)
            used(pool, "vec")
            pool.wait_ge(S("pads_set"), 5)
            pool.memset(vrow[NS:P, :], 0.0).then_inc(S("pads_set"), 1)
            pool.wait_ge(S("pads_set"), 6)
            pool.wait_ge(S("page_rows_ready"), 1)
            for u in range(4):
                gather_unit(pool, u, 0)
            pool_loop(pool)

        @block.tensor
        def _(pe):
            pe.wait_ge(S("constants_loaded"), 32)
            pe.wait_ge(S("rows_loaded"), 16 * 14)
            pe.wait_ge(S("log_dt_spread"), 1)
            b = fill(pe, "vec")
            pe.transpose(b[:, 0:NROW], vrow[0:NROW, :], ident[0:NROW, 0:NROW])
            pe.transpose(b[:, 128:256], sraw[:, 0:P], ident)
            filled(pe.transpose(b[:, 256:384], sraw[:, P:2 * P], ident), "vec")
            for i in range(TT):
                pe.wait_ge(S("xn_ready"), i + 1)
                for g in range(2):
                    b = fill(pe, f"xT{2 * i + g}")
                    for k in range(4):
                        c = i * D + (4 * g + k) * P
                        ins = pe.transpose(b[:, k * P:(k + 1) * P], xn[:, c:c + P], ident)
                    filled(ins, f"xT{2 * i + g}")
            pe.wait_ge(S("page_table_ready"), 1)
            b = fill(pe, "page")
            filled(pe.matmul(b[:, 0:16], C("pgsel", UP), pgf[0:UP, 0:16], start=True, stop=True), "page")
            for i in range(6):
                used(pe, f"xT{i}")
            for m in range(4):
                b = fill(pe, f"u{m}")
                for k in range(KD):
                    if m == 0 and k % 4 == 0:
                        pe.wait_ge(S(f"w_in_loaded{k // 4}"), 16)
                    ins = pe.matmul(b[:, 0:T], w_in[:, k, m * P:(m + 1) * P], nT[:, k, 0:T],
                                    start=(k == 0), stop=(k == KD - 1))
                filled(ins, f"u{m}")
            pe.wait_ge(S("c_loaded"), 64)
            for a in range(2):
                b = fill(pe, f"ct{a}")
                for m in range(4):
                    ins = pe.transpose(b[:, m * P:(m + 1) * P], craw[:, a, m].rearrange("p e s -> p (e s)"), ident)
                filled(ins, f"ct{a}")
            for i in range(TT):
                b = fill(pe, f"z{i}")
                for k in range(KD):
                    ins = pe.matmul(b[:, 0:ZW], nT[:, k, i * P:(i + 1) * P], w_in[:, k, SSM_W:DIN],
                                    start=(k == 0), stop=(k == KD - 1))
                filled(ins, f"z{i}")
            pe.wait_ge(S("b_spread"), 4)
            for a in range(2):
                b = fill(pe, f"bd{a}")
                for m in range(4):
                    ins = pe.transpose(b[:, m * P:(m + 1) * P],
                                       xst[:, a, 4 * m:4 * m + 4].rearrange("p i e c -> p (i e c)"), ident)
                filled(ins, f"bd{a}")
            used(pe, "bd0")
            used(pe, "bd1")
            used(pe, "u3")

            def input_products(m):
                for n, name in enumerate(bu_groups(m)):
                    bd = bd4[n % 2][:, n // 2]
                    b = fill(pe, name)
                    filled(pe.matmul(b[:, 0:T], bd[:, m * P:(m + 1) * P], uT[:, m * T:(m + 1) * T],
                                     start=True, stop=True), name)

            input_products(0)
            pe.wait_ge(S("cq_ready"), 3)
            for k in range(2):
                b = fill(pe, f"cq{k}")
                for i in range(TT):
                    ins = pe.transpose(b[:, i * P:(i + 1) * P], cqn[:, i, k * P:(k + 1) * P], ident)
                filled(ins, f"cq{k}")
            pe.wait_ge(S("latents_ready"), 2)
            b = fill(pe, "ckvT")
            for i in range(TT):
                ins = pe.transpose(b[:, i * P:(i + 1) * P], ckvn[:, i * KR:(i + 1) * KR], ident)
            filled(ins, "ckvT")
            for m in range(1, 4):
                input_products(m)
            used(pe, "cq0")
            used(pe, "cq1")
            pe.wait_ge(S("w_uq_loaded"), 16)
            for i in range(TT):
                for g, (lo, hi) in enumerate(((0, 512), (512, 768))):
                    b = fill(pe, f"q{i}{g}")
                    for k in range(2):
                        ins = pe.matmul(b[:, 0:hi - lo], cqT[:, k, i * P:(i + 1) * P], w_uq[:, k, lo:hi],
                                        start=(k == 0), stop=(k == 1))
                    filled(ins, f"q{i}{g}")
            pe.wait_ge(S("w_kv_loaded"), 32)
            used(pe, "ckvT")
            for i in range(TT):
                b = fill(pe, f"k{i}")
                filled(pe.matmul(b[:, :], ckvT[:, i * P:(i + 1) * P], w_uk[:, :], start=True, stop=True), f"k{i}")
            for i in range(2):
                b = fill(pe, f"v{i}")
                filled(pe.matmul(b[:, :], ckvT[:, i * P:(i + 1) * P], w_uv[:, :], start=True, stop=True), f"v{i}")
            for what, src, ready in (("qT", q, "q_ready"), ("kT", kk, "k_ready")):
                pe.wait_ge(S(ready), 1)
                for h in range(H):
                    b = fill(pe, f"{what}{h}")
                    for i in range(TT):
                        ins = pe.transpose(b[0:QK, i * P:(i + 1) * P], src[:, i, h, :], ident)
                    filled(ins, f"{what}{h}")
            for g in range(2):
                b = fill(pe, f"uk{g}")
                for h in range(4):
                    c = (4 * g + h) * NOPE
                    ins = pe.transpose(b[0:NOPE, h * P:(h + 1) * P], w_uk[:, c:c + NOPE], ident)
                filled(ins, f"uk{g}")
            b = fill(pe, "qr")
            pe.wait_ge(S("q_rope_spread"), 1)
            for h in range(H):
                ins = pe.transpose(b[:, h * NS:(h + 1) * NS], qr4[0:NS, h].rearrange("p e d -> p (e d)"), ident[0:NS, 0:NS])
            filled(ins, "qr")
            used(pe, "uk1")
            used(pe, "uk0")
            for h in range(H):
                used(pe, f"qT{h}")
                used(pe, f"kT{h}")
            b = fill(pe, "qa")
            for h in range(H):
                ins = pe.matmul(b[:, h * NS:(h + 1) * NS], w_ukT[0:NOPE, h, :], qT[0:NOPE, h, SEQ:T], start=True, stop=True)
            filled(ins, "qa")
            b = fill(pe, "sn")
            for h in range(H):
                ins = pe.matmul(b[0:NS, h * NS:(h + 1) * NS], kT[0:QK, h, SEQ:T], qT[0:QK, h, SEQ:T], start=True, stop=True)
            filled(ins, "sn")
            for i in range(8):
                pe.wait_ge(S(f"free{i}"), pre_uses[i])
            pe_loop(pe)

        @block.scalar
        def _(act):
            st = chain(act, "act_steps")

            def rsqrt(ap, scale=1.0):
                st.link(act.activation(ap, ap, ACT.Ln, bias=EPS, scale=scale))
                return act.activation(ap, ap, ACT.Exp, scale=-0.5)

            act.wait_ge(S("pads_set"), 1)
            for i in range(TT):
                act.wait_ge(S(f"x{i}_loaded"), 16)
                st.link(act.activation(junk, x[:, i * D:(i + 1) * D], ACT.Square, scale=1 / 32, accum_out=ms1[:, i:i + 1]))
            rsqrt(ms1).then_inc(S("rs1_ready"), 1)
            used(act, "vec")
            act.activation(p_dt, vcol("log_dt"), ACT.Exp).then_inc(S("pole_exps_ready"), 1)
            act.wait_ge(S("angles_ready"), 1)
            act.activation(p_mag, p_b, ACT.Exp).then_inc(S("pole_exps_ready"), 1)
            st.link(act.activation(p_ab, p_f, ACT.Abs))
            act.activation(p_sin, p_f, ACT.Sin, scale=TWO_PI).then_inc(S("trig0_ready"), 1)
            act.activation(p_cos, p_ab, ACT.Sin, scale=-TWO_PI, bias=math.pi / 2).then_inc(S("trig0_ready"), 1)
            for m in range(4):
                b = read(act, f"u{m}")
                was_read(act.activation(uT[:, m * T:(m + 1) * T], b[:, 0:T], ACT.Copy), f"u{m}")
            for i in range(TT):
                b = read(act, f"z{i}")
                was_read(act.activation(z[:, i, :], b[:, 0:ZW], ACT.Copy), f"z{i}")
                used(act, f"z{i}")
                st.inc(act.activation(junk[:, 0:QR], z[:, i, 0:QR], ACT.Square, scale=1 / 16, accum_out=ms2[:, i:i + 1]))
                st.inc(act.activation(junk[:, QR:QR + KR], z[:, i, QR:QR + KR], ACT.Square, scale=KR ** -0.5,
                                      accum_out=ms2[:, 3 + i:4 + i]))
                st.sync()
            rsqrt(ms2).then_inc(S("rs_latent_ready"), 1)
            for i in range(LT):
                b = read(act, f"bu{2 * i}")
                was_read(act.activation(bre[:, i * T:(i + 1) * T], b[:, 0:T], ACT.Copy), f"bu{2 * i}")
            for i in range(TT):
                for g, (lo, hi) in enumerate(((0, 512), (512, 768))):
                    b = read(act, f"q{i}{g}")
                    o = O1[:, i * 768 + lo:i * 768 + hi]
                    was_read(act.activation(o, b[:, 0:hi - lo], ACT.Copy), f"q{i}{g}")
            for i in range(TT):
                b = read(act, f"k{i}")
                was_read(act.activation(kk[:, i, :, 0:NOPE], v3(b[:, :], H), ACT.Copy), f"k{i}")
            for i in range(2):
                b = read(act, f"v{i}")
                was_read(act.activation(v[:, i * 512:(i + 1) * 512], b[:, :], ACT.Copy), f"v{i}")
            act.wait_ge(S("q_rotated"), 1)
            act.activation(QT[:, 0:2304], O1[:, 0:2304], ACT.Square, scale=QK ** -0.5).then_inc(S("qk_squared"), 1)
            act.wait_ge(S("k_filled"), 1)
            for i in range(TT):
                used(act, f"k{i}")
            act.activation(KT[:, 0:2304], O1[:, 2304:4608], ACT.Square, scale=QK ** -0.5).then_inc(S("qk_squared"), 1)
            act.wait_ge(S("qk_sums_ready"), 2)
            rsqrt(small[:, 16:64]).then_inc(S("rs_qk_ready"), 1)
            for h in range(H):
                b = read(act, f"kT{h}")
                was_read(act.activation(kT[0:QK, h, :], b[0:QK, 0:T], ACT.Copy), f"kT{h}")
            act_loop(act)

        @block.vector
        def _(ve):
            st = chain(ve, "dve_steps")
            ve.wait_ge(S("log_dt_loaded"), 16)
            ve.tensor_copy(v3(vrow[0:LT, :], 2), bc(ldt[0:LT, :], 2, SP)).then_inc(S("log_dt_spread"), 1)
            ve.wait_ge(S("pages_loaded"), 16)
            ve.tensor_copy(pgf[0:UP, 0:16], pgt[0:UP, :]).then_inc(S("page_table_ready"), 1)
            ve.wait_ge(S("rs1_ready"), 1)
            for i in range(TT):
                ve.tensor_scalar(xn[:, i * D:(i + 1) * D], x[:, i * D:(i + 1) * D], ms1[:, i:i + 1], None,
                                 ALU.mult).then_inc(S("xn_ready"), 1)
            b = read(ve, "vec")
            st.inc(ve.tensor_copy(st0[:, :], b[:, 128:384]))
            was_read(ve.tensor_copy(vec[:, :], b[:, 0:NROW]), "vec")
            used(ve, "vec")
            for i in range(6):
                b = read(ve, f"xT{i}")
                k0, t0 = 4 * (i % 2), (i // 2) * P
                was_read(ve.tensor_tensor(nT[:, k0:k0 + 4, t0:t0 + P], v3(b[:, :], 4),
                                          bc(vcol("norm1_g")[:, k0:k0 + 4], 2, P), ALU.mult), f"xT{i}")
            b = read(ve, "page")
            was_read(ve.tensor_scalar(page_all[:, :], b[:, 0:16], float(PAGE // RUN), C("pgrow"), ALU.mult, ALU.add), "page")
            used(ve, "page")
            ve.tensor_copy(page_idx[:, :], page_all[:, 0:4]).then_inc(S("page_rows_ready"), 1)
            ar, ai = vcol("ssm_a_re"), vcol("ssm_a_im")
            c1 = 6.28125
            ve.wait_ge(S("pole_exps_ready"), 1)
            st.inc(ve.tensor_tensor(p_ang, ai, p_dt, ALU.mult))
            st.link(ve.tensor_tensor(p_b, ar, p_dt, ALU.mult))
            st.link(ve.tensor_scalar(p_k, p_ang, 1 / (2 * math.pi), MAGIC, ALU.mult, ALU.add))
            st.link(ve.tensor_scalar(p_k, p_k, MAGIC, None, ALU.subtract))
            st.link(ve.scalar_tensor_tensor(out=p_th, in0=p_k, scalar=-c1, in1=p_ang, op0=ALU.mult, op1=ALU.add))
            st.link(ve.scalar_tensor_tensor(out=p_th, in0=p_k, scalar=-(2 * math.pi - c1), in1=p_th, op0=ALU.mult, op1=ALU.add))
            st.link(ve.tensor_scalar(p_f, p_th, 1 / (2 * math.pi), 0.5, ALU.mult, ALU.min))
            ve.tensor_scalar(p_f, p_f, -0.5, None, ALU.max).then_inc(S("angles_ready"), 1)
            ve.wait_ge(S("pole_exps_ready"), 2)
            ve.wait_ge(S("trig0_ready"), 2)
            ve.wait_ge(S("b_loaded"), 32)
            ve.wait_ge(S("pads_set"), 4)
            st.inc(ve.tensor_tensor(p_lr, p_mag, p_cos, ALU.mult))
            st.inc(ve.tensor_tensor(p_li, p_mag, p_sin, ALU.mult))
            st.inc(ve.tensor_tensor(p_a, ar, ar, ALU.mult))
            st.inc(ve.tensor_tensor(p_den, ai, ai, ALU.mult))
            st.sync()
            st.inc(ve.tensor_scalar(p_lr, p_lr, -1.0, None, ALU.add))
            st.link(ve.tensor_tensor(p_den, p_den, p_a, ALU.add))
            st.inc(ve.reciprocal(p_den, p_den))
            st.inc(ve.tensor_tensor(p_a, p_lr, ar, ALU.mult))
            st.inc(ve.tensor_tensor(p_b, p_li, ai, ALU.mult))
            st.inc(ve.tensor_tensor(p_k, p_li, ar, ALU.mult))
            st.inc(ve.tensor_tensor(p_th, p_lr, ai, ALU.mult))
            st.sync()
            st.inc(ve.tensor_tensor(p_cr, p_a, p_b, ALU.add))
            st.inc(ve.tensor_tensor(p_ci, p_k, p_th, ALU.subtract))
            st.sync()
            st.inc(ve.tensor_tensor(p_cr, p_cr, p_den, ALU.mult))
            st.inc(ve.tensor_tensor(p_ci, p_ci, p_den, ALU.mult))
            st.sync()
            t = [v3(rt[i][:, 0:256], LT) for i in range(4)]
            crb, cib = bc(p_cr, 2, CH), bc(p_ci, 2, CH)
            st.inc(ve.tensor_tensor(t[0], crb, braw[:, 0], ALU.mult))
            st.inc(ve.tensor_tensor(t[1], cib, braw[:, 1], ALU.mult))
            st.inc(ve.tensor_tensor(t[2], crb, braw[:, 1], ALU.mult))
            st.inc(ve.tensor_tensor(t[3], cib, braw[:, 0], ALU.mult))
            st.sync()
            for e in range(2):
                r = slice(64 * e, 64 * e + 64)
                ve.tensor_tensor(xst[r, 0, :, e, :], t[0][r], t[1][r], ALU.subtract).then_inc(S("b_spread"), 1)
                ve.tensor_tensor(xst[r, 1, :, e, :], t[2][r], t[3][r], ALU.add).then_inc(S("b_spread"), 1)
            for a in range(2):
                b = read(ve, f"bd{a}")
                for j in range(4):
                    ins = ve.tensor_scalar(bd4[a][:, j], b[:, :], C("quad")[:, j:j + 1], None, ALU.mult)
                was_read(ins, f"bd{a}")
            for a in range(2):
                s = v3(st0[:, a * P:(a + 1) * P], NB)
                st.inc(ve.tensor_tensor(s, s, bc(p_mag, 1, NB), ALU.mult))
            b = read(ve, "ct0")
            was_read(ve.tensor_tensor(v3(CT[:, 0:512], 4), v3(b[:, :], 4), bc(C("even"), 1, 4), ALU.mult), "ct0")
            b = read(ve, "ct1")
            was_read(ve.scalar_tensor_tensor(out=v3(CT[:, 512:1024], 4), in0=v3(b[:, :], 4), scalar=-1.0,
                                             in1=bc(C("even"), 1, 4), op0=ALU.mult, op1=ALU.mult), "ct1")

            def input_copies(first, last):
                for i in range(4 * first, 4 * last):
                    b = read(ve, f"bu{2 * i + 1}")
                    was_read(ve.tensor_copy(bim[:, i * T:(i + 1) * T], b[:, 0:T]), f"bu{2 * i + 1}")

            input_copies(0, 1)
            ve.wait_ge(S("rs_latent_ready"), 1)
            ve.wait_ge(S("gains_loaded"), 48)
            for i in range(TT):
                ve.tensor_scalar(cqn[:, i, :], z[:, i, 0:QR], ms2[:, i:i + 1], None, ALU.mult).then_inc(S("cq_ready"), 1)
            for i in range(TT):
                ins = ve.scalar_tensor_tensor(out=ckvn[:, i * KR:(i + 1) * KR], in0=z[:, i, QR:QR + KR],
                                              scalar=ms2[:, 3 + i:4 + i], in1=g_row[:, 0:KR], op0=ALU.mult, op1=ALU.mult)
                if i < 2:
                    st.inc(ins)
            ins.then_inc(S("latents_ready"), 1)
            cos3, sin3 = v3(C("cos"), TT), v3(C("sin"), TT)

            def rotate(x1, x2, cos, sin, t, out1, out2, sem):
                st.inc(ve.tensor_tensor(t[0], x1, cos, ALU.mult))
                st.inc(ve.tensor_tensor(t[1], x2, sin, ALU.mult))
                st.inc(ve.tensor_tensor(t[2], x1, sin, ALU.mult))
                st.inc(ve.tensor_tensor(t[3], x2, cos, ALU.mult))
                st.sync()
                st.inc(ve.tensor_tensor(out1, t[0], t[1], ALU.subtract))
                ve.tensor_tensor(out2, t[2], t[3], ALU.add).then_inc(sem, 1)

            kr3 = v3(krn[:, :], TT)
            zr = z[:, :, QR + KR:ZW]
            ve.wait_ge(S("b_spread"), 4)
            rotate(zr[:, :, 0:HR], zr[:, :, HR:ROPE], cos3, sin3, [v3(r[:, 0:TT * HR], TT) for r in rt],
                   kr3[:, :, 0:HR], kr3[:, :, HR:], S("latents_ready"))
            for o, gq, gk in ((g_row[:, KR:KR + QK], g_row[:, KR:KR + QK], g_row[:, KR + QK:]),
                              (vcol("qk_norm_q"), vcol("qk_norm_q"), vcol("qk_norm_k"))):
                st.link(ve.scalar_tensor_tensor(out=o, in0=gq, scalar=QK ** -0.5, in1=gk, op0=ALU.mult, op1=ALU.mult))
            for k in range(2):
                b = read(ve, f"cq{k}")
                was_read(ve.tensor_scalar(cqT[:, k, :], b[:, 0:TP], vcol("q_norm_g")[:, k:k + 1], None, ALU.mult), f"cq{k}")
            b = read(ve, "ckvT")
            was_read(ve.tensor_copy(ckvT[:, :], b[:, 0:TP]), "ckvT")
            input_copies(1, 4)
            for i in range(TT):
                used(ve, f"q{i}1")
            ve.wait_ge(S("latents_ready"), 2)
            t = [r.rearrange("p (i h d) -> p i h d", i=TT, h=H) for r in rt]
            rotate(q[:, :, :, NOPE:NOPE + HR], q[:, :, :, NOPE + HR:], bc(cos3, 2, H), bc(sin3, 2, H), t,
                   q[:, :, :, NOPE:NOPE + HR], q[:, :, :, NOPE + HR:], S("q_rotated"))
            ve.tensor_copy(kk[:, :, :, NOPE:], bc(kr3, 2, H)).then_inc(S("k_filled"), 1)
            ve.wait_ge(S("qk_squared"), 1)
            ve.tensor_reduce(msq, v3(QT[:, 0:2304], 24), AX, ALU.add).then_inc(S("qk_sums_ready"), 1)
            ve.wait_ge(S("qk_squared"), 2)
            ve.tensor_reduce(msk, v3(KT[:, 0:2304], 24), AX, ALU.add).then_inc(S("qk_sums_ready"), 1)
            ve.wait_ge(S("rs_qk_ready"), 1)
            qf, kf = v3(O1[:, 0:2304], 24), v3(O1[:, 2304:4608], 24)
            ve.tensor_tensor(qf, qf, bc(msq, 2, QK), ALU.mult).then_inc(S("q_ready"), 1)
            ve.wait_ge(S("q_ready"), 1)
            rope_gain = g_row[0:NS, KR + NOPE:KR + QK]
            for e in range(4):
                ins = ve.tensor_tensor(qr4[0:NS, :, e], q[0:NS, 2, :, NOPE:], bc(rope_gain, 1, H), ALU.mult)
            ins.then_inc(S("q_rope_spread"), 1)
            ve.tensor_tensor(kf, kf, bc(msk, 2, QK), ALU.mult).then_inc(S("k_ready"), 1)
            for h in range(H):
                b = read(ve, f"qT{h}")
                was_read(ve.tensor_scalar(qT[0:QK, h, :], b[0:QK, 0:T], vcol("qk_norm_q")[0:QK], None, ALU.mult), f"qT{h}")
            for g in range(2):
                b = read(ve, f"uk{g}")
                was_read(ve.tensor_copy(w_ukT[0:NOPE, 4 * g:4 * g + 4, :], v3(b[0:NOPE, :], 4)), f"uk{g}")
            for name, dst, rows in (("qr", qrp, P), ("qa", qa, P), ("sn", s_new, NS)):
                b = read(ve, name)
                o = dst[0:rows, :].rearrange("p (b h t) -> p h b t", b=NB, h=H)
                was_read(ve.tensor_copy(o, b[0:rows, :].rearrange("p (h b t) -> p h b t", h=H, b=NB)), name)
            ve_loop(ve)


_INS = ["x_prompt", "x_sample", "cache_ckv", "cache_krope", "state_ssm_re", "state_ssm_im", "page_table", "norm1_g",
        "w_in", "ssm_a_re", "ssm_a_im", "ssm_log_dt", "ssm_b_re", "ssm_b_im", "ssm_c_re", "ssm_c_im", "ssm_d",
        "ssm_w_glu", "ssm_b_glu", "q_norm_g", "w_uq", "kv_norm_g", "w_uk", "w_uv", "qk_norm_q", "qk_norm_k",
        "out_norm_ssm", "out_norm_attn", "w_out", "norm2_g", "w_router_group", "b_router_group", "w_router_expert",
        "b_router_expert", "w_gate", "w_up", "w_down"]
_OUTS = [("y_p", (1, SEQ, D)), ("y_s", (NB, NQ, D)), ("ckv_p", (1, 1, SEQ // PAGE, PAGE, KR)),
         ("kr_p", (1, 1, SEQ // PAGE, PAGE, ROPE)), ("re_p", (1, 1, GROUPS, SP)), ("im_p", (1, 1, GROUPS, SP)),
         ("ckv_s", (1, NB, NQ, KR)), ("kr_s", (1, NB, NQ, ROPE)), ("re_s", (1, NB, GROUPS, SP)), ("im_s", (1, NB, GROUPS, SP))]


def program_outputs(O):
    views = dict(O)
    for name in ("ckv_p", "kr_p"):
        views[name] = O[name][0]
    for name in ("re_p", "im_p"):
        views[name] = O[name][0]
    return views


def kernel(**inputs):
    import numpy as _np
    import concourse.bacc as _bacc
    from concourse import mybir as _mybir
    from concourse.bass_utils import run_bass_kernel_spmd as _run

    nc = _bacc.Bacc("TRN2", target_bir_lowering=False, num_devices=1)
    arrays, I, O = {}, {}, {}
    for name in _INS:
        a = _np.ascontiguousarray(inputs[name])
        arrays[f"in_{name}"] = a
        I[name] = nc.dram_tensor(f"in_{name}", a.shape, _mybir.dt.from_np(a.dtype), kind="ExternalInput").ap()
    a = shape_constants()
    arrays["in_shape_constants"] = a
    I["shape_constants"] = nc.dram_tensor("in_shape_constants", a.shape, _mybir.dt.from_np(a.dtype), kind="ExternalInput").ap()
    a = empty_lists()
    arrays["in_empty_lists"] = a
    I["empty_lists"] = nc.dram_tensor("in_empty_lists", a.shape, _mybir.dt.from_np(a.dtype), kind="ExternalInput").ap()
    for name, shape in _OUTS:
        O[name] = nc.dram_tensor(f"out_{name}", shape, F32, kind="ExternalOutput").ap()
    build_program(nc, I, program_outputs(O))
    r = _run(nc, [arrays], core_ids=[0])
    return tuple(r.results[0][f"out_{name}"] for name, _ in _OUTS)
```
